# Optimizing a Trainium2 kernel written in Bass

```python
import math
import jax, jax.numpy as jnp
from jax import lax
import numpy as np

D_MODEL = 1024
BATCH = 1
SEQ = 256
DEPTH = 2

N_A_LAYERS = DEPTH // 2
N_B_LAYERS = DEPTH - N_A_LAYERS
HEAD_DIM = 64
A_HEADS = D_MODEL // (2 * HEAD_DIM)
A_VDIM = 2 * HEAD_DIM
A_QK_WIDTH = A_HEADS * 2 * HEAD_DIM
A_V_WIDTH = A_HEADS * A_VDIM
B_HEADS = D_MODEL // HEAD_DIM
B_WIDTH = B_HEADS * HEAD_DIM
FFN_HIDDEN = 256 * ((8 * D_MODEL // 3 + 255) // 256)
BLOCK_Q = 128
NUM_BUCKETS = 32
MAX_DISTANCE = 128
N_MOD = 9
EPS = 1e-6


def rms_norm(x, g):
    xf = x.astype(jnp.float32)
    y = xf * lax.rsqrt(jnp.mean(xf * xf, axis=-1, keepdims=True) + EPS)
    return (y * g.astype(jnp.float32)).astype(x.dtype)

def modulate(h, shift, scale):
    return h * (1 + scale[:, None, :]) + shift[:, None, :]

def swiglu(h, w_in, w_out):
    g, u = jnp.split(h @ w_in, 2, axis=-1)
    return (jax.nn.silu(g) * u) @ w_out

def t5_bucket(rel):
    n = jnp.maximum(rel, 0)
    max_exact = NUM_BUCKETS // 2
    nf = jnp.maximum(n, 1).astype(jnp.float32)
    large = max_exact + (jnp.log(nf / max_exact) / math.log(MAX_DISTANCE / max_exact)
                         * (NUM_BUCKETS - max_exact)).astype(jnp.int32)
    large = jnp.minimum(large, NUM_BUCKETS - 1)
    return jnp.where(n < max_exact, n, large)

def to_blocks(t):
    b, s = t.shape[:2]
    t = t.reshape((b, s // BLOCK_Q, BLOCK_Q) + t.shape[2:])
    return jnp.moveaxis(t, 1, 0)

def from_blocks(t):
    t = jnp.moveaxis(t, 0, 1)
    return t.reshape((t.shape[0], t.shape[1] * t.shape[2]) + t.shape[3:])

def lambda_init_fn(layer):
    return 0.8 - 0.6 * math.exp(-0.3 * layer)

def diff_attention(h, w_qkv, w_o, lam_params, subln_g, rel_bias, lambda_init):
    b, s, _ = h.shape
    qkv = h @ w_qkv
    q, k, v = jnp.split(qkv, [A_QK_WIDTH, 2 * A_QK_WIDTH], axis=-1)
    q = q.reshape(b, s, A_HEADS, 2, HEAD_DIM)
    k = k.reshape(b, s, A_HEADS, 2, HEAD_DIM)
    v = v.reshape(b, s, A_HEADS, A_VDIM)
    lf = lam_params.astype(jnp.float32)
    lam = jnp.exp(jnp.sum(lf[0] * lf[1])) - jnp.exp(jnp.sum(lf[2] * lf[3])) + lambda_init
    table = rel_bias.astype(jnp.float32)
    k_pos = jnp.arange(s)
    scale = HEAD_DIM ** -0.5

    def block(args):
        qb, blk = args
        q_pos = blk * BLOCK_Q + jnp.arange(BLOCK_Q)
        rel = q_pos[:, None] - k_pos[None, :]
        bias = jnp.take(table, t5_bucket(rel), axis=0)
        bias = jnp.transpose(bias, (2, 0, 1))[None, :, None]
        logits = jnp.einsum('bqhmd,bkhmd->bhmqk', qb, k).astype(jnp.float32) * scale + bias
        logits = jnp.where(rel >= 0, logits, -jnp.inf)
        p = jax.nn.softmax(logits, axis=-1)
        w = p[:, :, 0] - lam * p[:, :, 1]
        return jnp.einsum('bhqk,bkhe->bqhe', w.astype(v.dtype), v)

    nb = s // BLOCK_Q
    o = from_blocks(lax.map(block, (to_blocks(q), jnp.arange(nb))))
    o = rms_norm(o, subln_g) * (1 - lambda_init)
    return o.reshape(b, s, A_V_WIDTH) @ w_o

def shared_kv(x, c_act, kv_ada_w, kv_ada_b, kv_norm_g, kv_w, fgate_w, fgate_b):
    b, s, _ = x.shape
    shift, scale = jnp.split(c_act @ kv_ada_w + kv_ada_b, 2, axis=-1)
    h = modulate(rms_norm(x, kv_norm_g), shift, scale)
    k, v = jnp.split(h @ kv_w, 2, axis=-1)
    k = k.reshape(b, s, B_HEADS, HEAD_DIM)
    v = v.reshape(b, s, B_HEADS, HEAD_DIM)
    log_f = jax.nn.log_sigmoid((h @ fgate_w + fgate_b).astype(jnp.float32))
    F = jnp.cumsum(log_f, axis=1)
    return k, v, F

def forgetting_attention(h, w_q, w_o, k, v, F):
    b, s, _ = h.shape
    q = (h @ w_q).reshape(b, s, B_HEADS, HEAD_DIM)
    k_pos = jnp.arange(s)
    F_k = jnp.transpose(F, (0, 2, 1))
    scale = HEAD_DIM ** -0.5

    def block(args):
        qb, Fqb, blk = args
        q_pos = blk * BLOCK_Q + jnp.arange(BLOCK_Q)
        causal = q_pos[:, None] >= k_pos[None, :]
        decay = jnp.transpose(Fqb, (0, 2, 1))[..., None] - F_k[:, :, None, :]
        logits = jnp.einsum('bqhd,bkhd->bhqk', qb, k).astype(jnp.float32) * scale + decay
        logits = jnp.where(causal, logits, -jnp.inf)
        p = jax.nn.softmax(logits, axis=-1)
        return jnp.einsum('bhqk,bkhd->bqhd', p.astype(v.dtype), v)

    nb = s // BLOCK_Q
    o = from_blocks(lax.map(block, (to_blocks(q), to_blocks(F), jnp.arange(nb))))
    return o.reshape(b, s, B_WIDTH) @ w_o

def first_inputs(seed: int = 0) -> dict:
    key = jax.random.key(seed)
    ks = jax.random.split(key, 21)
    f32 = jnp.float32
    D = D_MODEL

    def nrm(k, shape, std):
        return jax.random.normal(k, shape, f32) * std

    return {
        "x": nrm(ks[0], (BATCH, SEQ, D), 1.0),
        "c": nrm(ks[1], (BATCH, D), 1.0),
        "ada_w": nrm(ks[2], (DEPTH, D, N_MOD * D), 0.5 * D ** -0.5),
        "ada_b": nrm(ks[3], (DEPTH, N_MOD * D), 0.02),
        "norm_g": 1.0 + nrm(ks[4], (DEPTH, 3, D), 0.02),
        "ffn_w_in": nrm(ks[5], (DEPTH, 2, D, 2 * FFN_HIDDEN), D ** -0.5),
        "ffn_w_out": nrm(ks[6], (DEPTH, 2, FFN_HIDDEN, D), FFN_HIDDEN ** -0.5),
        "a_w_qkv": nrm(ks[7], (N_A_LAYERS, D, 2 * A_QK_WIDTH + A_V_WIDTH), D ** -0.5),
        "a_w_o": nrm(ks[8], (N_A_LAYERS, A_V_WIDTH, D), A_V_WIDTH ** -0.5),
        "a_lambda": nrm(ks[9], (N_A_LAYERS, 4, HEAD_DIM), 0.1),
        "a_subln_g": 1.0 + nrm(ks[10], (N_A_LAYERS, A_VDIM), 0.02),
        "rel_bias": nrm(ks[11], (NUM_BUCKETS, A_HEADS), 0.5),
        "kv_ada_w": nrm(ks[12], (D, 2 * D), 0.5 * D ** -0.5),
        "kv_ada_b": nrm(ks[13], (2 * D,), 0.02),
        "kv_norm_g": 1.0 + nrm(ks[14], (D,), 0.02),
        "kv_w": nrm(ks[15], (D, 2 * B_WIDTH), D ** -0.5),
        "fgate_w": nrm(ks[16], (D, B_HEADS), D ** -0.5),
        "fgate_b": jax.random.uniform(ks[17], (B_HEADS,), f32, minval=1.0, maxval=4.0),
        "b_w_q": nrm(ks[18], (N_B_LAYERS, D, B_WIDTH), D ** -0.5),
        "b_w_o": nrm(ks[19], (N_B_LAYERS, B_WIDTH, D), B_WIDTH ** -0.5),
        "final_g": 1.0 + nrm(ks[20], (D,), 0.02),
    }

def first_block(x, c, ada_w, ada_b, norm_g, ffn_w_in, ffn_w_out, a_w_qkv, a_w_o, a_lambda,
              a_subln_g, rel_bias, kv_ada_w, kv_ada_b, kv_norm_g, kv_w, fgate_w, fgate_b,
              b_w_q, b_w_o, final_g):
    c_act = jax.nn.silu(c)
    k_sh = v_sh = F_sh = None
    for layer in range(DEPTH):
        if layer == N_A_LAYERS:
            k_sh, v_sh, F_sh = shared_kv(x, c_act, kv_ada_w, kv_ada_b, kv_norm_g, kv_w,
                                         fgate_w, fgate_b)
        mod = c_act @ ada_w[layer] + ada_b[layer]
        sh1, sc1, g1, sh2, sc2, g2, sh3, sc3, g3 = jnp.split(mod, N_MOD, axis=-1)
        h = modulate(rms_norm(x, norm_g[layer, 0]), sh1, sc1)
        x = x + 0.5 * g1[:, None, :] * swiglu(h, ffn_w_in[layer, 0], ffn_w_out[layer, 0])
        h = modulate(rms_norm(x, norm_g[layer, 1]), sh2, sc2)
        if layer < N_A_LAYERS:
            mix = diff_attention(h, a_w_qkv[layer], a_w_o[layer], a_lambda[layer],
                                 a_subln_g[layer], rel_bias, lambda_init_fn(layer))
        else:
            j = layer - N_A_LAYERS
            mix = forgetting_attention(h, b_w_q[j], b_w_o[j], k_sh, v_sh, F_sh)
        x = x + g2[:, None, :] * mix
        h = modulate(rms_norm(x, norm_g[layer, 2]), sh3, sc3)
        x = x + 0.5 * g3[:, None, :] * swiglu(h, ffn_w_in[layer, 1], ffn_w_out[layer, 1])
    return rms_norm(x, final_g)


DEPTH_2 = 1

N_MEM = 256
SC_WIDTH = D_MODEL
SC_KERNEL = 3
CF_WIDTH = D_MODEL
CF_KERNEL = 31
XA_HEADS = 4
XA_HEAD_DIM = D_MODEL // XA_HEADS
PEER_HEADS = 8
PEER_NKEYS = 128
PEER_TOPK = 16
PEER_QDIM = 256
PEER_HALF = PEER_QDIM // 2
PEER_EXPERTS = PEER_NKEYS * PEER_NKEYS
PEER_CHUNK = 128
IN_COLS = 3 * SC_WIDTH + 2 * CF_WIDTH + 2 * D_MODEL


def rms_norm_2(x, g):
    xf = x.astype(jnp.float32)
    y = xf * lax.rsqrt(jnp.mean(xf * xf, axis=-1, keepdims=True) + EPS)
    return (y * g.astype(jnp.float32)).astype(x.dtype)

def layer_norm(x, g, b):
    xf = x.astype(jnp.float32)
    mu = jnp.mean(xf, axis=-1, keepdims=True)
    var = jnp.mean(jnp.square(xf - mu), axis=-1, keepdims=True)
    y = (xf - mu) * lax.rsqrt(var + EPS)
    return (y * g.astype(jnp.float32) + b.astype(jnp.float32)).astype(x.dtype)

def causal_depthwise_conv(x, w):
    k, c = w.shape
    return lax.conv_general_dilated(
        x, w.reshape(k, 1, c).astype(x.dtype), window_strides=(1,), padding=[(k - 1, 0)],
        dimension_numbers=('NWC', 'WIO', 'NWC'), feature_group_count=c)

def conv_mixers(h, w_in, cf_b_pw1, sc_conv_w, sc_w_out, cf_conv_w, cf_conv_b, cf_ln_g, cf_ln_b,
                cf_w_pw2, cf_b_pw2, w_mix_out):
    proj = jnp.einsum('bsd,dc->bsc', h, w_in)
    cuts = [SC_WIDTH, 2 * SC_WIDTH, 3 * SC_WIDTH, 3 * SC_WIDTH + CF_WIDTH,
            3 * SC_WIDTH + 2 * CF_WIDTH, 3 * SC_WIDTH + 2 * CF_WIDTH + D_MODEL]
    sc_b, sc_c, sc_x, cf_a, cf_g, gate_sc, gate_cf = jnp.split(proj, cuts, axis=-1)
    y_sc = sc_b * causal_depthwise_conv(sc_c * sc_x, sc_conv_w)
    y_sc = jnp.einsum('bsc,cd->bsd', y_sc, sc_w_out)
    cf = (cf_a + cf_b_pw1[:CF_WIDTH]) * jax.nn.sigmoid(cf_g + cf_b_pw1[CF_WIDTH:])
    cf = causal_depthwise_conv(cf, cf_conv_w) + cf_conv_b
    cf = jax.nn.silu(layer_norm(cf, cf_ln_g, cf_ln_b))
    y_cf = jnp.einsum('bsc,cd->bsd', cf, cf_w_pw2) + cf_b_pw2
    merged = jax.nn.sigmoid(gate_sc) * y_sc + jax.nn.sigmoid(gate_cf) * y_cf
    return jnp.einsum('bsd,de->bse', merged, w_mix_out)

def memory_cross_attention(h, mem_n, w_q, w_kv, w_xo):
    b, s, _ = h.shape
    m = mem_n.shape[1]
    q = jnp.einsum('bsd,de->bse', h, w_q).reshape(b, s, XA_HEADS, XA_HEAD_DIM)
    kv = jnp.einsum('bmd,de->bme', mem_n, w_kv).reshape(b, m, 2, XA_HEADS, XA_HEAD_DIM)
    k, v = kv[:, :, 0], kv[:, :, 1]
    scores = jnp.einsum('bshd,bmhd->bhsm', q, k).astype(jnp.float32) * (XA_HEAD_DIM ** -0.5)
    probs = jax.nn.softmax(scores, axis=-1).astype(v.dtype)
    o = jnp.einsum('bhsm,bmhd->bshd', probs, v).reshape(b, s, XA_HEADS * XA_HEAD_DIM)
    return jnp.einsum('bse,ed->bsd', o, w_xo)

def peer_ffn(h, w_pq, subkeys, u, v):
    b, s, d = h.shape
    q = jnp.einsum('bsd,dq->bsq', h, w_pq).reshape(b, s, PEER_HEADS, 2, PEER_HALF)
    sub_scores = jnp.einsum('bshpc,pnc->bshpn', q, subkeys).astype(jnp.float32)
    top_s, top_i = lax.top_k(sub_scores, PEER_TOPK)
    n_cand = PEER_TOPK * PEER_TOPK
    cand_s = (top_s[..., 0, :, None] + top_s[..., 1, None, :]).reshape(b, s, PEER_HEADS, n_cand)
    cand_i = (top_i[..., 0, :, None] * PEER_NKEYS + top_i[..., 1, None, :]).reshape(b, s, PEER_HEADS, n_cand)
    fin_s, fin_pos = lax.top_k(cand_s, PEER_TOPK)
    expert_idx = jnp.take_along_axis(cand_i, fin_pos, axis=-1)
    gates = jax.nn.softmax(fin_s, axis=-1).astype(h.dtype)
    n_chunks = (b * s) // PEER_CHUNK
    h_c = h.reshape(n_chunks, PEER_CHUNK, d)
    e_c = expert_idx.reshape(n_chunks, PEER_CHUNK, PEER_HEADS, PEER_TOPK)
    g_c = gates.reshape(n_chunks, PEER_CHUNK, PEER_HEADS, PEER_TOPK)

    def chunk(args):
        hc, ec, gc = args
        u_sel = jnp.take(u, ec, axis=0)
        act = jax.nn.gelu(jnp.einsum('chkd,cd->chk', u_sel, hc), approximate=False) * gc
        v_sel = jnp.take(v, ec, axis=0)
        return jnp.einsum('chk,chkd->cd', act, v_sel)

    out = lax.map(chunk, (h_c, e_c, g_c))
    return out.reshape(b, s, d)

def second_inputs(seed: int = 0) -> dict:
    key = jax.random.key(seed)
    ks = jax.random.split(key, 26)
    L = DEPTH_2

    def nrm(k, shape, scale):
        return jax.random.normal(k, shape, jnp.float32) * scale

    def gain(k, shape):
        return 1.0 + 0.02 * jax.random.normal(k, shape, jnp.float32)

    return {
        'x': nrm(ks[0], (BATCH, SEQ, D_MODEL), 1.0),
        'mem': nrm(ks[1], (BATCH, N_MEM, D_MODEL), 1.0),
        'norm_mix_g': gain(ks[2], (L, D_MODEL)),
        'w_in': nrm(ks[3], (L, D_MODEL, IN_COLS), D_MODEL ** -0.5),
        'cf_b_pw1': nrm(ks[4], (L, 2 * CF_WIDTH), 0.02),
        'sc_conv_w': nrm(ks[5], (L, SC_KERNEL, SC_WIDTH), SC_KERNEL ** -0.5),
        'sc_w_out': nrm(ks[6], (L, SC_WIDTH, D_MODEL), SC_WIDTH ** -0.5),
        'cf_conv_w': nrm(ks[7], (L, CF_KERNEL, CF_WIDTH), CF_KERNEL ** -0.5),
        'cf_conv_b': nrm(ks[8], (L, CF_WIDTH), 0.02),
        'cf_ln_g': gain(ks[9], (L, CF_WIDTH)),
        'cf_ln_b': nrm(ks[10], (L, CF_WIDTH), 0.02),
        'cf_w_pw2': nrm(ks[11], (L, CF_WIDTH, D_MODEL), CF_WIDTH ** -0.5),
        'cf_b_pw2': nrm(ks[12], (L, D_MODEL), 0.02),
        'w_mix_out': nrm(ks[13], (L, D_MODEL, D_MODEL), D_MODEL ** -0.5),
        'norm_xa_g': gain(ks[14], (L, D_MODEL)),
        'norm_mem_g': gain(ks[15], (L, D_MODEL)),
        'w_q': nrm(ks[16], (L, D_MODEL, XA_HEADS * XA_HEAD_DIM), D_MODEL ** -0.5),
        'w_kv': nrm(ks[17], (L, D_MODEL, 2 * XA_HEADS * XA_HEAD_DIM), D_MODEL ** -0.5),
        'w_xo': nrm(ks[18], (L, XA_HEADS * XA_HEAD_DIM, D_MODEL), D_MODEL ** -0.5),
        'norm_peer_g': gain(ks[19], (L, D_MODEL)),
        'w_peer_q': nrm(ks[20], (L, D_MODEL, PEER_HEADS * PEER_QDIM), D_MODEL ** -0.5),
        'peer_subkeys': nrm(ks[21], (L, 2, PEER_NKEYS, PEER_HALF), PEER_HALF ** -0.5),
        'peer_u': nrm(ks[22], (L, PEER_EXPERTS, D_MODEL), D_MODEL ** -0.5),
        'peer_v': nrm(ks[23], (L, PEER_EXPERTS, D_MODEL), PEER_HEADS ** -0.5),
        'final_norm_g': gain(ks[24], (D_MODEL,)),
    }

def second_block(x, mem, norm_mix_g, w_in, cf_b_pw1, sc_conv_w, sc_w_out, cf_conv_w, cf_conv_b, cf_ln_g,
              cf_ln_b, cf_w_pw2, cf_b_pw2, w_mix_out, norm_xa_g, norm_mem_g, w_q, w_kv, w_xo, norm_peer_g,
              w_peer_q, peer_subkeys, peer_u, peer_v, final_norm_g):
    for l in range(DEPTH_2):
        x = x + conv_mixers(rms_norm_2(x, norm_mix_g[l]), w_in[l], cf_b_pw1[l], sc_conv_w[l], sc_w_out[l],
                            cf_conv_w[l], cf_conv_b[l], cf_ln_g[l], cf_ln_b[l], cf_w_pw2[l], cf_b_pw2[l],
                            w_mix_out[l])
        mem_n = rms_norm_2(mem, norm_mem_g[l])
        x = x + memory_cross_attention(rms_norm_2(x, norm_xa_g[l]), mem_n, w_q[l], w_kv[l], w_xo[l])
        x = x + peer_ffn(rms_norm_2(x, norm_peer_g[l]), w_peer_q[l], peer_subkeys[l], peer_u[l], peer_v[l])
    return rms_norm_2(x, final_norm_g)


def setup_inputs(seed=0):
    out = dict(first_inputs(seed))
    for name, value in second_inputs(seed + 1).items():
        if name != "x":
            out[name + "_2"] = value
    return out


def reference(
    x, c, ada_w, ada_b, norm_g, ffn_w_in, ffn_w_out, a_w_qkv, a_w_o, a_lambda, a_subln_g,
    rel_bias, kv_ada_w, kv_ada_b, kv_norm_g, kv_w, fgate_w, fgate_b, b_w_q, b_w_o, final_g,
    mem_2, norm_mix_g_2, w_in_2, cf_b_pw1_2, sc_conv_w_2, sc_w_out_2, cf_conv_w_2, cf_conv_b_2,
    cf_ln_g_2, cf_ln_b_2, cf_w_pw2_2, cf_b_pw2_2, w_mix_out_2, norm_xa_g_2, norm_mem_g_2, w_q_2,
    w_kv_2, w_xo_2, norm_peer_g_2, w_peer_q_2, peer_subkeys_2, peer_u_2, peer_v_2,
    final_norm_g_2,
):
    x = first_block(
        x, c, ada_w, ada_b, norm_g, ffn_w_in, ffn_w_out, a_w_qkv, a_w_o, a_lambda, a_subln_g,
        rel_bias, kv_ada_w, kv_ada_b, kv_norm_g, kv_w, fgate_w, fgate_b, b_w_q, b_w_o, final_g,
    )
    return second_block(
        x, mem_2, norm_mix_g_2, w_in_2, cf_b_pw1_2, sc_conv_w_2, sc_w_out_2, cf_conv_w_2,
        cf_conv_b_2, cf_ln_g_2, cf_ln_b_2, cf_w_pw2_2, cf_b_pw2_2, w_mix_out_2, norm_xa_g_2,
        norm_mem_g_2, w_q_2, w_kv_2, w_xo_2, norm_peer_g_2, w_peer_q_2, peer_subkeys_2,
        peer_u_2, peer_v_2, final_norm_g_2,
    )


_drawn_inputs = setup_inputs


def setup_inputs(seed=0):
    import zlib

    import numpy as np

    out = dict(_drawn_inputs(seed))
    spreads = {}
    factors = {'norm_g': 3.036,
     'a_lambda': 4.542,
     'a_subln_g': 3.97,
     'kv_ada_b': 3.365,
     'kv_norm_g': 4.913,
     'cf_b_pw1_2': 4.069,
     'cf_conv_b_2': 2.688,
     'cf_ln_g_2': 3.91,
     'cf_ln_b_2': 4.441,
     'cf_b_pw2_2': 3.095,
     'norm_xa_g_2': 8.0,
     'norm_mem_g_2': 7.204,
     'final_norm_g_2': 8.036,
     'norm_peer_g_2': 8.0,
     'peer_u_2': 2.673}
    for name, (base, spread) in spreads.items():
        noise = np.random.default_rng([zlib.crc32(name.encode()), seed]).standard_normal(out[name].shape)
        drawn = base * np.exp(spread * noise) if base else spread * noise
        out[name] = __import__('jax').numpy.asarray(drawn.astype(out[name].dtype))
    for name, factor in factors.items():
        out[name] = (out[name] * factor).astype(out[name].dtype)
    return out
```

```python
import math
from contextlib import ExitStack

import numpy as np

import concourse.bass as bass
from concourse import mybir

F32 = mybir.dt.float32
U32 = mybir.dt.uint32
ACT = mybir.ActivationFunctionType
ALU = mybir.AluOpType
AX = mybir.AxisListType

P = 128
D = 1024
DC = D // P
SEQ = 256
TT = SEQ // P
FFN = 256 * ((8 * D // 3 + 255) // 256)
FC = FFN // P
HD = 64
A_HEADS = D // (2 * HD)
B_HEADS = D // HD
NB = 32
MAX_DISTANCE = 128
EPS = 1e-6
LAM_INIT = 0.8 - 0.6 * math.exp(-0.3 * 0)
NEG = -1e30
SCK, CFK = 3, 31
PH, NK, TK = 8, 128, 16
N_EXP = NK * NK
SLOTS_PER_TILE = PH * TK

_COLS = [("c", 8), ("ada_b", 160), ("norm_g", 48), ("kv_norm_g", 8), ("final_g", 8), ("norm_mix_g", 8),
         ("cf_b_pw1", 16), ("sc_w", SCK * 8), ("cf_w", CFK * 8), ("cf_conv_b", 8), ("ln_g", 8), ("ln_b", 8),
         ("b_pw2", 8), ("norm_xa_g", 8), ("norm_mem_g", 8), ("norm_peer_g", 8), ("subln_g", 1),
         ("fgate_w", DC * B_HEADS)]
COL, NCOL = {}, 0
for _n, _w in _COLS:
    COL[_n] = NCOL
    NCOL += _w

ADA_TILES = 40
MOD_L0, MOD_KV, MOD_L1 = 0, 72, 88

G = COL["norm_g"]
NORMS = [(G, MOD_L0), (G + 8, MOD_L0 + 24), (G + 16, MOD_L0 + 48), (COL["kv_norm_g"], MOD_KV),
         (G + 24, MOD_L1), (G + 32, MOD_L1 + 24), (G + 40, MOD_L1 + 48),
         (COL["final_g"], None), (COL["norm_mix_g"], None), (COL["norm_mem_g"], None),
         (COL["norm_xa_g"], None), (COL["norm_peer_g"], None)]
N_FINAL, N_MIX, N_MEM, N_XA, N_PEER = 7, 8, 9, 10, 11

RING = 4
TILE = 8 * 512
WO_TILE = FC * P
_LIN = [("f00_in", 11, 4, TILE, "adad"), ("f00_out", 8, 1, WO_TILE, "d"),
        ("a_qk", 4, 4, TILE, None), ("a_v", 2, 2, TILE, "ad"), ("a_o", 2, 4, TILE, "dddd"),
        ("f01_in", 11, 4, TILE, "adad"), ("f01_out", 8, 1, WO_TILE, "d"),
        ("s_k", 2, 4, TILE, "dddd"), ("s_v", 2, 2, TILE, "ad"),
        ("f10_in", 11, 4, TILE, "adad"), ("f10_out", 8, 1, WO_TILE, "d"),
        ("b_q", 2, 4, TILE, "aaaa"), ("b_o", 2, 4, TILE, "dddd"),
        ("f11_in", 11, 4, TILE, "adad"), ("f11_out", 8, 1, WO_TILE, "d"),
        ("mix_a", 8, 4, TILE, "adad"), ("mix_b", 6, 4, TILE, None),
        ("sc_out", 2, 4, TILE, "dddd"), ("cf_out", 2, 4, TILE, "dddd"), ("mix_out", 2, 4, TILE, "dddd"),
        ("x_k", 2, 4, TILE, "dddd"), ("x_v", 2, 2, TILE, "ad"), ("x_q", 2, 4, TILE, "aaaa"),
        ("x_o", 2, 4, TILE, "dddd"), ("pq", 4, 4, TILE, "adad")]


class Linear:
    pass


LIN, FREE = {}, []


def _plan():
    tile, counts = 0, {"a": 0, "d": 0}
    for name, tiles, per, width, who in _LIN:
        ln = Linear()
        ln.name, ln.tiles, ln.per, ln.width = name, tiles, per, width
        ln.tile0, ln.chunk0 = tile, len(FREE)
        for t in range(tiles):
            if name == "a_qk":
                pat = "aaaa" if t < 2 else "dddd"
            elif name == "mix_b":
                pat = "dddd" if t < 2 else "aaaa"
            else:
                pat = who
            for e in pat:
                counts[e] += 1
                FREE.append((e, counts[e]))
        ln.chunk_end = len(FREE)
        ln.freed_a, ln.freed_d = counts["a"], counts["d"]
        tile += tiles
        LIN[name] = ln


_plan()

STEPS = [("A", c) for c in range(DC)] + [("B", c) for c in range(DC)] + [("X", c) for c in range(2)]
STEP0 = {"A": 0, "B": 8, "X": 16}
STEP_END = {"A": 8, "B": 16, "X": 18}

GROUP = 16
N_GROUPS = SLOTS_PER_TILE // GROUP


def at(i, step, base):
    return base if i is None else i * step + base


class Chain:

    def __init__(self, eng, sem):
        self.eng, self.sem, self.n, self.i, self.step = eng, sem, 0, None, 0

    def __call__(self, ins, lag=0):
        ins.then_inc(self.sem, 1)
        self.n += 1
        if self.n > lag:
            self.eng.wait_ge(self.sem, at(self.i, self.step, self.n - lag))

    def enter(self, i, step):
        self.i, self.step, self.start = i, step, self.n

    def leave(self, rounds):
        assert self.n - self.start == self.step, (self.n - self.start, self.step)
        self.n = self.start + rounds * self.step
        self.i = None


def build_program(nc, a, out):
    ctx = ExitStack()
    with ctx:
        def sb(name, shape, dt=F32):
            return ctx.enter_context(nc.sbuf_tensor(name, shape, dt))

        def sem(name):
            return ctx.enter_context(nc.semaphore(name))

        ring = sb("ring", [P, RING * TILE])
        mod_ring = sb("mod_ring", [P, 2 * TILE])
        mod_acc = sb("mod_acc", [P, 2, 512])
        X = sb("X", [P, DC, SEQ])
        H = sb("H", [P, DC, SEQ])
        SQ = sb("SQ", [P, DC, SEQ])
        KS = sb("KS", [P, DC, SEQ])
        VS = sb("VS", [P, TT, D])
        bias = KS
        work = sb("work", [P, 14336])
        prm = sb("prm", [P, NCOL])
        mods = sb("mods", [P, 4 * ADA_TILES])
        c_act = sb("c_act", [P, DC])
        gain = sb("gain", [P, DC])
        half_gate = sb("half_gate", [P, DC])
        root = sb("root", [P, SEQ])
        rinv = sb("rinv", [P, SEQ])
        ident = sb("ident", [P, P])
        ones = sb("ones", [P, P])
        mask = sb("mask", [P, SEQ])
        iota16 = sb("iota16", [P, TK])
        table = sb("table", [NB + 1, A_HEADS])
        table_rep = work[0:NB + 1, 4096:5120].rearrange("p (h n) -> p h n", h=A_HEADS)
        onehot = work[0:NB + 1, 5120:5632]
        lamp = work[:, 5632:5632 + 4 * HD]
        lam_prod = work[:, 5888:5888 + 2 * HD].rearrange("p (a n) -> p a n", a=2)
        lam_sum = sb("lam_sum", [P, 2])
        lam_exp = sb("lam_exp", [P, 2])
        lam_vec = sb("lam_vec", [P, 2])
        sub_gain = sb("sub_gain", [P, 1])
        fgate_b = sb("fgate_b", [B_HEADS, 1])
        f_z = work[0:B_HEADS, 12288:12288 + SEQ]
        f_t = work[0:B_HEADS, 12288 + SEQ:12288 + 2 * SEQ]
        f_sum = sb("f_sum", [B_HEADS, SEQ])
        f_neg = sb("f_neg", [B_HEADS, SEQ])
        subk = sb("subk", [P, 2, NK])
        nmax = sb("nmax", [P, 2, 2, 2])
        rowmax = sb("rowmax", [P, 2, 2, 2])
        rowsum = sb("rowsum", [P, 2, 2, 2])
        rscale = sb("rscale", [P, 2, 2, 2])
        stage = sb("stage", [P, 2, GROUP], U32)
        dot16 = sb("dot16", [P, GROUP])
        coef16 = sb("coef16", [P, GROUP])
        eps = sb("eps", [P, 1])

        def wk(lo, n, *shape):
            v = work[:, lo:lo + n]
            if len(shape) == 2:
                return v.rearrange("p (a b) -> p a b", a=shape[0])
            if len(shape) == 3:
                return v.rearrange("p (a b c) -> p a b c", a=shape[0], b=shape[1])
            return v

        GU = wk(0, FC * SEQ, FC, SEQ)
        silu = wk(5632, 512, 2, SEQ)
        stg = wk(0, 4096, A_HEADS, 512)
        QT = wk(0, 2048, DC, SEQ)
        KT = wk(2048, 2048, DC, SEQ)
        V = wk(4096, 2048, TT, D)
        OT = wk(6144, 2048, DC, SEQ)
        LG = wk(8192, 1024, 2, 2, SEQ)
        EX = wk(9216, 1024, 2, 2, SEQ)
        PR = wk(10240, 1024, 2, 2, SEQ)
        PT = wk(11264, 1024, 2, 512)
        DQ = wk(2048, 2048, DC, SEQ)
        DK = wk(4096, 2048, DC, SEQ)
        UP = SEQ + SCK - 1
        VP = SEQ + CFK - 1
        U = wk(0, DC * UP, DC, UP)
        CV = wk(2064, DC * VP, DC, VP)
        C3 = wk(4352, 2048, DC, SEQ)
        Z = wk(6400, 2048, DC, SEQ)
        SG = wk(8448, 2048, DC, SEQ)
        CG = wk(10496, 2048, DC, SEQ)
        T0 = wk(12544, 512, 2, SEQ)
        T1 = wk(13056, 512, 2, SEQ)
        ZB = wk(13568, 256)
        S = wk(0, 2048, 2 * PH, NK)
        S2 = wk(2048, 2048, 2 * PH, NK)
        CA = wk(4096, 2048, PH, TK * TK)
        CA2 = wk(6144, 2048, PH, TK * TK)
        EQ = wk(0, 2048, SLOTS_PER_TILE, TK)
        EQ2 = wk(2048, 2048, SLOTS_PER_TILE, TK)
        QP = wk(8192, 4096, 2 * PH, SEQ)
        HTOK = wk(12288, 2048, TT, D)
        XTOK = SQ[:, :, :].rearrange("p c t -> p (c t)").rearrange("p (a b) -> p a b", a=TT)
        YACC = H[:, :, :].rearrange("p c t -> p (c t)").rearrange("p (a b) -> p a b", a=2)
        at_mr = [0]

        def mr(n, a0=None, dt=None):
            v = mod_ring[:, at_mr[0]:at_mr[0] + n]
            at_mr[0] += n
            if dt is not None:
                v = v.bitcast(dt)
            return v if a0 is None else v.rearrange("p (a b) -> p a b", a=a0)

        junk = mr(2048, 2)
        gfin = mr(D)
        YO = mr(2 * D, 2)
        TV = mr(256, 2 * PH)
        TI = mr(256, 2 * PH, U32)
        TIF = mr(256, 2 * PH)
        FV = mr(128, PH)
        FP = mr(128, PH, U32)
        AI = mr(128, None, U32)
        BI = mr(128, None, U32)
        AF = mr(128)
        BF = mr(128)
        I0 = mr(128)
        I1 = mr(128)
        IDX = mr(256, 2, U32)
        GT = mr(256, 2)
        DOT = mr(256, 2)
        CF = mr(256, 2)
        GS = mr(16)
        YS = mr(4)
        assert at_mr[0] <= 2 * TILE

        ps = ctx.enter_context(nc.psum_tensor("ps", [P, 8, 512], F32))
        ps_norm = ps[:, 4, 0:SEQ]
        ps_mod = ps[:, 7, 0:8]
        ps_s = (ps[:, 5:7, :], ps[:, 2:5:2, :])
        PT_BANK = (7, 3)
        ps_f = ps[0:B_HEADS, 5, 0:SEQ]

        bias_rows = nc.dram_tensor("bias_rows", (A_HEADS, P * 512), F32).ap()

        def col(name, k=0, n=1):
            return prm[:, COL[name] + k:COL[name] + k + n]

        def slot(n, width=TILE):
            s = (n % RING) * TILE
            return ring[:, s:s + width]

        prm_loaded = sem("prm_loaded")
        x_loaded = sem("x_loaded")
        small_loaded = sem("small_loaded")
        sub_loaded = sem("sub_loaded")
        w_loaded = [sem(f"w_loaded{s}") for s in range(RING)]
        mod_loaded = [sem(f"mod_loaded{s}") for s in range(2)]
        rows_written = sem("rows_written")
        bias_loaded = sem("bias_loaded")
        decay_loaded = sem("decay_loaded")
        mem_loaded = sem("mem_loaded")
        gfin_loaded = sem("gfin_loaded")
        out_written = sem("out_written")
        consts_ready = sem("consts_ready")
        pool_step = sem("pool_step")
        vec_consts = sem("vec_consts")
        dve_step = sem("dve_step")
        act_step = sem("act_step")
        c_ready = sem("c_ready")
        acc_ready = sem("acc_ready")
        modsum_ready = sem("modsum_ready")
        mods_ready = sem("mods_ready")
        lam_sum_ready = sem("lam_sum_ready")
        lam_exp_ready = sem("lam_exp_ready")
        table_ready = sem("table_ready")
        rows_ready = sem("rows_ready")
        rows_copied = sem("rows_copied")
        squares_ready = sem("squares_ready")
        sumsq_ready = sem("sumsq_ready")
        root_ready = sem("root_ready")
        scaled_ready = sem("scaled_ready")
        h_ready = sem("h_ready")
        chunk_done = sem("chunk_done")
        freed = {"a": sem("freed_by_scalar"), "d": sem("freed_by_vector")}
        scores_done = sem("scores_done")
        logits_ready = sem("logits_ready")
        exp_ready = sem("exp_ready")
        probs_ready = sem("probs_ready")
        turned = sem("turned")
        probsT_ready = sem("probsT_ready")
        pv_done = sem("pv_done")
        attn_ready = sem("attn_ready")
        sub_sq = sem("sub_sq")
        sub_sum = sem("sub_sum")
        sub_root = sem("sub_root")
        sub_done = sem("sub_done")
        fz_done = sem("fz_done")
        fz_ln = sem("fz_ln")
        f_ready = sem("f_ready")
        decay_cleared = sem("decay_cleared")
        pads_ready = sem("pads_ready")
        conv_done = sem("conv_done")
        mean_sum = sem("mean_sum")
        mean_ready = sem("mean_ready")
        centred = sem("centred")
        ln_sq = sem("ln_sq")
        ln_sum = sem("ln_sum")
        ln_root = sem("ln_root")
        ln_scaled = sem("ln_scaled")
        ln_ready = sem("ln_ready")
        tok_turned = sem("tok_turned")
        tok_ready = sem("tok_ready")
        sub_scores = sem("sub_scores")
        s_ready = sem("s_ready")
        s_used = sem("s_used")
        gate_diff = sem("gate_diff")
        gate_exp = sem("gate_exp")
        idx_ready = sem("idx_ready")
        dots_ready = sem("dots_ready")
        gelu_ready = sem("gelu_ready")
        staged = sem("staged")
        row_loaded = [sem(f"row_loaded{s}") for s in range(GROUP)]
        rows_free = sem("rows_free")
        rows_asked = sem("rows_asked")
        y_ready = sem("y_ready")
        yroot_ready = sem("yroot_ready")
        yo_ready = sem("yo_ready")

        block = ctx.enter_context(nc.Block())

        @block.sync
        def _(sp):
            sp.dma_start(prm[:, :], a["prm"]).then_inc(prm_loaded, 16)
            sp.dma_start(X[:, :, :], a["xT"]).then_inc(x_loaded, 16)

            def tiles(name, t0, n, i=None):
                ln = LIN[name]
                for t in range(t0, t0 + n):
                    g = ln.tile0 + t
                    if g >= RING:
                        sp.wait_ge(chunk_done, at(i, n * ln.per, tile_end(g - RING, ln, i)))
                    src = a[name][t] if i is None else a[name][bass.ds(i * n + t, 1)].rearrange("a p f -> (a p) f")
                    sp.dma_start(slot(g, ln.width), src).then_inc(w_loaded[g % RING], 16)

            def tile_end(g, ln, i):
                if i is not None and g < ln.tile0:
                    return ln.chunk0 + (g + 1 - ln.tile0) * ln.per
                for other in LIN.values():
                    if other.tile0 <= g < other.tile0 + other.tiles:
                        return other.chunk0 + (g + 1 - other.tile0) * other.per

            def ffn(w_in, w_out):
                if LIN[w_in].tile0 == 0:
                    tiles(w_in, 0, 11)
                else:
                    tiles(w_in, 0, 3)
                    with sp.Fori(0, 2) as i:
                        tiles(w_in, 3, 4, i)
                tiles(w_out, 0, 8)

            ffn("f00_in", "f00_out")
            tiles("a_qk", 0, 4)
            tiles("a_v", 0, 2)
            tiles("a_o", 0, 2)
            ffn("f01_in", "f01_out")
            tiles("s_k", 0, 2)
            tiles("s_v", 0, 2)
            ffn("f10_in", "f10_out")
            tiles("b_q", 0, 2)
            sp.wait_ge(f_ready, 1)
            sp.wait_ge(decay_cleared, 4)
            for odd in range(2):
                sp.dma_start(DQ[64 * odd:64 * odd + 1, :, :], f_sum[odd:B_HEADS:2, :]).then_inc(decay_loaded, 16)
                sp.dma_start(DK[64 * odd + 1:64 * odd + 2, :, :], f_neg[odd:B_HEADS:2, :]).then_inc(decay_loaded, 16)
            tiles("b_o", 0, 2)
            ffn("f11_in", "f11_out")
            sp.dma_start(KS[:, :, :], a["memT"]).then_inc(mem_loaded, 16)
            tiles("mix_a", 0, 8)
            tiles("mix_b", 0, 6)
            for name in ("sc_out", "cf_out", "mix_out", "x_k", "x_v", "x_q", "x_o", "pq"):
                tiles(name, 0, LIN[name].tiles)
            sp.dma_start(gfin, a["final_norm_g"].partition_broadcast(P).rearrange("q a n -> q (a n)")).then_inc(gfin_loaded, 16)
            for t in range(TT):
                sp.wait_ge(yo_ready, t + 1)
                sp.dma_start(out[t], YO[:, t, :]).then_inc(out_written, 16)
            sp.wait_ge(out_written, 16 * TT)

        @block.gpsimd
        def _(pool):
            step = Chain(pool, pool_step)
            pool.dma_start(table[0:NB, :], a["rel_bias"]).then_inc(small_loaded, 16)
            pool.dma_start(onehot[:, :], a["onehot"]).then_inc(small_loaded, 16)
            pool.dma_start(lamp[:, :], a["a_lambda"].partition_broadcast(P).rearrange("q a n -> q (a n)")).then_inc(small_loaded, 16)
            pool.dma_start(fgate_b[:, :], a["fgate_b"]).then_inc(small_loaded, 16)
            pool.dma_start(subk[:, :, :], a["subkT"]).then_inc(small_loaded, 16)
            step(nc.gpsimd.memset(ident[:, :], 0.0))
            nc.gpsimd.affine_select(out=ident[:, :], in_=ident[:, :], compare_op=ALU.not_equal, fill=1.0, base=0,
                                    pattern=[[-1, P]], channel_multiplier=1).then_inc(consts_ready, 1)
            step(nc.gpsimd.memset(mask[:, :], 0.0))
            nc.gpsimd.affine_select(out=mask[:, :], in_=mask[:, :], compare_op=ALU.is_ge, fill=NEG, base=P,
                                    pattern=[[-1, SEQ]], channel_multiplier=1).then_inc(consts_ready, 1)
            nc.gpsimd.iota(iota16[:, :], pattern=[[1, TK]], base=0, channel_multiplier=0,
                           allow_small_or_imprecise_dtypes=True).then_inc(consts_ready, 1)

            for s in range(2):
                pool.dma_start(mod_ring[:, s * TILE:(s + 1) * TILE], a["ada"][s]).then_inc(mod_loaded[s], 16)
            with pool.Fori(1, ADA_TILES // 2) as i:
                for s in range(2):
                    pool.wait_ge(acc_ready, i * 2 + (s - 1))
                    pool.dma_start(mod_ring[:, s * TILE:(s + 1) * TILE],
                                   a["ada"][bass.ds(i * 2 + s, 1)].rearrange("a p f -> (a p) f")).then_inc(mod_loaded[s], 16)

            for t in range(TT):
                pool.wait_ge(idx_ready, t + 1)
                for part, rows in enumerate((a["peer_u"], a["peer_v"])):
                    seg = 2 * t + part
                    with pool.Fori(0, N_GROUPS // 2) as i:
                        for g in range(2):
                            group = seg * N_GROUPS + g
                            lo = i * (2 * GROUP) + g * GROUP
                            nc.gpsimd.tensor_copy(stage[:, g, :], IDX[:, t, bass.ds(lo, GROUP)]).then_inc(staged, 1)
                            pool.wait_ge(staged, i * 2 + (group + 1))
                            for j in range(GROUP):
                                if j % 4 == 0:
                                    pool.wait_ge(rows_free, i * (2 * GROUP) + (group * GROUP + j + 4))
                                    pool.sem_inc(rows_asked, 1)
                                pool.indirect_dma_start(
                                    out=ring[:, j * D:(j + 1) * D], out_offset=None, in_=rows,
                                    in_offset=bass.IndirectOffsetOnAxis(ap=stage[:, g, j:j + 1], axis=0),
                                ).then_inc(row_loaded[j], 16)

        @block.tensor
        def _(pe):
            mm, turn = nc.tensor.matmul, nc.tensor.transpose

            def freed_wait(q, i, chunks):
                if q < 4:
                    return
                if i is None:
                    e, n = FREE[q - 4]
                    pe.wait_ge(freed[e], n)
                    return
                e, n = FREE[q - 4 + chunks]
                steps = sum(FREE[k][0] == e for k in range(q, q + chunks))
                pe.wait_ge(freed[e], i * steps + (n - steps))

            def tile_wait(g, i):
                pe.wait_ge(w_loaded[g % RING], at(i, 16, 16 * (g // RING + 1)))

            def feat_tile(name, t, rhs, i=None, n=4, before=None, h0=None):
                ln = LIN[name]
                g = ln.tile0 + t
                tile_wait(g, i)
                w = slot(g).rearrange("p (k n) -> p k n", k=DC)
                for m in range(4):
                    q = ln.chunk0 + 4 * t + m
                    freed_wait(q, i, 4 * n)
                    if m == 3 and before is not None:
                        before()
                    for k in range(DC):
                        if h0 is not None and t == 0 and m == 0:
                            pe.wait_ge(h_ready, h0 + k + 1)
                        last = mm(ps[:, q % 4, 0:SEQ], w[:, k, m * P:(m + 1) * P], rhs[:, k, :],
                                  start=(k == 0), stop=(k == DC - 1))
                    last.then_inc(chunk_done, 1)

            def tok_tile(name, t, lhs):
                ln = LIN[name]
                g = ln.tile0 + t
                tile_wait(g, None)
                w = slot(g).rearrange("p (k n) -> p k n", k=DC)
                for m in range(TT):
                    q = ln.chunk0 + TT * t + m
                    freed_wait(q, None, 0)
                    for k in range(DC):
                        last = mm(ps[:, q % 4, :], lhs[:, k, m * P:(m + 1) * P], w[:, k, :],
                                  start=(k == 0), stop=(k == DC - 1))
                    last.then_inc(chunk_done, 1)

            def mod_sum(n, i=None):
                pe.wait_ge(acc_ready, at(i, 2, n + 1))
                if n >= 1:
                    pe.wait_ge(mods_ready, at(i, 2, n))
                s = n % 2
                for m in range(4):
                    last = mm(ps_mod[:, 4 * s + m:4 * s + m + 1], mod_acc[:, s, m * P:(m + 1) * P], ones[:, 0:1],
                              start=True, stop=True)
                last.then_inc(modsum_ready, 1)

            def norm_sum(n):
                pe.wait_ge(squares_ready, n + 1)
                for k in range(DC):
                    last = mm(ps_norm, ones[:, :], SQ[:, k, :], start=(k == 0), stop=(k == DC - 1))
                last.then_inc(sumsq_ready, 1)

            def ffn(w_in, w_out, norm, ada):
                norm_sum(norm)
                more = ada is not None
                feat_tile(w_in, 0, H, h0=8 * norm)
                feat_tile(w_in, 1, H, before=(lambda: mod_sum(ada)) if more else None)
                feat_tile(w_in, 2, H, before=(lambda: mod_sum(ada + 1)) if more else None)
                with pe.Fori(0, 2) as i:
                    for t in range(3, 7):
                        k = ada + 2 + (t - 3) // 2 if more else 0
                        feat_tile(w_in, t, H, i, before=(lambda: mod_sum(k, i)) if more and t % 2 == 0 else None)
                pe.wait_ge(freed["d"], LIN[w_in].freed_d)
                pe.wait_ge(freed["a"], LIN[w_in].freed_a)
                ln = LIN[w_out]
                with pe.Fori(0, 2) as i:
                    for t in range(4):
                        g = ln.tile0 + t
                        tile_wait(g, i)
                        q = ln.chunk0 + t
                        freed_wait(q, i, 4)
                        w = slot(g, WO_TILE).rearrange("p (k n) -> p k n", k=FC)
                        for k in range(FC):
                            last = mm(ps[:, q % 4, 0:SEQ], w[:, k, :], GU[:, k, :], start=(k == 0), stop=(k == FC - 1))
                        last.then_inc(chunk_done, 1)
                        if more and t % 2 == 1:
                            mod_sum(ada + 6 + t // 2, i)

            def attention(kind):
                s0, s1 = STEP0[kind], STEP_END[kind]
                kt = KS if kind == "B" else KT
                v = VS if kind == "B" else V
                hw = {"A": 128, "B": 64, "X": 256}[kind]

                def scores(s):
                    c = s - s0
                    for qt in range(TT):
                        u = 2 * s + qt
                        if s > s0 or s0:
                            pe.wait_ge(logits_ready, u - 1)
                        nk = SEQ if kind == "X" or qt == 1 else P
                        for m in range(2):
                            o = ps_s[qt][:, m, 0:nk]
                            if kind == "X":
                                for e in range(2):
                                    cc = 4 * c + 2 * m + e
                                    last = mm(o, QT[:, cc, qt * P:(qt + 1) * P], kt[:, cc, 0:nk],
                                              start=(e == 0), stop=(e == 1))
                            else:
                                r = slice(64 * m, 64 * m + 64)
                                last = mm(o, QT[r, c, qt * P:(qt + 1) * P], kt[r, c, 0:nk],
                                          start=True, stop=(kind == "A"))
                                if kind == "B":
                                    r = slice(64 * m, 64 * m + 2)
                                    last = mm(o, DQ[r, c, qt * P:(qt + 1) * P], DK[r, c, 0:nk], start=False, stop=True)
                        last.then_inc(scores_done, 1)

                scores(s0)
                for s in range(s0, s1):
                    c = s - s0
                    if s + 1 < s1:
                        scores(s + 1)
                    pe.wait_ge(probs_ready, 2 * s + 2)
                    if s:
                        pe.wait_ge(probsT_ready, s)
                    for m in range(1 if kind == "A" else 2):
                        bank = PT_BANK[m]
                        blocks = [(0, 0), (0, 1), (1, 1)] if kind != "X" else [(0, 0), (0, 1), (1, 0), (1, 1)]
                        for b, (k, qt) in enumerate(blocks):
                            last = turn(ps[:, bank, b * P:(b + 1) * P], PR[:, qt, m, k * P:(k + 1) * P], ident[:, :])
                    last.then_inc(turned, 1)
                    pe.wait_ge(probsT_ready, s + 1)
                    if s:
                        pe.wait_ge(attn_ready, s)
                    if kind == "X":
                        for m in range(2):
                            for e in range(2):
                                f = (2 * c + m) * hw + e * P
                                for k in range(2):
                                    last = mm(ps[:, m, e * SEQ:(e + 1) * SEQ], v[:, k, f:f + P],
                                              PT[:, m, k * SEQ:(k + 1) * SEQ], start=(k == 0), stop=(k == 1))
                    else:
                        for m in range(1 if kind == "A" else 2):
                            f = c * P + m * hw
                            rows = slice(m * hw, m * hw + hw)
                            mm(ps[rows, 0, 0:SEQ], v[:, 0, f:f + hw], PT[:, m, 0:SEQ], start=True, stop=False)
                            last = mm(ps[rows, 0, P:SEQ], v[:, 1, f:f + hw], PT[:, m, SEQ:SEQ + P],
                                      start=False, stop=True)
                    last.then_inc(pv_done, 1)

            pe.wait_ge(vec_consts, 1)
            pe.wait_ge(consts_ready, 3)
            pe.wait_ge(table_ready, 1)
            pe.wait_ge(small_loaded, 80)
            for h in range(A_HEADS):
                if h >= 4:
                    pe.wait_ge(rows_copied, h - 3)
                mm(ps[:, h % 4, :], table_rep[:, h, :], onehot[:, :], start=True, stop=True).then_inc(rows_ready, 1)
            for n in range(6):
                mod_sum(n)
            pe.wait_ge(rows_copied, A_HEADS)
            ffn("f00_in", "f00_out", 0, 6)

            norm_sum(1)
            for t in range(4):
                feat_tile("a_qk", t, H, h0=8, before=(lambda: mod_sum(16 + t - 2)) if t >= 2 else None)
            for t in range(2):
                tok_tile("a_v", t, H)
            pe.wait_ge(freed["a"], LIN["a_v"].freed_a)
            pe.wait_ge(freed["d"], LIN["a_v"].freed_d)
            attention("A")
            for b in range(4):
                pe.wait_ge(sub_sq, b + 1)
                mm(ps[:, b, :], ones[:, :], SQ[:, 2 * b:2 * b + 2, :], start=True, stop=True).then_inc(sub_sum, 1)
            pe.wait_ge(sub_done, 4)
            for t in range(2):
                feat_tile("a_o", t, OT)

            ffn("f01_in", "f01_out", 2, 18)
            norm_sum(3)
            for t in range(2):
                feat_tile("s_k", t, H, h0=24)
            for t in range(2):
                tok_tile("s_v", t, H)
            fw = col("fgate_w", 0, DC * B_HEADS).rearrange("p (k n) -> p k n", k=DC)
            for k in range(DC):
                last = mm(ps_f, fw[:, k, :], H[:, k, :], start=(k == 0), stop=(k == DC - 1))
            last.then_inc(fz_done, 1)

            ffn("f10_in", "f10_out", 4, 28)
            norm_sum(5)
            for t in range(2):
                feat_tile("b_q", t, H, h0=40, before=(lambda: mod_sum(38 + t)))
            pe.wait_ge(freed["a"], LIN["b_q"].freed_a)
            pe.wait_ge(freed["d"], LIN["s_v"].freed_d)
            pe.wait_ge(decay_loaded, 64)
            attention("B")
            pe.wait_ge(attn_ready, STEP_END["B"])
            for t in range(2):
                feat_tile("b_o", t, OT)
            ffn("f11_in", "f11_out", 6, None)
            norm_sum(N_FINAL)

            norm_sum(N_MIX)
            for t in range(8):
                feat_tile("mix_a", t, H, h0=8 * N_MIX)
            for t in range(6):
                feat_tile("mix_b", t, H)
                if t == 1:
                    pe.wait_ge(conv_done, DC)
                    for k in range(DC):
                        last = mm(ps_norm, ones[:, :], Z[:, k, :], start=(k == 0), stop=(k == DC - 1))
                    last.then_inc(mean_sum, 1)
                if t == 3:
                    pe.wait_ge(ln_sq, 1)
                    for k in range(DC):
                        last = mm(ps_norm, ones[:, :], SQ[:, k, :], start=(k == 0), stop=(k == DC - 1))
                    last.then_inc(ln_sum, 1)
            pe.wait_ge(freed["d"], LIN["mix_b"].freed_d)
            for t in range(2):
                feat_tile("sc_out", t, C3)
            pe.wait_ge(ln_ready, DC)
            for t in range(2):
                feat_tile("cf_out", t, H)
            pe.wait_ge(freed["d"], LIN["cf_out"].freed_d)
            for t in range(2):
                feat_tile("mix_out", t, SG)

            norm_sum(N_MEM)
            for t in range(2):
                feat_tile("x_k", t, H, h0=8 * N_MEM)
            for t in range(2):
                tok_tile("x_v", t, H)
            norm_sum(N_XA)
            for t in range(2):
                feat_tile("x_q", t, H, h0=8 * N_XA)
            pe.wait_ge(freed["a"], LIN["x_q"].freed_a)
            pe.wait_ge(freed["d"], LIN["x_v"].freed_d)
            attention("X")
            pe.wait_ge(attn_ready, STEP_END["X"])
            for t in range(2):
                feat_tile("x_o", t, OT)

            norm_sum(N_PEER)
            for t in range(4):
                feat_tile("pq", t, H, h0=8 * N_PEER)
            pe.wait_ge(freed["a"], LIN["pq"].freed_a)
            pe.wait_ge(freed["d"], LIN["pq"].freed_d)
            for t in range(TT):
                if t:
                    pe.wait_ge(s_ready, 4 * t)
                for hp in range(2 * PH):
                    last = mm(ps[:, hp // 4, (hp % 4) * NK:(hp % 4 + 1) * NK], QP[:, hp, t * P:(t + 1) * P],
                              subk[:, hp % 2, :], start=True, stop=True)
                    if hp % 4 == 3:
                        last.then_inc(sub_scores, 1)
            for n, src in enumerate((H, X)):
                for t in range(TT):
                    for half in range(2):
                        b = (2 * n + t) * 2 + half
                        if b >= 2:
                            pe.wait_ge(tok_ready, b - 1)
                        for c in range(4):
                            last = turn(ps[:, 5 + b % 2, c * P:(c + 1) * P], src[:, 4 * half + c, t * P:(t + 1) * P],
                                        ident[:, :])
                        last.then_inc(tok_turned, 1)

        @block.scalar
        def _(act):
            step = Chain(act, act_step)
            f = nc.scalar.activation

            def norm(n, src, ready):
                ready()
                f(SQ[:, :, :], src[:, :, :], ACT.Square).then_inc(squares_ready, 1)
                act.wait_ge(sumsq_ready, n + 1)
                f(root[:, :], ps_norm, ACT.Sqrt, scale=1.0 / D, bias=eps[:, :]).then_inc(root_ready, 1)
                if NORMS[n][1] is not None:
                    for k in range(DC):
                        act.wait_ge(scaled_ready, 8 * n + k + 1)
                        f(H[:, k, :], H[:, k, :], ACT.Identity,
                          bias=mods[:, NORMS[n][1] + k:NORMS[n][1] + k + 1]).then_inc(h_ready, 1)

            def silus(w_in):
                ln = LIN[w_in]

                def one(j, i=None):
                    q = ln.chunk0 + 2 * j
                    act.wait_ge(chunk_done, at(i, 16, q + 1))
                    if j >= 2:
                        act.wait_ge(freed["d"], at(i, 8, FREE[q - 3][1]))
                    f(silu[:, j % 2, :], ps[:, q % 4, 0:SEQ], ACT.Silu).then_inc(freed["a"], 1)

                for j in range(6):
                    one(j)
                with act.Fori(0, 2) as i:
                    for j in range(6, 14):
                        one(j, i)

            def take(name, q, dst, func=ACT.Copy, **kw):
                q = LIN[name].chunk0 + q
                act.wait_ge(chunk_done, q + 1)
                assert FREE[q][0] == "a"
                n = dst.shape[-1]
                f(dst, ps[:, q % 4, 0:n], func, **kw).then_inc(freed["a"], 1)

            def exps(s):
                par = s % 2
                kind = STEPS[s][0]
                for qt in range(TT):
                    act.wait_ge(logits_ready, 2 * s + qt + 1)
                    if s:
                        act.wait_ge(probs_ready, 2 * s + qt - 1)
                    nk = SEQ if kind == "X" or qt == 1 else P
                    for m in range(2):
                        last = f(EX[:, qt, m, 0:nk], LG[:, qt, m, 0:nk], ACT.Exp, bias=nmax[:, par, qt, m:m + 1],
                                 accum_out=rowsum[:, par, qt, m:m + 1])
                    last.then_inc(exp_ready, 1)

            def attention(kind):
                s0, s1 = STEP0[kind], STEP_END[kind]
                exps(s0)
                for s in range(s0, s1):
                    c = s - s0
                    act.wait_ge(turned, s + 1)
                    if s:
                        act.wait_ge(pv_done, s)
                    n = 512 if kind == "X" else 384
                    for m in range(1 if kind == "A" else 2):
                        last = f(PT[:, m, 0:n], ps[:, PT_BANK[m], 0:n], ACT.Copy)
                    last.then_inc(probsT_ready, 1)
                    if s + 1 < s1:
                        exps(s + 1)
                    act.wait_ge(pv_done, s + 1)
                    if kind == "X":
                        f(OT[:, 4 * c:4 * c + 4, :].rearrange("p (a b) n -> p a (b n)", a=2), ps[:, 0:2, :],
                          ACT.Copy).then_inc(attn_ready, 1)
                    else:
                        f(OT[:, c, :], ps[:, 0, 0:SEQ], ACT.Copy).then_inc(attn_ready, 1)

            act.wait_ge(prm_loaded, 16)
            act.wait_ge(vec_consts, 1)
            f(c_act[:, :], col("c", 0, DC), ACT.Silu).then_inc(c_ready, 1)
            act.wait_ge(lam_sum_ready, 1)
            f(lam_exp[:, :], lam_sum[:, :], ACT.Exp).then_inc(lam_exp_ready, 1)
            for h in range(A_HEADS):
                act.wait_ge(rows_ready, h + 1)
                f(stg[:, h, :], ps[:, h % 4, :], ACT.Copy).then_inc(rows_copied, 1)
            act.wait_ge(rows_copied, A_HEADS)
            act.dma_start(bias_rows.rearrange("h (p j) -> p h j", p=P), stg).then_inc(rows_written, 16)
            act.wait_ge(rows_written, 16)
            act.dma_start(bias[:, :, :], bias_rows[:, 0:P * 511].rearrange("h (p x) -> p h x", p=P)[:, :, 127:127 + SEQ]
                          ).then_inc(bias_loaded, 16)
            norm(0, X, lambda: act.wait_ge(x_loaded, 16))
            silus("f00_in")

            norm(1, X, lambda: act.wait_ge(freed["d"], LIN["f00_out"].freed_d))
            for q in range(8):
                take("a_qk", q, QT[:, q, :], scale=HD ** -0.5)
            for t in range(2):
                take("a_v", 2 * t, V[:, 0, t * 512:(t + 1) * 512])
            attention("A")
            for b in range(4):
                act.wait_ge(attn_ready, 2 * b + 2)
                f(SQ[:, 2 * b:2 * b + 2, :], OT[:, 2 * b:2 * b + 2, :], ACT.Square).then_inc(sub_sq, 1)
            for b in range(4):
                act.wait_ge(sub_sum, b + 1)
                f(H[:, 2 * b:2 * b + 2, :].rearrange("p a n -> p (a n)"), ps[:, b, :], ACT.Sqrt, scale=1.0 / P,
                  bias=eps[:, :]).then_inc(sub_root, 1)

            norm(2, X, lambda: act.wait_ge(freed["d"], LIN["a_o"].freed_d))
            silus("f01_in")
            norm(3, X, lambda: act.wait_ge(freed["d"], LIN["f01_out"].freed_d))
            for t in range(2):
                take("s_v", 2 * t, VS[:, 0, t * 512:(t + 1) * 512])
            act.wait_ge(fz_done, 1)
            step(f(f_z[:, :], ps_f, ACT.Identity, bias=fgate_b[:, :]))
            step(f(f_t[:, :], f_z[:, :], ACT.Abs))
            step(f(f_t[:, :], f_t[:, :], ACT.Exp, scale=-1.0))
            f(f_t[:, :], f_t[:, :], ACT.Ln, bias=1.0).then_inc(fz_ln, 1)

            norm(4, X, lambda: None)
            silus("f10_in")
            norm(5, X, lambda: act.wait_ge(freed["d"], LIN["f10_out"].freed_d))
            for q in range(8):
                take("b_q", q, QT[:, q, :], scale=HD ** -0.5)
            attention("B")
            norm(6, X, lambda: act.wait_ge(freed["d"], LIN["b_o"].freed_d))
            silus("f11_in")
            norm(N_FINAL, X, lambda: act.wait_ge(freed["d"], LIN["f11_out"].freed_d))

            norm(N_MIX, X, lambda: act.wait_ge(h_ready, 8 * (N_FINAL + 1)))
            for t in range(8):
                if t >= 2:
                    act.wait_ge(freed["d"], FREE[LIN["mix_a"].chunk0 + 4 * (t - 2) + 3][1])
                take("mix_a", 4 * t, T0[:, t % 2, :])
                take("mix_a", 4 * t + 2, T1[:, t % 2, :], ACT.Sigmoid, bias=col("cf_b_pw1", 8 + t))
            act.wait_ge(mean_sum, 1)
            f(ZB, ps_norm, ACT.Copy, scale=1.0 / D).then_inc(mean_ready, 1)
            for q in range(4):
                take("mix_b", 8 + q, SG[:, q, :], ACT.Sigmoid)
            act.wait_ge(centred, 1)
            f(SQ[:, :, :], Z, ACT.Square).then_inc(ln_sq, 1)
            for q in range(4, 8):
                take("mix_b", 8 + q, SG[:, q, :], ACT.Sigmoid)
            act.wait_ge(ln_sum, 1)
            f(root[:, :], ps_norm, ACT.Sqrt, scale=1.0 / D, bias=eps[:, :]).then_inc(ln_root, 1)
            for q in range(8):
                take("mix_b", 16 + q, CG[:, q, :], ACT.Sigmoid)
            act.wait_ge(ln_scaled, 1)
            act.wait_ge(chunk_done, LIN["mix_b"].chunk_end)
            for k in range(DC):
                f(H[:, k, :], Z[:, k, :], ACT.Silu, scale=col("ln_g", k), bias=col("ln_b", k)).then_inc(ln_ready, 1)

            norm(N_MEM, KS, lambda: act.wait_ge(mem_loaded, 16))
            for t in range(2):
                take("x_v", 2 * t, V[:, 0, t * 512:(t + 1) * 512])
            norm(N_XA, X, lambda: act.wait_ge(freed["d"], LIN["mix_out"].freed_d))
            for q in range(8):
                take("x_q", q, QT[:, q, :], scale=(D // 4) ** -0.5)
            attention("X")
            norm(N_PEER, X, lambda: act.wait_ge(freed["d"], LIN["x_o"].freed_d))
            for q in range(0, 16, 2):
                take("pq", q, QP[:, q, :])
            for t in range(TT):
                if t:
                    act.wait_ge(s_used, t)
                for b in range(4):
                    act.wait_ge(sub_scores, 4 * t + b + 1)
                    f(S[:, 4 * b:4 * b + 4, :].rearrange("p a n -> p (a n)"), ps[:, b, :], ACT.Copy).then_inc(s_ready, 1)
                if t == 0:
                    for b in range(8):
                        dst = (HTOK, XTOK)[b // 4]
                        act.wait_ge(tok_turned, b + 1)
                        f(dst[:, (b // 2) % 2, (b % 2) * 512:(b % 2 + 1) * 512], ps[:, 5 + b % 2, :],
                          ACT.Copy).then_inc(tok_ready, 1)
                act.wait_ge(gate_diff, t + 1)
                f(GT[:, t, :], GT[:, t, :], ACT.Exp).then_inc(gate_exp, 1)
            for t in range(TT):
                act.wait_ge(dots_ready, t + 1)
                f(DOT[:, t, :], DOT[:, t, :], ACT.Gelu).then_inc(gelu_ready, 1)
                act.wait_ge(y_ready, t + 1)
                f(YO[:, t, :], YACC[:, 0, :], ACT.Square, accum_out=YS[:, t:t + 1]).then_inc(act_step, 1)
                step.n += 1
                act.wait_ge(act_step, step.n)
                f(YS[:, t:t + 1], YS[:, t:t + 1], ACT.Sqrt, scale=1.0 / D, bias=eps[:, :]).then_inc(yroot_ready, 1)

        @block.vector
        def _(dve):
            step = Chain(dve, dve_step)
            v = nc.vector

            def mod_acc_tile(n, i=None):
                s = n % 2
                dve.wait_ge(mod_loaded[s], at(i, 16, 16 * (n // 2 + 1)))
                w = mod_ring[:, s * TILE:(s + 1) * TILE].rearrange("p (k n) -> p k n", k=DC)
                step(v.tensor_scalar(mod_acc[:, s, :], w[:, 0, :], c_act[:, 0:1], None, ALU.mult))
                for k in range(1, DC):
                    ins = v.scalar_tensor_tensor(mod_acc[:, s, :], w[:, k, :], c_act[:, k:k + 1], mod_acc[:, s, :],
                                                 ALU.mult, ALU.add)
                    if k < DC - 1:
                        step(ins)
                ins.then_inc(acc_ready, 1)

            def mod_take(n, i=None):
                dve.wait_ge(modsum_ready, at(i, 2, n + 1))
                s = n % 2
                if i is None:
                    dst, b = mods[:, 4 * n:4 * n + 4], col("ada_b", 4 * n, 4)
                else:
                    dst = mods[:, bass.ds(i * 8 + 4 * n, 4)]
                    b = prm[:, bass.ds(i * 8 + (COL["ada_b"] + 4 * n), 4)]
                v.tensor_tensor(dst, ps_mod[:, 4 * s:4 * s + 4], b, ALU.add).then_inc(mods_ready, 1)

            def norm(n, src, dst, mods_done=None, h_free=None):
                g, m0 = NORMS[n]
                if m0 is not None:
                    dve.wait_ge(mods_ready, mods_done)
                    step(v.scalar_tensor_tensor(gain[:, :], mods[:, m0 + 8:m0 + 16], 1.0, prm[:, g:g + 8],
                                                ALU.add, ALU.mult))
                dve.wait_ge(root_ready, n + 1)
                step(v.reciprocal(rinv[:, :], root[:, :]))
                if h_free is not None:
                    dve.wait_ge(chunk_done, h_free)
                for k in range(DC):
                    gk = prm[:, g + k:g + k + 1] if m0 is None else gain[:, k:k + 1]
                    ins = v.scalar_tensor_tensor(dst[:, k, :], src[:, k, :], gk, rinv[:, :], ALU.mult, ALU.mult)
                    if m0 is None:
                        ins.then_inc(h_ready, 1)
                    else:
                        ins.then_inc(scaled_ready, 1)
                if m0 is None:
                    dve.wait_ge(h_ready, 8 * (n + 1))
                    dve.sem_inc(scaled_ready, 8)

            def take(name, q, op, sig=None):
                q = LIN[name].chunk0 + q
                dve.wait_ge(chunk_done, q + 1)
                assert FREE[q][0] == "d"
                op(ps[:, q % 4, :]).then_inc(freed["d"], 1)

            def ffn(w_in, w_out, gate0, ada):
                ln = LIN[w_in]
                more = ada is not None

                def product(j, i=None):
                    q = ln.chunk0 + 2 * j + 1
                    dve.wait_ge(chunk_done, at(i, 16, q + 1))
                    dve.wait_ge(freed["a"], at(i, 8, FREE[q - 1][1]))
                    dst = GU[:, j, :] if i is None else GU[:, bass.ds(i * 8 + j, 1), :].rearrange("p a n -> p (a n)")
                    v.tensor_tensor(dst, ps[:, q % 4, 0:SEQ], silu[:, j % 2, :], ALU.mult).then_inc(freed["d"], 1)

                def tile(t, n, i=None):
                    if n is not None:
                        mod_acc_tile(n, i)
                    product(2 * t, i)
                    if n is not None:
                        mod_take(n, i)
                    product(2 * t + 1, i)

                tile(0, None)
                tile(1, ada if more else None)
                tile(2, ada + 1 if more else None)
                with dve.Fori(0, 2) as i:
                    if more:
                        step.enter(i, 14)
                    for t in range(3, 7):
                        tile(t, ada + 2 + (t - 3) // 2 if more and t % 2 == 0 else None, i)
                    if more:
                        step.leave(2)
                step(v.tensor_scalar(half_gate[:, :], mods[:, gate0:gate0 + 8], 0.5, None, ALU.mult))
                lo = LIN[w_out]
                with dve.Fori(0, 2) as i:
                    if more:
                        step.enter(i, 14)
                    for t in range(4):
                        n = ada + 6 + t // 2 if more else None
                        if more and t % 2 == 0:
                            mod_acc_tile(n, i)
                        q = lo.chunk0 + t
                        dve.wait_ge(chunk_done, i * 4 + (q + 1))
                        xk = X[:, bass.ds(i * 4 + t, 1), :].rearrange("p a n -> p (a n)")
                        v.scalar_tensor_tensor(xk, ps[:, q % 4, 0:SEQ], half_gate[:, bass.ds(i * 4 + t, 1)], xk,
                                               ALU.mult, ALU.add).then_inc(freed["d"], 1)
                        if more and t % 2 == 1:
                            mod_take(n, i)
                    if more:
                        step.leave(2)

            def logits(s):
                kind, c = STEPS[s]
                par = s % 2
                for qt in range(TT):
                    u = 2 * s + qt
                    dve.wait_ge(scores_done, u + 1)
                    if s:
                        dve.wait_ge(exp_ready, u - 1)
                    nk = SEQ if kind == "X" or qt == 1 else P
                    k0 = 0 if nk == SEQ else P
                    lg, sc = LG[:, qt, :, 0:nk], ps_s[qt][:, :, 0:nk]
                    if kind == "X":
                        step(v.tensor_copy(lg, sc))
                    else:
                        b = bias[:, c, k0:SEQ] if kind == "A" else mask[:, k0:SEQ]
                        step(v.tensor_tensor(lg, sc, b.unsqueeze(1).broadcast_to([P, 2, nk]), ALU.add))
                    step(v.reduce_max(rowmax[:, par, qt, :], lg, axis=AX.X))
                    v.tensor_scalar(nmax[:, par, qt, :], rowmax[:, par, qt, :], -1.0, None, ALU.mult
                                    ).then_inc(logits_ready, 1)

            def probs(s):
                kind, c = STEPS[s]
                par = s % 2
                for qt in range(TT):
                    dve.wait_ge(exp_ready, 2 * s + qt + 1)
                    nk = SEQ if kind == "X" or qt == 1 else P
                    r = rscale[:, par, qt, :]
                    step(v.reciprocal(r, rowsum[:, par, qt, :]))
                    if s:
                        dve.wait_ge(turned, s)
                    if kind == "A":
                        step(v.tensor_tensor(r, r, lam_vec[:, :], ALU.mult))
                        step(v.tensor_scalar(PR[:, qt, 0, 0:nk], EX[:, qt, 0, 0:nk], r[:, 0:1], None, ALU.mult))
                        v.scalar_tensor_tensor(PR[:, qt, 0, 0:nk], EX[:, qt, 1, 0:nk], r[:, 1:2],
                                               PR[:, qt, 0, 0:nk], ALU.mult, ALU.add).then_inc(probs_ready, 1)
                    else:
                        v.tensor_tensor(PR[:, qt, :, 0:nk], EX[:, qt, :, 0:nk],
                                        r.unsqueeze(2).broadcast_to([P, 2, nk]), ALU.mult).then_inc(probs_ready, 1)

            def attention(kind):
                s0, s1 = STEP0[kind], STEP_END[kind]
                logits(s0)
                for s in range(s0, s1):
                    if s + 1 < s1:
                        logits(s + 1)
                    probs(s)

            v.memset(eps[:, :], EPS)
            step(v.memset(ones[:, :], 1.0))
            v.memset(table[NB:NB + 1, :], NEG)
            step(v.memset(lam_vec[:, :], 1.0))
            dve.sem_inc(vec_consts, 1)
            dve.wait_ge(small_loaded, 80)
            v.tensor_copy(table_rep[:, :, :], table[:, :].unsqueeze(2).broadcast_to([NB + 1, A_HEADS, P])
                          ).then_inc(table_ready, 1)
            lp = lamp[:, :].rearrange("p (a b n) -> p a b n", a=2, b=2)
            step(v.tensor_tensor(lam_prod[:, :, :], lp[:, :, 0, :], lp[:, :, 1, :], ALU.mult))
            v.reduce_sum(lam_sum[:, :], lam_prod[:, :, :], axis=AX.X).then_inc(lam_sum_ready, 1)
            dve.wait_ge(prm_loaded, 16)
            dve.wait_ge(c_ready, 1)
            mod_acc_tile(0)
            dve.wait_ge(lam_exp_ready, 1)
            step(v.tensor_tensor(lam_vec[:, 1:2], lam_exp[:, 1:2], lam_exp[:, 0:1], ALU.subtract))
            step(v.tensor_scalar(lam_vec[:, 1:2], lam_vec[:, 1:2], -LAM_INIT, None, ALU.add))
            step(v.tensor_scalar(sub_gain[:, :], col("subln_g"), 1.0 - LAM_INIT, None, ALU.mult))
            for n in range(1, 6):
                mod_acc_tile(n)
                mod_take(n - 1)
            mod_take(5)
            dve.wait_ge(x_loaded, 16)
            norm(0, X, H, 6)
            dve.wait_ge(rows_written, 16)
            ffn("f00_in", "f00_out", MOD_L0 + 16, 6)

            norm(1, X, H, 12)
            for q in range(8, 16):
                if q in (8, 12):
                    mod_acc_tile(16 + (q - 8) // 4)
                if q in (11, 15):
                    mod_take(16 + (q - 8) // 4)
                take("a_qk", q, lambda p: v.tensor_copy(KT[:, q - 8, :], p[:, 0:SEQ]))
            for t in range(2):
                take("a_v", 2 * t + 1, lambda p: v.tensor_copy(V[:, 1, t * 512:(t + 1) * 512], p))
            dve.wait_ge(bias_loaded, 16)
            attention("A")
            for b in range(4):
                hq = H[:, 2 * b:2 * b + 2, :]
                oq = OT[:, 2 * b:2 * b + 2, :]
                dve.wait_ge(sub_root, b + 1)
                step(v.reciprocal(hq, hq))
                v.scalar_tensor_tensor(oq, oq, sub_gain[:, :], hq, ALU.mult, ALU.mult).then_inc(sub_done, 1)

            def residual(name, gate0=None):
                for q in range(8):
                    if gate0 is None:
                        take(name, q, lambda p: v.tensor_tensor(X[:, q, :], p[:, 0:SEQ], X[:, q, :], ALU.add))
                    else:
                        take(name, q, lambda p: v.scalar_tensor_tensor(
                            X[:, q, :], p[:, 0:SEQ], mods[:, gate0 + q:gate0 + q + 1], X[:, q, :], ALU.mult, ALU.add))

            residual("a_o", MOD_L0 + 40)
            norm(2, X, H, 18)
            ffn("f01_in", "f01_out", MOD_L0 + 64, 18)

            norm(3, X, H, 22)
            for q in range(8):
                take("s_k", q, lambda p: v.tensor_copy(KS[:, q, :], p[:, 0:SEQ]))
            for t in range(2):
                take("s_v", 2 * t + 1, lambda p: v.tensor_copy(VS[:, 1, t * 512:(t + 1) * 512], p))
            dve.wait_ge(fz_ln, 1)
            step(v.tensor_scalar(f_z[:, :], f_z[:, :], 0.0, None, ALU.min))
            step(v.tensor_tensor(f_z[:, :], f_z[:, :], f_t[:, :], ALU.subtract))
            step(v.memset(f_t[:, :], 1.0))
            step(v.tensor_tensor_scan(f_sum[:, :], f_t[:, :], f_z[:, :], 0.0, ALU.mult, ALU.add))
            v.tensor_scalar(f_neg[:, :], f_sum[:, :], -1.0, None, ALU.mult).then_inc(f_ready, 1)

            norm(4, X, H, 28)
            ffn("f10_in", "f10_out", MOD_L1 + 16, 28)
            for tile_ in (DQ, DK):
                for odd in range(2):
                    v.memset(tile_[64 * odd:64 * odd + 2, :, :], 1.0).then_inc(decay_cleared, 1)
            norm(5, X, H, 34)
            for t in range(2):
                mod_acc_tile(38 + t)
                mod_take(38 + t)
            attention("B")
            residual("b_o", MOD_L1 + 40)
            norm(6, X, H, 40)
            ffn("f11_in", "f11_out", MOD_L1 + 64, None)
            norm(N_FINAL, X, X)

            v.memset(U[:, :, 0:SCK - 1], 0.0)
            step(v.memset(CV[:, :, 0:CFK - 1], 0.0))
            norm(N_MIX, X, H)
            for c in range(DC):
                fa = FREE[LIN["mix_a"].chunk0 + 4 * c][1]
                dve.wait_ge(freed["a"], fa)
                take("mix_a", 4 * c + 1, lambda p: v.tensor_tensor(U[:, c, SCK - 1:], p[:, 0:SEQ], T0[:, c % 2, :], ALU.mult))
                dve.wait_ge(freed["a"], fa + 1)
                take("mix_a", 4 * c + 3, lambda p: v.scalar_tensor_tensor(
                    CV[:, c, CFK - 1:], p[:, 0:SEQ], col("cf_b_pw1", c), T1[:, c % 2, :], ALU.add, ALU.mult))
                dve.wait_ge(freed["d"], FREE[LIN["mix_a"].chunk0 + 4 * c + 3][1])
                w3 = lambda k: col("sc_w", 8 * k + c)
                w31 = lambda k: col("cf_w", 8 * k + c)
                step(v.tensor_scalar(Z[:, c, :], CV[:, c, 0:SEQ], w31(0), col("cf_conv_b", c), ALU.mult, ALU.add), lag=1)
                step(v.tensor_scalar(SQ[:, c, :], CV[:, c, 1:1 + SEQ], w31(1), None, ALU.mult), lag=1)
                for k in range(2, CFK):
                    dst = (Z, SQ)[k % 2]
                    step(v.scalar_tensor_tensor(dst[:, c, :], CV[:, c, k:k + SEQ], w31(k), dst[:, c, :],
                                                ALU.mult, ALU.add), lag=1)
                step(v.tensor_scalar(C3[:, c, :], U[:, c, 0:SEQ], w3(0), None, ALU.mult))
                v.tensor_tensor(Z[:, c, :], Z[:, c, :], SQ[:, c, :], ALU.add).then_inc(conv_done, 1)
                for k in range(1, SCK):
                    step(v.scalar_tensor_tensor(C3[:, c, :], U[:, c, k:k + SEQ], w3(k), C3[:, c, :], ALU.mult, ALU.add))
            for q in range(8):
                take("mix_b", q, lambda p: v.tensor_tensor(C3[:, q, :], p[:, 0:SEQ], C3[:, q, :], ALU.mult))
            dve.wait_ge(mean_ready, 1)
            v.tensor_tensor(Z, Z, ZB.unsqueeze(1).broadcast_to([P, DC, SEQ]), ALU.subtract).then_inc(centred, 1)
            dve.wait_ge(ln_root, 1)
            dve.wait_ge(ln_sq, 1)
            step(v.reciprocal(rinv[:, :], root[:, :]))
            v.tensor_tensor(Z, Z, rinv[:, :].unsqueeze(1).broadcast_to([P, DC, SEQ]), ALU.mult).then_inc(ln_scaled, 1)
            dve.wait_ge(freed["a"], LIN["mix_b"].freed_a)
            for q in range(8):
                take("sc_out", q, lambda p: v.tensor_tensor(SG[:, q, :], p[:, 0:SEQ], SG[:, q, :], ALU.mult))
            for q in range(8):
                qq = LIN["cf_out"].chunk0 + q
                dve.wait_ge(chunk_done, qq + 1)
                step(v.scalar_tensor_tensor(CG[:, q, :], ps[:, qq % 4, 0:SEQ], col("b_pw2", q), CG[:, q, :],
                                            ALU.add, ALU.mult))
                v.tensor_tensor(SG[:, q, :], SG[:, q, :], CG[:, q, :], ALU.add).then_inc(freed["d"], 1)
            residual("mix_out")

            norm(N_MEM, KS, H, h_free=LIN["mix_out"].chunk_end)
            for q in range(8):
                take("x_k", q, lambda p: v.tensor_copy(KT[:, q, :], p[:, 0:SEQ]))
            for t in range(2):
                take("x_v", 2 * t + 1, lambda p: v.tensor_copy(V[:, 1, t * 512:(t + 1) * 512], p))
            norm(N_XA, X, H, h_free=LIN["x_v"].chunk_end)
            attention("X")
            residual("x_o")
            norm(N_PEER, X, H)
            for q in range(1, 16, 2):
                take("pq", q, lambda p: v.tensor_copy(QP[:, q, :], p[:, 0:SEQ]))

            def select(t):
                for hp in range(2 * PH):
                    if hp % 4 == 0:
                        dve.wait_ge(s_ready, 4 * t + hp // 4 + 1)
                    step(v.max(TV[:, hp, 0:8], S[:, hp, :]), lag=1)
                step(v.memset(GS[:, 0:8], 0.0))
                for hp in range(2 * PH):
                    step(v.max_index(TI[:, hp, 0:8], TV[:, hp, 0:8], S[:, hp, :]), lag=1)
                    step(v.match_replace(S2[:, hp, :], TV[:, hp, 0:8], S[:, hp, :], -3.0e38), lag=1)
                step(v.memset(GS[:, 0:8], 0.0))
                for hp in range(2 * PH):
                    step(v.max(TV[:, hp, 8:16], S2[:, hp, :]), lag=1)
                step(v.memset(GS[:, 0:8], 0.0))
                for hp in range(2 * PH):
                    step(v.max_index(TI[:, hp, 8:16], TV[:, hp, 8:16], S2[:, hp, :]), lag=1)
                step(v.memset(GS[:, 0:8], 0.0))
                v.tensor_copy(TIF, TI)
                tv = TV.rearrange("p (h s) k -> p h s k", s=2)
                tif = TIF.rearrange("p (h s) k -> p h s k", s=2)
                full = [P, PH, TK, TK]
                step(v.tensor_tensor(CA.rearrange("p h (a b) -> p h a b", a=TK), tv[:, :, 0, :].unsqueeze(3).broadcast_to(full),
                                     tv[:, :, 1, :].unsqueeze(2).broadcast_to(full), ALU.add))
                for h in range(PH):
                    step(v.max(FV[:, h, 0:8], CA[:, h, :]), lag=1)
                step(v.memset(GS[:, 0:8], 0.0))
                for h in range(PH):
                    step(v.max_index(FP[:, h, 0:8], FV[:, h, 0:8], CA[:, h, :]), lag=1)
                    step(v.match_replace(CA2[:, h, :], FV[:, h, 0:8], CA[:, h, :], -3.0e38), lag=1)
                step(v.memset(GS[:, 0:8], 0.0))
                for h in range(PH):
                    step(v.max(FV[:, h, 8:16], CA2[:, h, :]), lag=1)
                step(v.memset(GS[:, 0:8], 0.0))
                for h in range(PH):
                    step(v.max_index(FP[:, h, 8:16], FV[:, h, 8:16], CA2[:, h, :]), lag=1)
                step(v.memset(GS[:, 0:8], 0.0))
                gt = GT[:, t, :].rearrange("p (h k) -> p h k", h=PH)
                v.tensor_tensor(gt, FV, FV[:, :, 0:1].broadcast_to([P, PH, TK]), ALU.subtract).then_inc(gate_diff, 1)
                fp = FP.rearrange("p h k -> p (h k)")
                v.tensor_scalar(AI, fp, 4, None, ALU.logical_shift_right)
                step(v.tensor_scalar(BI, fp, TK - 1, None, ALU.bitwise_and))
                v.tensor_copy(AF, AI)
                step(v.tensor_copy(BF, BI))
                for src, half, dst, eq in ((AF, 0, I0, EQ), (BF, 1, I1, EQ2)):
                    step(v.tensor_tensor(eq, src.unsqueeze(2).broadcast_to([P, SLOTS_PER_TILE, TK]),
                                         iota16[:, :].unsqueeze(1).broadcast_to([P, SLOTS_PER_TILE, TK]), ALU.is_equal))
                    e4 = eq.rearrange("p (h k) j -> p h k j", h=PH)
                    step(v.tensor_tensor(e4, e4, tif[:, :, half, :].unsqueeze(2).broadcast_to(full), ALU.mult))
                    step(v.reduce_sum(dst, eq, axis=AX.X))
                v.scalar_tensor_tensor(IDX[:, t, :], I0, float(NK), I1, ALU.mult, ALU.add).then_inc(idx_ready, 1)
                dve.wait_ge(idx_ready, t + 1)
                dve.sem_inc(s_used, 1)
                dve.wait_ge(gate_exp, t + 1)
                step(v.reduce_sum(GS[:, 8:16], gt, axis=AX.X))
                step(v.reciprocal(GS[:, 8:16], GS[:, 8:16]))
                step(v.tensor_tensor(gt, gt, GS[:, 8:16].unsqueeze(2).broadcast_to([P, PH, TK]), ALU.mult))

            dve.sem_inc(rows_free, GROUP)
            select(0)
            select(1)
            dve.wait_ge(tok_ready, 8)
            dve.wait_ge(gfin_loaded, 16)
            for t in range(TT):
                seg = 2 * t
                with dve.Fori(0, N_GROUPS) as i:
                    base = seg * N_GROUPS
                    for j in range(GROUP):
                        dve.wait_ge(row_loaded[j], i * 16 + 16 * (base + 1))
                        v.tensor_tensor_reduce(out=junk[:, j % 2, :], in0=ring[:, j * D:(j + 1) * D], in1=HTOK[:, t, :],
                                               scale=1.0, scalar=0.0, op0=ALU.mult, op1=ALU.add,
                                               accum_out=dot16[:, j:j + 1]).then_inc(rows_free, 1)
                        if j >= 1:
                            dve.wait_ge(rows_free, i * GROUP + (GROUP * (base + 1) + j))
                    dve.wait_ge(rows_free, i * GROUP + GROUP * (base + 2))
                    step.enter(i, 1)
                    step(v.tensor_copy(DOT[:, t, bass.ds(i * GROUP, GROUP)], dot16[:, :]))
                    step.leave(1)
                    step.n -= 1
                step.n += N_GROUPS
                dve.sem_inc(dots_ready, 1)
                step(v.memset(YACC[:, 0, :], 0.0))
                step(v.memset(YACC[:, 1, :], 0.0))
                dve.wait_ge(gelu_ready, t + 1)
                step(v.tensor_tensor(CF[:, t, :], DOT[:, t, :], GT[:, t, :], ALU.mult))
                seg = 2 * t + 1
                with dve.Fori(0, N_GROUPS) as i:
                    base = seg * N_GROUPS
                    step.enter(i, 1)
                    step(v.tensor_copy(coef16[:, :], CF[:, t, bass.ds(i * GROUP, GROUP)]))
                    step.leave(1)
                    step.n -= 1
                    for j in range(GROUP):
                        dve.wait_ge(row_loaded[j], i * 16 + 16 * (base + 1))
                        y = YACC[:, j % 2, :]
                        v.scalar_tensor_tensor(y, ring[:, j * D:(j + 1) * D], coef16[:, j:j + 1], y,
                                               ALU.mult, ALU.add).then_inc(rows_free, 1)
                        if j >= 1:
                            dve.wait_ge(rows_free, i * GROUP + (GROUP * (base + 1) + j))
                    dve.wait_ge(rows_free, i * GROUP + GROUP * (base + 2))
                step.n += N_GROUPS
                step(v.tensor_tensor(YACC[:, 0, :], YACC[:, 0, :], YACC[:, 1, :], ALU.add))
                v.tensor_tensor(YACC[:, 0, :], YACC[:, 0, :], XTOK[:, t, :], ALU.add).then_inc(y_ready, 1)
                dve.wait_ge(yroot_ready, t + 1)
                step(v.reciprocal(YS[:, 2 + t:3 + t], YS[:, t:t + 1]))
                v.scalar_tensor_tensor(YO[:, t, :], YACC[:, 0, :], YS[:, 2 + t:3 + t], gfin,
                                       ALU.mult, ALU.mult).then_inc(yo_ready, 1)


def relative_buckets():
    rel = 255 - np.arange(512)
    n = np.maximum(rel, 0)
    exact = NB // 2
    large = exact + (np.log(np.maximum(n, 1).astype(np.float32) / exact) / math.log(MAX_DISTANCE / exact)
                     * (NB - exact)).astype(np.int32)
    bucket = np.where(n < exact, n, np.minimum(large, NB - 1))
    bucket = np.where(rel >= 0, bucket, NB)
    return (np.arange(NB + 1)[:, None] == bucket[None, :]).astype(np.float32)


def kernel(**inputs):
    import numpy as _np
    import concourse.bacc as _bacc
    from concourse import mybir as _mybir
    from concourse.bass_utils import run_bass_kernel_spmd as _run

    x = {k: _np.asarray(v) for k, v in inputs.items()}
    cat = _np.concatenate

    def cols(v):
        return v.reshape(-1, P).T

    def tiles(w, order=None):
        k, n = w.shape
        w = w.reshape(k // P, P, n // P, P)
        if order is not None:
            w = w[:, :, order]
        w = w.reshape(k // P, P, -1, 4, P)
        return w.transpose(2, 1, 0, 3, 4).reshape(w.shape[2], P, -1)

    def out_tiles(w):
        return w.reshape(FC, P, DC, P).transpose(2, 1, 0, 3).reshape(DC, P, FC * P)

    pairs = [m + half * FC for m in range(FC) for half in range(2)]
    a = {}
    for la in range(2):
        for s in range(2):
            a[f"f{la}{s}_in"] = tiles(x["ffn_w_in"][la, s], pairs)
            a[f"f{la}{s}_out"] = out_tiles(x["ffn_w_out"][la, s])
    qkv = x["a_w_qkv"][0]
    a["a_qk"], a["a_v"], a["a_o"] = tiles(qkv[:, :2 * D]), tiles(qkv[:, 2 * D:]), tiles(x["a_w_o"][0])
    a["s_k"], a["s_v"] = tiles(x["kv_w"][:, :D]), tiles(x["kv_w"][:, D:])
    a["b_q"], a["b_o"] = tiles(x["b_w_q"][0]), tiles(x["b_w_o"][0])
    a["mix_a"] = tiles(x["w_in_2"][0], [b * DC + c for c in range(DC) for b in (1, 2, 4, 3)])
    a["mix_b"] = tiles(x["w_in_2"][0], [b * DC + c for b in (0, 5, 6) for c in range(DC)])
    a["sc_out"], a["cf_out"] = tiles(x["sc_w_out_2"][0]), tiles(x["cf_w_pw2_2"][0])
    a["mix_out"] = tiles(x["w_mix_out_2"][0])
    a["x_k"], a["x_v"] = tiles(x["w_kv_2"][0][:, :D]), tiles(x["w_kv_2"][0][:, D:])
    a["x_q"], a["x_o"], a["pq"] = tiles(x["w_q_2"][0]), tiles(x["w_xo_2"][0]), tiles(x["w_peer_q_2"][0])
    a["ada"] = cat([tiles(x["ada_w"][0]), tiles(x["kv_ada_w"]), tiles(x["ada_w"][1])])
    a["prm"] = cat([
        cols(x["c"]), cols(x["ada_b"][0]), cols(x["kv_ada_b"]), cols(x["ada_b"][1]), cols(x["norm_g"]),
        cols(x["kv_norm_g"]), cols(x["final_g"]), cols(x["norm_mix_g_2"]), cols(x["cf_b_pw1_2"]),
        cols(x["sc_conv_w_2"]), cols(x["cf_conv_w_2"]), cols(x["cf_conv_b_2"]), cols(x["cf_ln_g_2"]),
        cols(x["cf_ln_b_2"]), cols(x["cf_b_pw2_2"]), cols(x["norm_xa_g_2"]), cols(x["norm_mem_g_2"]),
        cols(x["norm_peer_g_2"]), cols(x["a_subln_g"]),
        x["fgate_w"].reshape(DC, P, B_HEADS).transpose(1, 0, 2).reshape(P, -1)], axis=1)
    a["xT"] = x["x"][0].reshape(SEQ, DC, P).transpose(2, 1, 0)
    a["memT"] = x["mem_2"][0].reshape(SEQ, DC, P).transpose(2, 1, 0)
    a["rel_bias"] = x["rel_bias"]
    a["onehot"] = relative_buckets()
    a["a_lambda"] = x["a_lambda"].reshape(1, -1)
    a["fgate_b"] = x["fgate_b"].reshape(-1, 1)
    a["subkT"] = x["peer_subkeys_2"][0].transpose(2, 0, 1)
    a["final_norm_g"] = x["final_norm_g_2"].reshape(1, -1)
    a["peer_u"], a["peer_v"] = x["peer_u_2"][0], x["peer_v_2"][0]

    nc = _bacc.Bacc("TRN2", target_bir_lowering=False, num_devices=1)
    arrays, aps = {}, {}
    for name, v in a.items():
        arrays["in_" + name] = _np.ascontiguousarray(v)
        aps[name] = nc.dram_tensor("in_" + name, v.shape, _mybir.dt.from_np(v.dtype), kind="ExternalInput").ap()
    out = nc.dram_tensor("out", (TT, P, D), _mybir.dt.float32, kind="ExternalOutput").ap()
    build_program(nc, aps, out)
    r = _run(nc, [arrays], core_ids=[0])
    return r.results[0]["out"].reshape(1, SEQ, D)
```

```python
import math
from contextlib import ExitStack

import numpy as np

import concourse.bass as bass
from concourse import mybir

F32 = mybir.dt.float32
F32R = mybir.dt.float32r
U32 = mybir.dt.uint32
ACT = mybir.ActivationFunctionType
ALU = mybir.AluOpType
AX = mybir.AxisListType

P = 128
D = 1024
DC = D // P
SEQ = 256
TT = SEQ // P
FFN = 256 * ((8 * D // 3 + 255) // 256)
FC = FFN // P
HD = 64
A_HEADS = D // (2 * HD)
B_HEADS = D // HD
NB = 32
MAX_DISTANCE = 128
EPS = 1e-6
LAM_INIT = 0.8 - 0.6 * math.exp(-0.3 * 0)
NEG = -1e30
SCK, CFK = 3, 31
PH, NK, TK = 8, 128, 16
N_EXP = NK * NK
SLOTS_PER_TILE = PH * TK

_COLS = [("c", 8), ("ada_b", 160), ("norm_g", 48), ("kv_norm_g", 8), ("final_g", 8), ("norm_mix_g", 8),
         ("cf_b_pw1", 16), ("sc_w", SCK * 8), ("cf_w", CFK * 8), ("cf_conv_b", 8), ("ln_g", 8), ("ln_b", 8),
         ("b_pw2", 8), ("norm_xa_g", 8), ("norm_mem_g", 8), ("norm_peer_g", 8), ("subln_g", 1),
         ("fgate_w", DC * B_HEADS)]
COL, NCOL = {}, 0
for _n, _w in _COLS:
    COL[_n] = NCOL
    NCOL += _w

ADA_TILES = 80
MOD_L0, MOD_KV, MOD_L1 = 0, 72, 88

G = COL["norm_g"]
NORMS = [(G, MOD_L0), (G + 8, MOD_L0 + 24), (G + 16, MOD_L0 + 48), (COL["kv_norm_g"], MOD_KV),
         (G + 24, MOD_L1), (G + 32, MOD_L1 + 24), (G + 40, MOD_L1 + 48),
         (COL["final_g"], None), (COL["norm_mix_g"], None), (COL["norm_mem_g"], None),
         (COL["norm_xa_g"], None), (COL["norm_peer_g"], None)]
N_FINAL, N_MIX, N_MEM, N_XA, N_PEER = 7, 8, 9, 10, 11

RING = 3
BANKS = 3
BODY = 6
TILE = DC * 2 * P
WO_K = FC // 2
WO_TILE = WO_K * P
_LIN = [("f00_in", 22, TILE, "ad"), ("f00_out", 16, WO_TILE, "d"),
        ("a_q", 4, TILE, "aa"), ("a_k", 4, TILE, "dd"), ("a_v", 4, TILE, "ad"), ("a_o", 4, TILE, "dd"),
        ("f01_in", 22, TILE, "ad"), ("f01_out", 16, WO_TILE, "d"),
        ("s_k", 4, TILE, "dd"), ("s_v", 4, TILE, "ad"),
        ("f10_in", 22, TILE, "ad"), ("f10_out", 16, WO_TILE, "d"),
        ("b_q", 4, TILE, "aa"), ("b_o", 4, TILE, "dd"),
        ("f11_in", 22, TILE, "ad"), ("f11_out", 16, WO_TILE, "d"),
        ("mix_a", 16, TILE, "ad"), ("mix_b", 4, TILE, "dd"), ("mix_g", 8, TILE, "aa"),
        ("sc_out", 4, TILE, "dd"), ("cf_out", 4, TILE, "dd"), ("mix_out", 4, TILE, "dd"),
        ("x_k", 4, TILE, "dd"), ("x_v", 4, TILE, "ad"), ("x_q", 4, TILE, "aa"),
        ("x_o", 4, TILE, "dd"), ("pq", 8, TILE, "ad")]
POOL_SPLITS = ("mix_a", "pq")


class Linear:
    pass


LIN = {}
FREE = []
CHUNK_UNIT = []
TILE_UNIT = []
TILE_WIDTH = []
TILE_POOL = []


def _plan():
    counts, unit = {"a": 0, "d": 0}, 0
    for e in "adadadad":
        counts[e] += 1
        unit += 1
        FREE.append((e, counts[e]))
        CHUNK_UNIT.append(unit)
    for name, tiles, width, who in _LIN:
        ln = Linear()
        ln.name, ln.tiles, ln.width = name, tiles, width
        ln.tile0, ln.chunk0, ln.unit0 = len(TILE_UNIT), len(FREE), unit
        for t in range(tiles):
            TILE_WIDTH.append(width)
            TILE_POOL.append(name in POOL_SPLITS and t >= 2)
            if len(who) == 1:
                unit += 1
                if t % 2:
                    counts[who] += 1
                    FREE.append((who, counts[who]))
                    CHUNK_UNIT.append(unit)
            else:
                for e in who:
                    unit += 1
                    counts[e] += 1
                    FREE.append((e, counts[e]))
                    CHUNK_UNIT.append(unit)
            TILE_UNIT.append(unit)
        ln.unit_end, ln.freed_a, ln.freed_d = unit, counts["a"], counts["d"]
        LIN[name] = ln


_plan()
N_TILES = len(TILE_UNIT)
ROWS_UNITS = A_HEADS

_SETS = ["n0", "n1", "attA", "n2", "n3", "n4", "n5", "attB", "n6", "n8", "cf", "n9", "attX", "n11"]
SET = {name: 8 * k for k, name in enumerate(_SETS)}
ESET = {name: 8 * k for k, name in enumerate(["c3", "merged", "n10"])}
RANK = {n: k for k, n in enumerate([0, 1, 2, 3, 5, 6, N_FINAL, N_MIX, N_MEM, N_XA, N_PEER])}

STEPS = [("A", c) for c in range(DC)] + [("B", c) for c in range(DC)] + [("X", c) for c in range(2)]
STEP0 = {"A": 0, "B": 8, "X": 16}
STEP_END = {"A": 8, "B": 16, "X": 18}

GROUP = 16
HALF = PH // 2
N_GROUPS = SLOTS_PER_TILE // GROUP


def at(i, step, base):
    return base if i is None else i * step + base


class Chain:

    def __init__(self, eng, sem):
        self.eng, self.sem, self.n, self.i, self.step = eng, sem, 0, None, 0

    def __call__(self, ins, lag=0):
        ins.then_inc(self.sem, 1)
        self.n += 1
        if self.n > lag:
            self.eng.wait_ge(self.sem, at(self.i, self.step, self.n - lag))

    def enter(self, i, step):
        self.i, self.step, self.start = i, step, self.n

    def leave(self, rounds):
        assert self.n - self.start == self.step, (self.n - self.start, self.step)
        self.n = self.start + rounds * self.step
        self.i = None


def build_program(nc, a, out):
    ctx = ExitStack()
    with ctx:
        def sb(name, shape, dt=F32):
            return ctx.enter_context(nc.sbuf_tensor(name, shape, dt))

        def sem(name):
            return ctx.enter_context(nc.semaphore(name))

        arena_at = (nc.sbuf_base + 31) // 32 * 32
        KF = 1024
        RAW_AT, WH_AT, WL_AT = 0, 6 * KF, 12 * KF
        MOD_AT, HH_AT, HL_AT, SQ_AT, KS_AT, VS_AT, X_AT = (18 * KF, 22 * KF, 24 * KF, 26 * KF, 28 * KF, 30 * KF, 32 * KF)
        WORK_AT = 34 * KF
        ARENA = 48 * KF
        sb("arena", [P, ARENA])

        def place(name, at_, n, dt=F32, parts=P):
            assert at_ + n <= ARENA
            return nc.alloc_sbuf_tensor_at(name, [parts, n], dt, offset=arena_at + 4 * at_)

        def three(t, k):
            return t[:, :].rearrange("p (a b) -> p a b", a=k)

        raw = place("raw", RAW_AT, RING * TILE)
        w_hi = place("w_hi", WH_AT, RING * TILE, F32R)
        w_lo = place("w_lo", WL_AT, RING * TILE, F32R)
        rows_ring = place("rows_ring", RAW_AT, GROUP * D)
        YO = three(place("YO", RAW_AT + GROUP * D, TT * D), TT)
        mod_ring = place("mod_ring", MOD_AT, 2 * TILE)
        HH = three(place("HH", HH_AT, DC * SEQ, F32R), DC)
        HL = three(place("HL", HL_AT, DC * SEQ, F32R), DC)
        YACC = three(place("YACC", HH_AT, 2 * D), 2)
        junk = three(place("junk", HL_AT, 2 * D), 2)
        SQ = three(place("SQ", SQ_AT, DC * SEQ), DC)
        XTOK = three(place("XTOK", SQ_AT, TT * D), TT)
        KS = three(place("KS", KS_AT, DC * SEQ), DC)
        bias = KS
        EH = three(place("EH", KS_AT, DC * SEQ, F32R), DC)
        CA2 = three(place("CA2", KS_AT, PH * TK * TK), PH)
        VS = three(place("VS", VS_AT, TT * D), TT)
        EL = three(place("EL", VS_AT, DC * SEQ, F32R), DC)
        HTOK = three(place("HTOK", VS_AT, TT * D), TT)
        X = three(place("X", X_AT, DC * SEQ), DC)
        work = place("work", WORK_AT, 14 * KF)
        GUH = three(place("GUH", WORK_AT, FC * SEQ, F32R), FC)
        GUL = three(place("GUL", WORK_AT + FC * SEQ, FC * SEQ, F32R), FC)

        mod_acc = sb("mod_acc", [P, 2, 2 * P])
        prm = sb("prm", [P, NCOL])
        mods = sb("mods", [P, 2 * ADA_TILES])
        c_act = sb("c_act", [P, DC])
        gain = sb("gain", [P, DC])
        half_gate = sb("half_gate", [P, DC])
        root = sb("root", [P, SEQ])
        rinv = sb("rinv", [P, SEQ])
        ident = sb("ident", [P, P])
        ones = sb("ones", [P, P])
        mask = sb("mask", [P, SEQ])
        iota16 = sb("iota16", [P, TK])
        table = sb("table", [NB + 1, A_HEADS])
        table_rep = work[0:NB + 1, 4096:5120].rearrange("p (h n) -> p h n", h=A_HEADS)
        onehot = work[0:NB + 1, 5120:5632]
        lamp = work[:, 5632:5632 + 4 * HD]
        lam_prod = work[:, 5888:5888 + 2 * HD].rearrange("p (a n) -> p a n", a=2)
        lam_sum = sb("lam_sum", [P, 2])
        lam_exp = sb("lam_exp", [P, 2])
        lam_vec = sb("lam_vec", [P, 4])
        sub_gain = sb("sub_gain", [P, 1])
        fgate_b = sb("fgate_b", [B_HEADS, 1])
        f_z = work[0:B_HEADS, 0:SEQ]
        f_t = work[0:B_HEADS, SEQ:2 * SEQ]
        f_sum = sb("f_sum", [B_HEADS, SEQ])
        f_neg = sb("f_neg", [B_HEADS, SEQ])
        subk = sb("subk", [P, 2, NK])
        nmax = sb("nmax", [P, 2, 4])
        rowsum = sb("rowsum", [P, 2, 4])
        rscale = sb("rscale", [P, 2, 4])
        stage = sb("stage", [P, 2, GROUP], U32)
        dot16 = sb("dot16", [P, GROUP])
        coef16 = sb("coef16", [P, GROUP])
        eps = sb("eps", [P, 1])

        def wk(lo, n, *shape):
            v = work[:, lo:lo + n]
            if len(shape) == 2:
                return v.rearrange("p (a b) -> p a b", a=shape[0])
            if len(shape) == 3:
                return v.rearrange("p (a b c) -> p a b c", a=shape[0], b=shape[1])
            return v

        silu = wk(2 * FC * SEQ, 512, 2, SEQ)
        graw = wk(2 * FC * SEQ + 512, 512, 2, SEQ)
        stg = wk(0, 4096, A_HEADS, 512)
        T = wk(12288, 2048, DC, SEQ)
        QT = wk(0, 2048, DC, SEQ)
        KT = wk(2048, 2048, DC, SEQ)
        V = wk(4096, 2048, TT, D)
        OT = wk(6144, 2048, DC, SEQ)
        LG = wk(8192, 1024, 2, 2, SEQ)
        EX = (wk(9216, 1024, 2, 2, SEQ), wk(12288, 1024, 2, 2, SEQ))
        PR = wk(10240, 1024, 2, 2, SEQ)
        PT = wk(11264, 1024, 2, 512)
        DQ = wk(2048, 2048, DC, SEQ)
        DK = wk(4096, 2048, DC, SEQ)
        UP = SEQ + SCK - 1
        VP = SEQ + CFK - 1
        U = wk(0, DC * UP, DC, UP)
        CV = wk(2064, DC * VP, DC, VP)
        C3 = wk(4352, 2048, DC, SEQ)
        MEM = C3
        Z = wk(6400, 2048, DC, SEQ)
        SG = wk(8448, 2048, DC, SEQ)
        CG = wk(10496, 2048, DC, SEQ)
        T0 = wk(12544, 512, 2, SEQ)
        T1 = wk(13056, 512, 2, SEQ)
        ZB = wk(13568, 256)
        S = (wk(0, 2048, 2 * PH, NK), wk(2048, 2048, 2 * PH, NK))
        S2 = wk(4096, 2048, 2 * PH, NK)
        CA = wk(6144, 2048, PH, TK * TK)
        NS = HALF * TK
        QP = wk(8192, 4096, 2 * PH, SEQ)
        at_mr = [0]

        def mr(n, a0=None, dt=None):
            v = mod_ring[:, at_mr[0]:at_mr[0] + n]
            at_mr[0] += n
            if dt is not None:
                v = v.bitcast(dt)
            return v if a0 is None else v.rearrange("p (a b) -> p a b", a=a0)

        gfin = mr(D)
        TV = mr(256, 2 * PH)
        TI = mr(256, 2 * PH, U32)
        TIF = mr(256, 2 * PH)
        FV = mr(128, PH)
        FP = mr(128, PH, U32)
        AI = mr(128, None, U32)
        BI = mr(128, None, U32)
        AF = mr(128)
        BF = mr(128)
        I0 = mr(128)
        I1 = mr(128)
        IDX = mr(256, 2, U32)
        GT = mr(256, 2)
        DOT = mr(256, 2)
        CF = mr(256, 2)
        GS = mr(16)
        YS = mr(4)
        assert at_mr[0] <= 2 * TILE

        ps = ctx.enter_context(nc.psum_tensor("ps", [P, 8, 512], F32))
        ps_norm = ps[:, 4, 0:SEQ]
        ps_mod = ps[:, 7, 0:8]
        ps_s = (ps[:, 5:7, :], ps[:, 2:5:2, :])
        PT_BANK = (7, 3)
        ps_f = ps[0:B_HEADS, 5, 0:SEQ]
        SUB_BANK = (1, 3, 0, 2)

        bias_rows = nc.dram_tensor("bias_rows", (A_HEADS, P * 512), F32).ap()

        def col(name, k=0, n=1):
            return prm[:, COL[name] + k:COL[name] + k + n]

        def slot(ring_, g, width=None):
            lo = (g % RING) * TILE
            return ring_[:, lo:lo + (TILE_WIDTH[g] if width is None else width)]

        def f32(ap):
            return ap.bitcast(F32)

        prm_loaded = sem("prm_loaded")
        x_loaded = sem("x_loaded")
        small_loaded = sem("small_loaded")
        sub_loaded = sem("sub_loaded")
        w_loaded = [sem(f"w_loaded{s}") for s in range(RING)]
        hi_ready = sem("hi_ready")
        lo_ready = sem("lo_ready")
        mod_loaded = [sem(f"mod_loaded{s}") for s in range(2)]
        rows_written = sem("rows_written")
        bias_loaded = sem("bias_loaded")
        decay_loaded = sem("decay_loaded")
        mem_loaded = sem("mem_loaded")
        gfin_loaded = sem("gfin_loaded")
        out_written = sem("out_written")
        consts_ready = sem("consts_ready")
        pool_step = sem("pool_step")
        vec_consts = sem("vec_consts")
        dve_step = sem("dve_step")
        act_step = sem("act_step")
        c_ready = sem("c_ready")
        acc_ready = sem("acc_ready")
        modsum_ready = sem("modsum_ready")
        mods_ready = sem("mods_ready")
        lam_sum_ready = sem("lam_sum_ready")
        lam_exp_ready = sem("lam_exp_ready")
        table_ready = sem("table_ready")
        rows_ready = sem("rows_ready")
        rows_copied = sem("rows_copied")
        squares_ready = sem("squares_ready")
        sumsq_ready = sem("sumsq_ready")
        root_ready = sem("root_ready")
        t_ready = sem("t_ready")
        hh_ready = sem("hh_ready")
        hl_ready = sem("hl_ready")
        hidden_hi = sem("hidden_hi")
        hidden_lo = sem("hidden_lo")
        eh_ready = sem("eh_ready")
        el_ready = sem("el_ready")
        units_done = sem("units_done")
        freed = {"a": sem("freed_by_scalar"), "d": sem("freed_by_vector")}
        scores_done = sem("scores_done")
        logits_ready = sem("logits_ready")
        exp_ready = sem("exp_ready")
        probs_ready = sem("probs_ready")
        turned = sem("turned")
        probsT_ready = sem("probsT_ready")
        pv_done = sem("pv_done")
        attn_ready = sem("attn_ready")
        sub_scaled = sem("sub_scaled")
        sub_sq = sem("sub_sq")
        sub_sum = sem("sub_sum")
        sub_root = sem("sub_root")
        sub_done = sem("sub_done")
        fz_done = sem("fz_done")
        fz_ln = sem("fz_ln")
        f_ready = sem("f_ready")
        decay_cleared = sem("decay_cleared")
        pads_ready = sem("pads_ready")
        conv_done = sem("conv_done")
        mean_sum = sem("mean_sum")
        mean_ready = sem("mean_ready")
        centred = sem("centred")
        ln_sq = sem("ln_sq")
        ln_sum = sem("ln_sum")
        ln_root = sem("ln_root")
        ln_scaled = sem("ln_scaled")
        ln_ready = sem("ln_ready")
        tok_turned = sem("tok_turned")
        tok_ready = sem("tok_ready")
        sub_scores = sem("sub_scores")
        s_ready = sem("s_ready")
        gate_diff = sem("gate_diff")
        gate_exp = sem("gate_exp")
        idx_ready = sem("idx_ready")
        dots_ready = sem("dots_ready")
        gelu_ready = sem("gelu_ready")
        staged = sem("staged")
        row_loaded = [sem(f"row_loaded{s}") for s in range(GROUP)]
        rows_free = sem("rows_free")
        rows_asked = sem("rows_asked")
        y_ready = sem("y_ready")
        yroot_ready = sem("yroot_ready")
        yo_ready = sem("yo_ready")

        block = ctx.enter_context(nc.Block())

        @block.sync
        def _(sp):
            sp.dma_start(prm[:, :], a["prm"]).then_inc(prm_loaded, 16)
            sp.dma_start(X[:, :, :], a["xT"]).then_inc(x_loaded, 16)

            def tiles(name, t0=0, n=None, i=None):
                ln = LIN[name]
                for t in range(t0, t0 + (ln.tiles if n is None else n)):
                    g = ln.tile0 + t
                    if g >= RING:
                        sp.wait_ge(lo_ready, at(i, BODY, g - RING + 1))
                    src = a[name][t] if i is None else a[name][bass.ds(i * BODY + t, 1)].rearrange("a p f -> (a p) f")
                    sp.dma_start(slot(raw, g), src).then_inc(w_loaded[g % RING], 16)

            def ffn(w_in, w_out):
                tiles(w_in, 0, RING)
                with sp.Fori(0, 3) as i:
                    tiles(w_in, RING, BODY, i)
                tiles(w_in, 21, 1)
                tiles(w_out)

            ffn("f00_in", "f00_out")
            for name in ("a_q", "a_k", "a_v", "a_o"):
                tiles(name)
            ffn("f01_in", "f01_out")
            tiles("s_k")
            tiles("s_v")
            ffn("f10_in", "f10_out")
            tiles("b_q")
            sp.wait_ge(f_ready, 1)
            sp.wait_ge(decay_cleared, 4)
            for odd in range(2):
                sp.dma_start(DQ[64 * odd:64 * odd + 1, :, :], f_sum[odd:B_HEADS:2, :]).then_inc(decay_loaded, 16)
                sp.dma_start(DK[64 * odd + 1:64 * odd + 2, :, :], f_neg[odd:B_HEADS:2, :]).then_inc(decay_loaded, 16)
            tiles("b_o")
            ffn("f11_in", "f11_out")
            for name in ("mix_a", "mix_b", "mix_g", "sc_out"):
                tiles(name)
            sp.wait_ge(el_ready, ESET["c3"] + DC)
            sp.dma_start(MEM, a["memT"]).then_inc(mem_loaded, 16)
            for name in ("cf_out", "mix_out"):
                tiles(name)
            for name in ("x_k", "x_v", "x_q", "x_o", "pq"):
                tiles(name)
            sp.dma_start(gfin, a["final_norm_g"].partition_broadcast(P).rearrange("q a n -> q (a n)")).then_inc(gfin_loaded, 16)
            for t in range(TT):
                sp.wait_ge(yo_ready, t + 1)
                sp.dma_start(out[t], YO[:, t, :]).then_inc(out_written, 16)
            sp.wait_ge(out_written, 16 * TT)

        @block.gpsimd
        def _(pool):
            step = Chain(pool, pool_step)
            pool.dma_start(table[0:NB, :], a["rel_bias"]).then_inc(small_loaded, 16)
            pool.dma_start(onehot[:, :], a["onehot"]).then_inc(small_loaded, 16)
            pool.dma_start(lamp[:, :], a["a_lambda"].partition_broadcast(P).rearrange("q a n -> q (a n)")).then_inc(small_loaded, 16)
            pool.dma_start(fgate_b[:, :], a["fgate_b"]).then_inc(small_loaded, 16)
            pool.dma_start(subk[:, :, :], a["subkT"]).then_inc(small_loaded, 16)
            step(nc.gpsimd.memset(ident[:, :], 0.0))
            nc.gpsimd.affine_select(out=ident[:, :], in_=ident[:, :], compare_op=ALU.not_equal, fill=1.0, base=0,
                                    pattern=[[-1, P]], channel_multiplier=1).then_inc(consts_ready, 1)
            step(nc.gpsimd.memset(mask[:, :], 0.0))
            nc.gpsimd.affine_select(out=mask[:, :], in_=mask[:, :], compare_op=ALU.is_ge, fill=NEG, base=P,
                                    pattern=[[-1, SEQ]], channel_multiplier=1).then_inc(consts_ready, 1)
            nc.gpsimd.iota(iota16[:, :], pattern=[[1, TK]], base=0, channel_multiplier=0,
                           allow_small_or_imprecise_dtypes=True).then_inc(consts_ready, 1)

            def splits(name):
                ln = LIN[name]
                for g in range(ln.tile0, ln.tile0 + ln.tiles):
                    if TILE_POOL[g]:
                        pool.wait_ge(lo_ready, g)
                        pool.wait_ge(hi_ready, g + 1)
                        nc.gpsimd.tensor_tensor(slot(w_lo, g), slot(raw, g), f32(slot(w_hi, g)), ALU.subtract
                                                ).then_inc(lo_ready, 1)

            def lows(name, src):
                for k in range(DC):
                    pool.wait_ge(hh_ready, SET[name] + k + 1)
                    nc.gpsimd.tensor_tensor(HL[:, k, :], src[:, k, :], f32(HH[:, k, :]), ALU.subtract
                                            ).then_inc(hl_ready, 1)

            def second_lows(name, src):
                for k in range(DC):
                    pool.wait_ge(eh_ready, ESET[name] + k + 1)
                    nc.gpsimd.tensor_tensor(EL[:, k, :], src[:, k, :], f32(EH[:, k, :]), ALU.subtract
                                            ).then_inc(el_ready, 1)

            def hidden(n):
                def one(j, i=None):
                    pool.wait_ge(hidden_hi, at(i, BODY, FC * n + j + 1))
                    if i is None:
                        lo, hi = GUL[:, j, :], GUH[:, j, :]
                    else:
                        lo, hi = (g_[:, bass.ds(i * BODY + j, 1), :].rearrange("p a n -> p (a n)") for g_ in (GUL, GUH))
                    nc.gpsimd.tensor_tensor(lo, graw[:, j % 2, :], f32(hi), ALU.subtract).then_inc(hidden_lo, 1)

                with pool.Fori(0, 3) as i:
                    for j in range(BODY):
                        one(j, i)
                for j in range(3 * BODY, FC):
                    one(j)

            pool.sem_inc(hidden_lo, 2)
            hidden(0)
            lows("attA", OT)
            hidden(1)
            hidden(2)
            lows("attB", OT)
            hidden(3)
            lows("n8", T)
            splits("mix_a")
            second_lows("c3", C3)
            lows("cf", Z)
            second_lows("merged", SG)
            lows("n9", T)
            second_lows("n10", T)
            lows("attX", OT)
            lows("n11", T)
            splits("pq")
            pool.wait_ge(units_done, LIN["pq"].unit_end)

            def gather(t, part, first, pairs):
                rows = (a["peer_u"], a["peer_v"])[part]
                seg = 2 * t + part
                with pool.Fori(0, pairs) as i:
                    for g in range(2):
                        group = seg * N_GROUPS + first + g
                        lo = i * (2 * GROUP) + (first + g) * GROUP
                        nc.gpsimd.tensor_copy(stage[:, g, :], IDX[:, t, bass.ds(lo, GROUP)]).then_inc(staged, 1)
                        pool.wait_ge(staged, i * 2 + (group + 1))
                        for j in range(GROUP):
                            if j % 4 == 0:
                                pool.wait_ge(rows_free, i * (2 * GROUP) + (group * GROUP + j + 4))
                                pool.sem_inc(rows_asked, 1)
                            pool.indirect_dma_start(
                                out=rows_ring[:, j * D:(j + 1) * D], out_offset=None, in_=rows,
                                in_offset=bass.IndirectOffsetOnAxis(ap=stage[:, g, j:j + 1], axis=0),
                            ).then_inc(row_loaded[j], 16)

            for t in range(TT):
                for half in range(2):
                    pool.wait_ge(idx_ready, 2 * t + half + 1)
                    gather(t, 0, half * N_GROUPS // 2, N_GROUPS // 4)
                gather(t, 1, 0, N_GROUPS // 2)

        @block.tensor
        def _(pe):
            mm, turn = nc.tensor.matmul, nc.tensor.transpose

            def freed_wait(q, i):
                if i is None:
                    e, n = FREE[q - BANKS]
                    pe.wait_ge(freed[e], n)
                    return
                e, n = FREE[q - BANKS + 2 * BODY]
                pe.wait_ge(freed[e], i * BODY + (n - BODY))

            def product(out_, whole, split, k0, k1, first, last, left=False):
                for k in range(k0, k1):
                    for n, (u, v_) in enumerate(((0, 0), (0, 1), (1, 0))):
                        ops = (whole(u, k), split(v_, k))
                        ins = mm(out_, ops[1] if left else ops[0], ops[0] if left else ops[1],
                                 start=(first and k == k0 and n == 0), stop=(last and k == k1 - 1 and n == 2))
                return ins

            def tile_wait(g, i=None):
                pe.wait_ge(lo_ready, at(i, BODY, g + 1))

            def wparts(g):
                k = DC if TILE_WIDTH[g] == TILE else WO_K
                return [slot(r, g).rearrange("p (k n) -> p k n", k=k) for r in (w_hi, w_lo)]

            def feat_tile(name, t, i=None, mid=None, new=None):
                ln = LIN[name]
                g = ln.tile0 + t
                tile_wait(g, i)
                w = wparts(g)
                second = name in ("sc_out", "mix_out", "x_q")
                src = (EH, EL) if second else (HH, HL)
                for m in range(2):
                    q = ln.chunk0 + 2 * t + m
                    freed_wait(q, i)
                    if m == 1 and mid is not None:
                        mid()
                    o = ps[:, q % BANKS, 0:SEQ]
                    wk_ = lambda u, k: w[u][:, k, m * P:(m + 1) * P]
                    xk_ = lambda u, k: src[u][:, k, :]
                    if new is not None and t == 0 and m == 0:
                        for k in range(DC):
                            if second:
                                pe.wait_ge(el_ready, ESET[new] + k + 1)
                            else:
                                pe.wait_ge(hl_ready, SET[new] + k + 1)
                            last = product(o, wk_, xk_, k, k + 1, k == 0, k == DC - 1)
                    else:
                        last = product(o, wk_, xk_, 0, DC, True, True)
                    last.then_inc(units_done, 1)

            def tok_tile(name, t, mid=None):
                ln = LIN[name]
                g = ln.tile0 + t
                tile_wait(g)
                w = wparts(g)
                for m in range(TT):
                    q = ln.chunk0 + TT * t + m
                    freed_wait(q, None)
                    if m == 1 and mid is not None:
                        mid()
                    product(ps[:, q % BANKS, 0:2 * P], lambda u, k: w[u][:, k, :],
                            lambda u, k: (HH, HL)[u][:, k, m * P:(m + 1) * P], 0, DC, True, True, left=True
                            ).then_inc(units_done, 1)

            def mod_sum(n, i=None):
                pe.wait_ge(acc_ready, at(i, 4, n + 1))
                if n >= 1:
                    pe.wait_ge(mods_ready, at(i, 4, n))
                for m in range(2):
                    last = mm(ps_mod[:, m:m + 1], mod_acc[:, n % 2, m * P:(m + 1) * P], ones[:, 0:1],
                              start=True, stop=True)
                last.then_inc(modsum_ready, 1)

            def norm_sum(n, ks=range(DC)):
                for k in ks:
                    pe.wait_ge(squares_ready, 8 * RANK[n] + k + 1)
                    last = mm(ps_norm, ones[:, :], SQ[:, k, :], start=(k == 0), stop=(k == DC - 1))
                    if k == DC - 1:
                        last.then_inc(sumsq_ready, 1)

            def ffn(f, w_in, w_out, new, nxt, ada):
                ln = LIN[w_in]
                more = ada is not None
                pe.wait_ge(freed["a"], FREE[ln.chunk0][1] - 1)
                pe.wait_ge(freed["d"], FREE[ln.chunk0 + 1][1] - 1)
                for k in range(DC):
                    pe.wait_ge(hl_ready, SET[new] + k + 1)
                with pe.Fori(0, 3) as i:
                    for t in range(BODY):
                        n = {1: 0, 2: 1, 4: 2, 5: 3}.get(t)
                        feat_tile(w_in, t, i=i, mid=(lambda: mod_sum(ada + n, i)) if more and n is not None else None)
                for t in range(18, 22):
                    n = {19: 12, 20: 13}.get(t)
                    feat_tile(w_in, t, mid=(lambda: mod_sum(ada + n)) if more and n is not None else None)
                lo = LIN[w_out]
                for t in range(16):
                    g = lo.tile0 + t
                    tile_wait(g)
                    m, half = t // 2, t % 2
                    q = lo.chunk0 + m
                    if half == 0:
                        freed_wait(q, None)
                    if m == 0:
                        pe.wait_ge(hidden_lo, 2 + FC * f + WO_K * (half + 1))
                    w = wparts(g)
                    product(ps[:, q % BANKS, 0:SEQ], lambda u, k: w[u][:, k - WO_K * half, :],
                            lambda u, k: (GUH, GUL)[u][:, k, :], WO_K * half, WO_K * (half + 1), half == 0, half == 1
                            ).then_inc(units_done, 1)
                    if more and half == 0 and 1 <= m <= 6:
                        mod_sum(ada + 14 + m - 1)
                    if half == 1 and m >= 2:
                        norm_sum(nxt, [m - 2])
                norm_sum(nxt, [DC - 2, DC - 1])

            def residual(name, new, nxt):
                for t in range(4):
                    feat_tile(name, t, new=new)
                    if nxt is not None and t:
                        norm_sum(nxt, [2 * t - 2, 2 * t - 1])
                if nxt is not None:
                    norm_sum(nxt, [DC - 2, DC - 1])

            def attention(kind):
                s0, s1 = STEP0[kind], STEP_END[kind]
                kt = KS if kind == "B" else KT
                v = VS if kind == "B" else V
                hw = {"A": 128, "B": 64, "X": 256}[kind]

                def scores(s):
                    c = s - s0
                    for qt in range(TT):
                        u = 2 * s + qt
                        if s and kind == "X" and s > s0:
                            pe.wait_ge(exp_ready, u - 1)
                        elif s:
                            pe.wait_ge(logits_ready, u - 1)
                        nk = SEQ if kind == "X" or qt == 1 else P
                        for m in range(2):
                            o = ps_s[qt][:, m, 0:nk]
                            if kind == "X":
                                for e in range(2):
                                    cc = 4 * c + 2 * m + e
                                    last = mm(o, QT[:, cc, qt * P:(qt + 1) * P], kt[:, cc, 0:nk],
                                              start=(e == 0), stop=(e == 1))
                            else:
                                r = slice(64 * m, 64 * m + 64)
                                last = mm(o, QT[r, c, qt * P:(qt + 1) * P], kt[r, c, 0:nk],
                                          start=True, stop=(kind == "A"))
                                if kind == "B":
                                    r = slice(64 * m, 64 * m + 2)
                                    last = mm(o, DQ[r, c, qt * P:(qt + 1) * P], DK[r, c, 0:nk], start=False, stop=True)
                        last.then_inc(scores_done, 1)

                def turn_probs(s):
                    pe.wait_ge(probs_ready, 2 * s + 2)
                    if s:
                        pe.wait_ge(probsT_ready, s)
                    for m in range(1 if kind == "A" else 2):
                        bank = PT_BANK[m]
                        blocks = [(0, 0), (0, 1), (1, 1)] if kind != "X" else [(0, 0), (0, 1), (1, 0), (1, 1)]
                        for b, (k, qt) in enumerate(blocks):
                            last = turn(ps[:, bank, b * P:(b + 1) * P], PR[:, qt, m, k * P:(k + 1) * P], ident[:, :])
                    last.then_inc(turned, 1)

                def values(s):
                    c = s - s0
                    pe.wait_ge(probsT_ready, s + 1)
                    if s:
                        pe.wait_ge(attn_ready, s)
                    if kind == "X":
                        for m in range(2):
                            for e in range(2):
                                f = (2 * c + m) * hw + e * P
                                for k in range(2):
                                    last = mm(ps[:, m, e * SEQ:(e + 1) * SEQ], v[:, k, f:f + P],
                                              PT[:, m, k * SEQ:(k + 1) * SEQ], start=(k == 0), stop=(k == 1))
                    else:
                        for m in range(1 if kind == "A" else 2):
                            f = c * P + m * hw
                            rows = slice(m * hw, m * hw + hw)
                            mm(ps[rows, 0, 0:SEQ], v[:, 0, f:f + hw], PT[:, m, 0:SEQ], start=True, stop=False)
                            last = mm(ps[rows, 0, P:SEQ], v[:, 1, f:f + hw], PT[:, m, SEQ:SEQ + P],
                                      start=False, stop=True)
                    last.then_inc(pv_done, 1)

                scores(s0)
                scores(s0 + 1)
                for s in range(s0, s1):
                    turn_probs(s)
                    if s + 2 < s1:
                        scores(s + 2)
                    values(s)

            pe.wait_ge(vec_consts, 1)
            pe.wait_ge(consts_ready, 3)
            pe.wait_ge(table_ready, 1)
            for h in range(A_HEADS):
                if h >= BANKS:
                    freed_wait(h, None)
                mm(ps[:, h % BANKS, :], table_rep[:, h, :], onehot, start=True, stop=True).then_inc(units_done, 1)
            norm_sum(0)
            for n in range(8):
                mod_sum(n)
            ffn(0, "f00_in", "f00_out", "n0", 1, 8)

            for t in range(4):
                feat_tile("a_q", t, new="n1", mid=(lambda: mod_sum(28 + t - 1)) if t else None)
            for t in range(4):
                feat_tile("a_k", t, mid=lambda: mod_sum(31 + t))
            for t in range(4):
                tok_tile("a_v", t, mid=(lambda: mod_sum(35)) if t == 0 else None)
            pe.wait_ge(freed["a"], LIN["a_v"].freed_a)
            pe.wait_ge(freed["d"], LIN["a_v"].freed_d)
            attention("A")
            pe.wait_ge(attn_ready, STEP_END["A"])
            for b in range(4):
                pe.wait_ge(sub_sq, b + 1)
                mm(ps[:, SUB_BANK[b], :], ones[:, :], SQ[:, 2 * b:2 * b + 2, :], start=True, stop=True
                   ).then_inc(sub_sum, 1)
            pe.wait_ge(sub_root, 4)
            residual("a_o", "attA", 2)

            ffn(1, "f01_in", "f01_out", "n2", 3, 36)
            for t in range(4):
                feat_tile("s_k", t, new="n3")
            for t in range(4):
                tok_tile("s_v", t)
            fw = col("fgate_w", 0, DC * B_HEADS).rearrange("p (k n) -> p k n", k=DC)
            for k in range(DC):
                for n, part in enumerate((HH, HL)):
                    last = mm(ps_f, fw[:, k, :], f32(part[:, k, :]), start=(k == 0 and n == 0),
                              stop=(k == DC - 1 and n == 1))
            last.then_inc(fz_done, 1)

            ffn(2, "f10_in", "f10_out", "n4", 5, 56)
            for t in range(4):
                feat_tile("b_q", t, new="n5", mid=(lambda: mod_sum(76 + t - 1)) if t else None)
            mod_sum(79)
            pe.wait_ge(freed["a"], LIN["b_q"].freed_a)
            pe.wait_ge(mods_ready, 80)
            pe.wait_ge(decay_loaded, 64)
            attention("B")
            pe.wait_ge(attn_ready, STEP_END["B"])
            residual("b_o", "attB", 6)
            ffn(3, "f11_in", "f11_out", "n6", N_FINAL, None)

            norm_sum(N_MIX)
            for t in range(16):
                feat_tile("mix_a", t, new="n8")
            for t in range(4):
                feat_tile("mix_b", t)
            for k in range(DC):
                pe.wait_ge(conv_done, k + 1)
                last = mm(ps_norm, ones[:, :], Z[:, k, :], start=(k == 0), stop=(k == DC - 1))
            last.then_inc(mean_sum, 1)
            for t in range(8):
                feat_tile("mix_g", t)
                if t == 1:
                    for k in range(DC):
                        pe.wait_ge(ln_sq, k + 1)
                        last = mm(ps_norm, ones[:, :], SQ[:, k, :], start=(k == 0), stop=(k == DC - 1))
                    last.then_inc(ln_sum, 1)
            for t in range(4):
                feat_tile("sc_out", t, new="c3")
            for t in range(4):
                feat_tile("cf_out", t, new="cf")
            norm_sum(N_MEM)
            residual("mix_out", "merged", N_XA)

            for t in range(4):
                feat_tile("x_k", t, new="n9")
            for t in range(4):
                tok_tile("x_v", t)
            for t in range(4):
                feat_tile("x_q", t, new="n10")
            pe.wait_ge(freed["a"], LIN["x_q"].freed_a)
            pe.wait_ge(freed["d"], LIN["x_v"].freed_d)
            attention("X")
            pe.wait_ge(attn_ready, STEP_END["X"])
            residual("x_o", "attX", N_PEER)

            def head_scores(h):
                pe.wait_ge(freed["a"], FREE[LIN["pq"].chunk0 + 2 * h][1])
                pe.wait_ge(freed["d"], FREE[LIN["pq"].chunk0 + 2 * h + 1][1])
                for t in range(TT):
                    if h >= 2:
                        pe.wait_ge(s_ready, 2 * (h - 2) + t + 1)
                    for p_ in range(2):
                        last = mm(ps[:, 3 + 2 * (h % 2) + t, p_ * NK:(p_ + 1) * NK], QP[:, 2 * h + p_, t * P:(t + 1) * P],
                                  subk[:, p_, :], start=True, stop=True)
                    last.then_inc(sub_scores, 1)

            for t in range(8):
                feat_tile("pq", t, new="n11", mid=(lambda: head_scores(t - 1)) if t else None)
            head_scores(7)
            for b in range(8):
                src, t, half = (T, X)[b // 4], (b // 2) % 2, b % 2
                if b >= 2:
                    pe.wait_ge(tok_ready, b - 1)
                for c in range(4):
                    last = turn(ps[:, b % 2, c * P:(c + 1) * P], src[:, 4 * half + c, t * P:(t + 1) * P], ident[:, :])
                last.then_inc(tok_turned, 1)

        @block.scalar
        def _(act):
            step = Chain(act, act_step)
            f = nc.scalar.activation

            def split(g, i=None):
                if g >= N_TILES:
                    return
                act.wait_ge(w_loaded[g % RING], at(i, 16 * BODY // RING, 16 * (g // RING + 1)))
                if g >= RING:
                    act.wait_ge(units_done, at(i, 2 * BODY, TILE_UNIT[g - RING]))
                f(slot(w_hi, g), slot(raw, g), ACT.Copy).then_inc(hi_ready, 1)

            def load_mod(n, i=None):
                act.wait_ge(acc_ready, at(i, 4, n - 1))
                src = a["ada"][n] if i is None else a["ada"][bass.ds(i * 4 + n, 1)].rearrange("a p f -> (a p) f")
                act.dma_start(mod_ring[:, (n % 2) * TILE:(n % 2 + 1) * TILE], src).then_inc(mod_loaded[n % 2], 16)

            def square(n, k, ready=None):
                if ready is not None:
                    act.wait_ge(freed["d"], ready)
                f(SQ[:, k, :], X[:, k, :], ACT.Square).then_inc(squares_ready, 1)

            def residual(name, nxt):
                ln = LIN[name]
                for t in range(4):
                    split(ln.tile0 + t + 2)
                    if nxt is not None and t:
                        for k in (2 * t - 2, 2 * t - 1):
                            square(nxt, k, FREE[ln.chunk0 + k][1])
                if nxt is not None:
                    for k in (6, 7):
                        square(nxt, k, FREE[ln.chunk0 + k][1])

            def norm_root(n):
                act.wait_ge(sumsq_ready, RANK[n] + 1)
                f(root[:, :], ps_norm, ACT.Sqrt, scale=1.0 / D, bias=eps[:, :]).then_inc(root_ready, 1)

            def shift_high(name, n):
                m0 = NORMS[n][1]
                for k in range(DC):
                    act.wait_ge(t_ready, 8 * n + k + 1)
                    f(HH[:, k, :], T[:, k, :], ACT.Identity, bias=mods[:, m0 + k:m0 + k + 1]).then_inc(hh_ready, 1)

            def norm_high(n, second=False):
                for k in range(DC):
                    act.wait_ge(t_ready, 8 * n + k + 1)
                    if second:
                        f(EH[:, k, :], T[:, k, :], ACT.Copy).then_inc(eh_ready, 1)
                    else:
                        f(HH[:, k, :], T[:, k, :], ACT.Copy).then_inc(hh_ready, 1)

            def take(name, q, dst, func=ACT.Copy, **kw):
                q = LIN[name].chunk0 + q
                act.wait_ge(units_done, CHUNK_UNIT[q])
                assert FREE[q][0] == "a"
                f(dst, ps[:, q % BANKS, 0:SEQ], func, **kw).then_inc(freed["a"], 1)

            def ffn(n, w_in, w_out, nxt, ada):
                ln = LIN[w_in]
                more = ada is not None

                def slot_(t, i=None):
                    split(ln.tile0 + t + 2, i)
                    if more and t in (1, 2, 4, 5, 19, 20):
                        k = {1: 0, 2: 1, 4: 2, 5: 3, 19: 12, 20: 13}[t]
                        load_mod(ada + k + 2, i)
                    q = ln.chunk0 + 2 * t
                    act.wait_ge(units_done, at(i, 2 * BODY, CHUNK_UNIT[q]))
                    act.wait_ge(freed["d"], at(i, BODY, FREE[q + 1][1] - 2))
                    f(silu[:, t % 2, :], ps[:, q % BANKS, 0:SEQ], ACT.Silu).then_inc(freed["a"], 1)
                    act.wait_ge(freed["d"], at(i, BODY, FREE[q + 1][1]))
                    dst = GUH[:, t, :] if i is None else GUH[:, bass.ds(i * BODY + t, 1), :].rearrange("p a n -> p (a n)")
                    f(dst, graw[:, t % 2, :], ACT.Copy).then_inc(hidden_hi, 1)

                with act.Fori(0, 3) as i:
                    for t in range(BODY):
                        slot_(t, i)
                for t in range(18, 22):
                    slot_(t)
                lo = LIN[w_out]
                for m in range(DC):
                    split(lo.tile0 + 2 * m + 2)
                    if more and 1 <= m <= 6 and ada + 14 + m + 1 < ADA_TILES:
                        load_mod(ada + 14 + m + 1)
                    split(lo.tile0 + 2 * m + 3)
                    if m:
                        square(nxt, m - 1, FREE[lo.chunk0 + m - 1][1])
                square(nxt, 7, FREE[lo.chunk0 + 7][1])

            def exps(s):
                par = s % 2
                kind = STEPS[s][0]
                for qt in range(TT):
                    act.wait_ge(logits_ready, 2 * s + qt + 1)
                    if s >= 2:
                        act.wait_ge(probs_ready, 2 * s + qt - 3)
                    nk = SEQ if kind == "X" or qt == 1 else P
                    for m in range(2):
                        b = 2 * qt + m
                        src, sign = (ps_s[qt][:, m, 0:nk], 1.0) if kind == "X" else (LG[:, qt, m, 0:nk], -1.0)
                        last = f(EX[par][:, qt, m, 0:nk], src, ACT.Exp, bias=nmax[:, par, b:b + 1], scale=sign,
                                 accum_out=rowsum[:, par, b:b + 1])
                    last.then_inc(exp_ready, 1)

            def attention(kind):
                s0, s1 = STEP0[kind], STEP_END[kind]
                def output(s):
                    c = s - s0
                    act.wait_ge(pv_done, s + 1)
                    if kind == "X":
                        f(OT[:, 4 * c:4 * c + 4, :].rearrange("p (a b) n -> p a (b n)", a=2), ps[:, 0:2, :],
                          ACT.Copy).then_inc(attn_ready, 1)
                    else:
                        f(OT[:, c, :], ps[:, 0, 0:SEQ], ACT.Copy).then_inc(attn_ready, 1)
                    if kind != "A" or c % 2:
                        act.wait_ge(attn_ready, s + 1)
                    if kind == "X":
                        for k in range(4 * c, 4 * c + 4):
                            f(HH[:, k, :], OT[:, k, :], ACT.Copy).then_inc(hh_ready, 1)
                    elif kind == "B":
                        f(HH[:, c, :], OT[:, c, :], ACT.Copy).then_inc(hh_ready, 1)
                    elif c % 2:
                        f(SQ[:, c - 1:c + 1, :], OT[:, c - 1:c + 1, :], ACT.Square).then_inc(sub_sq, 1)

                exps(s0)
                for s in range(s0, s1):
                    if s + 1 < s1:
                        exps(s + 1)
                    act.wait_ge(turned, s + 1)
                    if s:
                        act.wait_ge(pv_done, s)
                    n = 512 if kind == "X" else 384
                    for m in range(1 if kind == "A" else 2):
                        last = f(PT[:, m, 0:n], ps[:, PT_BANK[m], 0:n], ACT.Copy)
                    last.then_inc(probsT_ready, 1)
                    if s > s0:
                        output(s - 1)
                output(s1 - 1)

            for n in range(2):
                act.dma_start(mod_ring[:, n * TILE:(n + 1) * TILE], a["ada"][n]).then_inc(mod_loaded[n], 16)
            act.wait_ge(prm_loaded, 16)
            act.wait_ge(vec_consts, 1)
            f(c_act[:, :], col("c", 0, DC), ACT.Silu).then_inc(c_ready, 1)
            act.wait_ge(lam_sum_ready, 1)
            f(lam_exp[:, :], lam_sum[:, :], ACT.Exp).then_inc(lam_exp_ready, 1)
            for h in range(0, A_HEADS, 2):
                act.wait_ge(units_done, h + 1)
                f(stg[:, h, :], ps[:, h % BANKS, :], ACT.Copy).then_inc(freed["a"], 1)
            load_mod(2)
            load_mod(3)
            act.wait_ge(x_loaded, 16)
            for k in range(DC):
                square(0, k)
            norm_root(0)
            act.wait_ge(freed["a"], 4)
            act.wait_ge(freed["d"], 4)
            act.dma_start(bias_rows.rearrange("h (p j) -> p h j", p=P), stg).then_inc(rows_written, 16)
            load_mod(4)
            split(0)
            load_mod(5)
            split(1)
            for n in range(6, 10):
                load_mod(n)
            act.wait_ge(rows_written, 16)
            act.dma_start(bias, bias_rows[:, 0:P * 511].rearrange("h (p x) -> p h x", p=P)[:, :, 127:127 + SEQ]
                          ).then_inc(bias_loaded, 16)
            shift_high("n0", 0)
            ffn(0, "f00_in", "f00_out", 1, 8)

            norm_root(1)
            shift_high("n1", 1)
            for t in range(4):
                split(LIN["a_q"].tile0 + t + 2)
                if t:
                    load_mod(28 + t + 1)
                for m in range(2):
                    q = 2 * t + m
                    take("a_q", q, QT[:, q, :], scale=HD ** -0.5)
            for t in range(4):
                split(LIN["a_k"].tile0 + t + 2)
                load_mod(32 + t + 1)
            for t in range(4):
                split(LIN["a_v"].tile0 + t + 2)
                if t == 0:
                    load_mod(37)
                take("a_v", 2 * t, V[:, 0, t * 256:(t + 1) * 256])
            attention("A")
            for b in range(4):
                act.wait_ge(sub_sum, b + 1)
                f(T[:, 2 * b:2 * b + 2, :].rearrange("p a n -> p (a n)"), ps[:, SUB_BANK[b], :], ACT.Sqrt, scale=1.0 / P,
                  bias=eps[:, :]).then_inc(sub_root, 1)
            for c in range(DC):
                act.wait_ge(sub_done, c // 2 + 1)
                f(HH[:, c, :], OT[:, c, :], ACT.Copy).then_inc(hh_ready, 1)
            residual("a_o", 2)

            norm_root(2)
            shift_high("n2", 2)
            ffn(1, "f01_in", "f01_out", 3, 36)
            norm_root(3)
            shift_high("n3", 3)
            for t in range(4):
                split(LIN["s_k"].tile0 + t + 2)
            for t in range(4):
                split(LIN["s_v"].tile0 + t + 2)
                take("s_v", 2 * t, VS[:, 0, t * 256:(t + 1) * 256])
            act.wait_ge(fz_done, 1)
            step(f(f_z, ps_f, ACT.Identity, bias=fgate_b[:, :]))
            step(f(f_t, f_z, ACT.Abs))
            step(f(f_t, f_t, ACT.Exp, scale=-1.0))
            f(f_t, f_t, ACT.Ln, bias=1.0).then_inc(fz_ln, 1)

            shift_high("n4", 4)
            act.wait_ge(f_ready, 1)
            ffn(2, "f10_in", "f10_out", 5, 56)
            norm_root(5)
            shift_high("n5", 5)
            for t in range(4):
                split(LIN["b_q"].tile0 + t + 2)
                if t in (1, 2):
                    load_mod(76 + t + 1)
                for m in range(2):
                    q = 2 * t + m
                    take("b_q", q, QT[:, q, :], scale=HD ** -0.5)
            attention("B")
            residual("b_o", 6)
            norm_root(6)
            shift_high("n6", 6)
            ffn(3, "f11_in", "f11_out", N_FINAL, None)
            norm_root(N_FINAL)

            for k in range(DC):
                act.wait_ge(t_ready, 8 * N_FINAL + k + 1)
                square(N_MIX, k)
            norm_root(N_MIX)
            norm_high(N_MIX)
            for c in range(DC):
                split(LIN["mix_a"].tile0 + 2 * c + 2)
                if c >= 2:
                    act.wait_ge(freed["d"], FREE[LIN["mix_a"].chunk0 + 4 * (c - 2) + 3][1])
                take("mix_a", 4 * c, T0[:, c % 2, :])
                split(LIN["mix_a"].tile0 + 2 * c + 3)
                take("mix_a", 4 * c + 2, T1[:, c % 2, :], ACT.Sigmoid, bias=col("cf_b_pw1", 8 + c))
            for t in range(4):
                split(LIN["mix_b"].tile0 + t + 2)
            act.wait_ge(mean_sum, 1)
            f(ZB, ps_norm, ACT.Copy, scale=1.0 / D).then_inc(mean_ready, 1)
            for t in range(8):
                split(LIN["mix_g"].tile0 + t + 2)
                if t == 1:
                    for k in range(DC):
                        act.wait_ge(centred, k // 4 + 1)
                        f(SQ[:, k, :], Z[:, k, :], ACT.Square).then_inc(ln_sq, 1)
                if t == 2:
                    act.wait_ge(ln_sum, 1)
                    f(root[:, :], ps_norm, ACT.Sqrt, scale=1.0 / D, bias=eps[:, :]).then_inc(ln_root, 1)
                    for k in range(DC):
                        act.wait_ge(freed["d"], FREE[LIN["mix_b"].chunk0 + k][1])
                        f(EH[:, k, :], C3[:, k, :], ACT.Copy).then_inc(eh_ready, 1)
                for m in range(2):
                    q = 2 * t + m
                    take("mix_g", q, SG[:, q, :] if q < DC else CG[:, q - DC, :], ACT.Sigmoid)
            for k in range(DC):
                act.wait_ge(ln_scaled, k // 4 + 1)
                f(Z[:, k, :], Z[:, k, :], ACT.Silu, scale=col("ln_g", k), bias=col("ln_b", k)).then_inc(ln_ready, 1)
            for t in range(2):
                split(LIN["sc_out"].tile0 + t + 2)
            act.wait_ge(ln_ready, DC)
            act.wait_ge(units_done, LIN["mix_g"].unit_end)
            for k in range(DC):
                f(HH[:, k, :], Z[:, k, :], ACT.Copy).then_inc(hh_ready, 1)
            for t in range(2, 4):
                split(LIN["sc_out"].tile0 + t + 2)

            def merged_high(k):
                act.wait_ge(freed["d"], FREE[LIN["cf_out"].chunk0 + k][1])
                f(EH[:, k, :], SG[:, k, :], ACT.Copy).then_inc(eh_ready, 1)

            for t in range(4):
                split(LIN["cf_out"].tile0 + t + 2)
                if t == 1:
                    act.wait_ge(mem_loaded, 16)
                    for k in range(DC):
                        f(SQ[:, k, :], MEM[:, k, :], ACT.Square).then_inc(squares_ready, 1)
                if t:
                    merged_high(2 * t - 2)
                    merged_high(2 * t - 1)
            merged_high(6)
            merged_high(7)
            norm_root(N_MEM)
            norm_high(N_MEM)
            residual("mix_out", N_XA)
            norm_root(N_XA)
            for t in range(4):
                split(LIN["x_k"].tile0 + t + 2)
                if t == 0:
                    norm_high(N_XA, second=True)
            for t in range(4):
                split(LIN["x_v"].tile0 + t + 2)
                take("x_v", 2 * t, V[:, 0, t * 256:(t + 1) * 256])
            for t in range(4):
                split(LIN["x_q"].tile0 + t + 2)
                for q in (2 * t, 2 * t + 1):
                    take("x_q", q, QT[:, q, :], scale=(D // 4) ** -0.5)
            attention("X")
            residual("x_o", N_PEER)
            norm_root(N_PEER)
            norm_high(N_PEER)

            def sub_copies(h):
                for t in range(TT):
                    act.wait_ge(sub_scores, 2 * h + t + 1)
                    f(S[t][:, 2 * h:2 * h + 2, :].rearrange("p a n -> p (a n)"), ps[:, 3 + 2 * (h % 2) + t, 0:2 * NK],
                      ACT.Copy).then_inc(s_ready, 1)

            for t in range(8):
                split(LIN["pq"].tile0 + t + 2)
                take("pq", 2 * t, QP[:, 2 * t, :])
                if t:
                    sub_copies(t - 1)
            sub_copies(7)
            for b in range(8):
                dst = (HTOK, XTOK)[b // 4]
                act.wait_ge(tok_turned, b + 1)
                f(dst[:, (b // 2) % 2, (b % 2) * 512:(b % 2 + 1) * 512], ps[:, b % 2, :], ACT.Copy).then_inc(tok_ready, 1)
            for n in range(2 * TT):
                t, cs = n // 2, slice(n % 2 * HALF * TK, (n % 2 + 1) * HALF * TK)
                act.wait_ge(gate_diff, n + 1)
                f(GT[:, t, cs], GT[:, t, cs], ACT.Exp).then_inc(gate_exp, 1)
            for t in range(TT):
                act.wait_ge(dots_ready, t + 1)
                f(DOT[:, t, :], DOT[:, t, :], ACT.Gelu).then_inc(gelu_ready, 1)
                act.wait_ge(y_ready, t + 1)
                step(f(YO[:, t, :], YACC[:, 0, :], ACT.Square, accum_out=YS[:, t:t + 1]))
                f(YS[:, t:t + 1], YS[:, t:t + 1], ACT.Sqrt, scale=1.0 / D, bias=eps[:, :]).then_inc(yroot_ready, 1)

        @block.vector
        def _(dve):
            step = Chain(dve, dve_step)
            v = nc.vector

            def split(g, i=None):
                if g >= N_TILES or TILE_POOL[g]:
                    return
                if g and TILE_POOL[g - 1]:
                    dve.wait_ge(lo_ready, g)
                dve.wait_ge(hi_ready, at(i, BODY, g + 1))
                v.tensor_tensor(slot(w_lo, g), slot(raw, g), f32(slot(w_hi, g)), ALU.subtract).then_inc(lo_ready, 1)

            def mod_acc_tile(n, i=None):
                s = n % 2
                dve.wait_ge(mod_loaded[s], at(i, 32, 16 * (n // 2 + 1)))
                w = mod_ring[:, s * TILE:(s + 1) * TILE].rearrange("p (k n) -> p k n", k=DC)
                step(v.tensor_scalar(mod_acc[:, s, :], w[:, 0, :], c_act[:, 0:1], None, ALU.mult))
                for k in range(1, DC):
                    ins = v.scalar_tensor_tensor(mod_acc[:, s, :], w[:, k, :], c_act[:, k:k + 1], mod_acc[:, s, :],
                                                 ALU.mult, ALU.add)
                    if k < DC - 1:
                        step(ins)
                ins.then_inc(acc_ready, 1)

            def mod_take(n, i=None):
                dve.wait_ge(modsum_ready, at(i, 4, n + 1))
                if i is None:
                    dst, b = mods[:, 2 * n:2 * n + 2], col("ada_b", 2 * n, 2)
                else:
                    dst = mods[:, bass.ds(i * 8 + 2 * n, 2)]
                    b = prm[:, bass.ds(i * 8 + (COL["ada_b"] + 2 * n), 2)]
                v.tensor_tensor(dst, ps_mod[:, 0:2], b, ALU.add).then_inc(mods_ready, 1)

            def norm(n, src, name=None, mods_done=None, dst=None):
                g, m0 = NORMS[n]
                dst = T if dst is None else dst
                if m0 is not None:
                    dve.wait_ge(mods_ready, mods_done)
                    step(v.scalar_tensor_tensor(gain[:, :], mods[:, m0 + 8:m0 + 16], 1.0, prm[:, g:g + 8],
                                                ALU.add, ALU.mult))
                if n in RANK:
                    dve.wait_ge(root_ready, RANK[n] + 1)
                    step(v.reciprocal(rinv[:, :], root[:, :]))

                def low(k):
                    dve.wait_ge(hh_ready, SET[name] + k + 1)
                    v.scalar_tensor_tensor(HL[:, k, :], T[:, k, :], mods[:, m0 + k:m0 + k + 1], f32(HH[:, k, :]),
                                           ALU.add, ALU.subtract).then_inc(hl_ready, 1)

                for k in range(DC):
                    gk = prm[:, g + k:g + k + 1] if m0 is None else gain[:, k:k + 1]
                    v.scalar_tensor_tensor(dst[:, k, :], src[:, k, :], gk, rinv[:, :], ALU.mult, ALU.mult
                                           ).then_inc(t_ready, 1)
                    if m0 is not None and k >= 2:
                        low(k - 2)
                if m0 is not None:
                    low(DC - 2)
                    low(DC - 1)

            def take(name, q, op):
                q = LIN[name].chunk0 + q
                dve.wait_ge(units_done, CHUNK_UNIT[q])
                assert FREE[q][0] == "d"
                op(ps[:, q % BANKS, 0:SEQ]).then_inc(freed["d"], 1)

            def ffn(n, w_in, w_out, gate0, ada):
                ln = LIN[w_in]
                more = ada is not None

                def slot_(t, i=None):
                    acc = {0: 0, 1: 1, 3: 2, 4: 3, 18: 12, 19: 13}.get(t) if more else None
                    got = {1: 0, 2: 1, 4: 2, 5: 3, 19: 12, 20: 13}.get(t) if more else None
                    if acc is not None:
                        mod_acc_tile(ada + acc, i)
                    split(ln.tile0 + t + 2, i)
                    if got is not None:
                        mod_take(ada + got, i)
                    q = ln.chunk0 + 2 * t + 1
                    dve.wait_ge(units_done, at(i, 2 * BODY, CHUNK_UNIT[q]))
                    dve.wait_ge(freed["a"], at(i, BODY, FREE[q - 1][1]))
                    dve.wait_ge(hidden_lo, at(i, BODY, FC * n + t + 1))
                    v.tensor_tensor(graw[:, t % 2, :], ps[:, q % BANKS, 0:SEQ], silu[:, t % 2, :], ALU.mult
                                    ).then_inc(freed["d"], 1)

                with dve.Fori(0, 3) as i:
                    if more:
                        step.enter(i, 28)
                    for t in range(BODY):
                        slot_(t, i)
                    if more:
                        step.leave(3)
                for t in range(18, 22):
                    slot_(t)
                dve.wait_ge(mods_ready, ada + 14 if more else ADA_TILES)
                step(v.tensor_scalar(half_gate[:, :], mods[:, gate0:gate0 + 8], 0.5, None, ALU.mult))
                lo = LIN[w_out]
                for m in range(DC):
                    with_mod = more and 1 <= m <= 6
                    if with_mod:
                        mod_acc_tile(ada + 14 + m - 1)
                    split(lo.tile0 + 2 * m + 2)
                    split(lo.tile0 + 2 * m + 3)
                    if with_mod:
                        mod_take(ada + 14 + m - 1)
                    take(w_out, m, lambda p: v.scalar_tensor_tensor(
                        X[:, m, :], p, half_gate[:, m:m + 1], X[:, m, :], ALU.mult, ALU.add))

            def residual(name, gate0=None):
                for t in range(4):
                    split(LIN[name].tile0 + t + 2)
                    for q in (2 * t, 2 * t + 1):
                        if gate0 is None:
                            take(name, q, lambda p: v.tensor_tensor(X[:, q, :], p, X[:, q, :], ALU.add))
                        else:
                            take(name, q, lambda p: v.scalar_tensor_tensor(
                                X[:, q, :], p, mods[:, gate0 + q:gate0 + q + 1], X[:, q, :], ALU.mult, ALU.add))

            def logits(s):
                kind, c = STEPS[s]
                par = s % 2
                for qt in range(TT):
                    u = 2 * s + qt
                    dve.wait_ge(scores_done, u + 1)
                    if s:
                        dve.wait_ge(exp_ready, u - 1)
                    if kind == "X":
                        v.reduce_max(nmax[:, par, 2 * qt:2 * qt + 2], ps_s[qt][:, :, 0:SEQ], axis=AX.X, negate=True
                                     ).then_inc(logits_ready, 1)
                        continue
                    nk = SEQ if qt == 1 else P
                    b = bias[:, c, SEQ - nk:SEQ] if kind == "A" else mask[:, SEQ - nk:SEQ]
                    for m in range(2):
                        last = v.tensor_tensor_reduce(out=LG[:, qt, m, 0:nk], in0=ps_s[qt][:, m, 0:nk], in1=b,
                                                      scale=-1.0, scalar=3.0e38, op0=ALU.add, op1=ALU.min,
                                                      accum_out=nmax[:, par, 2 * qt + m:2 * qt + m + 1])
                    last.then_inc(logits_ready, 1)

            def probs(s):
                kind, c = STEPS[s]
                par = s % 2
                dve.wait_ge(exp_ready, 2 * s + 2)
                r = rscale[:, par, :]
                step(v.reciprocal(r, rowsum[:, par, :]))
                if kind == "A":
                    step(v.tensor_tensor(r, r, lam_vec[:, :], ALU.mult))
                if s:
                    dve.wait_ge(turned, s)
                if kind == "A":
                    for qt, nk in ((0, P), (1, SEQ)):
                        step(v.tensor_scalar(PR[:, qt, 0, 0:nk], EX[par][:, qt, 0, 0:nk], r[:, 2 * qt:2 * qt + 1], None,
                                             ALU.mult), lag=1)
                    for qt, nk in ((0, P), (1, SEQ)):
                        if qt:
                            dve.wait_ge(dve_step, step.n)
                        v.scalar_tensor_tensor(PR[:, qt, 0, 0:nk], EX[par][:, qt, 1, 0:nk], r[:, 2 * qt + 1:2 * qt + 2],
                                               PR[:, qt, 0, 0:nk], ALU.mult, ALU.add).then_inc(probs_ready, 1)
                    return
                for qt in range(TT):
                    nk = SEQ if kind == "X" or qt == 1 else P
                    v.tensor_tensor(PR[:, qt, :, 0:nk], EX[par][:, qt, :, 0:nk],
                                    r[:, 2 * qt:2 * qt + 2].unsqueeze(2).broadcast_to([P, 2, nk]), ALU.mult
                                    ).then_inc(probs_ready, 1)

            def attention(kind):
                s0, s1 = STEP0[kind], STEP_END[kind]
                logits(s0)
                for s in range(s0, s1):
                    if s + 1 < s1:
                        logits(s + 1)
                    probs(s)

            v.memset(eps[:, :], EPS)
            step(v.memset(ones[:, :], 1.0))
            v.memset(table[NB:NB + 1, :], NEG)
            step(v.memset(lam_vec[:, :], 1.0))
            dve.sem_inc(vec_consts, 1)
            dve.wait_ge(small_loaded, 80)
            v.tensor_copy(table_rep[:, :, :], table[:, :].unsqueeze(2).broadcast_to([NB + 1, A_HEADS, P])
                          ).then_inc(table_ready, 1)
            lp = lamp[:, :].rearrange("p (a b n) -> p a b n", a=2, b=2)
            step(v.tensor_tensor(lam_prod[:, :, :], lp[:, :, 0, :], lp[:, :, 1, :], ALU.mult))
            v.reduce_sum(lam_sum[:, :], lam_prod[:, :, :], axis=AX.X).then_inc(lam_sum_ready, 1)
            for h in range(1, A_HEADS, 2):
                dve.wait_ge(units_done, h + 1)
                v.tensor_copy(stg[:, h, :], ps[:, h % BANKS, :]).then_inc(freed["d"], 1)
            dve.wait_ge(prm_loaded, 16)
            dve.wait_ge(c_ready, 1)
            dve.wait_ge(lam_exp_ready, 1)
            step(v.tensor_tensor(lam_vec[:, 1:2], lam_exp[:, 1:2], lam_exp[:, 0:1], ALU.subtract))
            step(v.tensor_scalar(lam_vec[:, 1:2], lam_vec[:, 1:2], -LAM_INIT, None, ALU.add))
            step(v.tensor_copy(lam_vec[:, 3:4], lam_vec[:, 1:2]))
            step(v.tensor_scalar(sub_gain[:, :], col("subln_g"), 1.0 - LAM_INIT, None, ALU.mult))
            for n in range(8):
                if n >= 2:
                    mod_take(n - 2)
                mod_acc_tile(n)
                if n in (5, 6):
                    split(n - 5)
            mod_take(6)
            mod_take(7)
            norm(0, X, "n0", 8)
            ffn(0, "f00_in", "f00_out", MOD_L0 + 16, 8)

            norm(1, X, "n1", 28)
            for t in range(4):
                mod_acc_tile(28 + t)
                split(LIN["a_q"].tile0 + t + 2)
                if t:
                    mod_take(28 + t - 1)
            for t in range(4):
                mod_acc_tile(32 + t)
                split(LIN["a_k"].tile0 + t + 2)
                mod_take(31 + t)
                for q in (2 * t, 2 * t + 1):
                    take("a_k", q, lambda p: v.tensor_copy(KT[:, q, :], p))
            for t in range(4):
                split(LIN["a_v"].tile0 + t + 2)
                if t == 0:
                    mod_take(35)
                take("a_v", 2 * t + 1, lambda p: v.tensor_copy(V[:, 1, t * 256:(t + 1) * 256], p))
            dve.wait_ge(bias_loaded, 16)
            attention("A")
            for b in range(4):
                tq = T[:, 2 * b:2 * b + 2, :]
                oq = OT[:, 2 * b:2 * b + 2, :]
                dve.wait_ge(sub_root, b + 1)
                step(v.reciprocal(tq, tq))
                v.scalar_tensor_tensor(oq, oq, sub_gain[:, :], tq, ALU.mult, ALU.mult).then_inc(sub_done, 1)
            residual("a_o", MOD_L0 + 40)
            norm(2, X, "n2", 36)
            ffn(1, "f01_in", "f01_out", MOD_L0 + 64, 36)

            norm(3, X, "n3", 56)
            for t in range(4):
                split(LIN["s_k"].tile0 + t + 2)
                for q in (2 * t, 2 * t + 1):
                    take("s_k", q, lambda p: v.tensor_copy(KS[:, q, :], p))
            for t in range(4):
                split(LIN["s_v"].tile0 + t + 2)
                take("s_v", 2 * t + 1, lambda p: v.tensor_copy(VS[:, 1, t * 256:(t + 1) * 256], p))
            dve.wait_ge(fz_ln, 1)
            step(v.tensor_scalar(f_z[:, :], f_z[:, :], 0.0, None, ALU.min))
            step(v.tensor_tensor(f_z[:, :], f_z[:, :], f_t[:, :], ALU.subtract))
            step(v.memset(f_t[:, :], 1.0))
            step(v.tensor_tensor_scan(f_sum[:, :], f_t[:, :], f_z[:, :], 0.0, ALU.mult, ALU.add))
            v.tensor_scalar(f_neg[:, :], f_sum[:, :], -1.0, None, ALU.mult).then_inc(f_ready, 1)

            norm(4, X, "n4", 56)
            ffn(2, "f10_in", "f10_out", MOD_L1 + 16, 56)
            for tile_ in (DQ, DK):
                for odd in range(2):
                    v.memset(tile_[64 * odd:64 * odd + 2, :, :], 1.0).then_inc(decay_cleared, 1)
            norm(5, X, "n5", 76)
            for t in range(4):
                mod_acc_tile(76 + t)
                split(LIN["b_q"].tile0 + t + 2)
                if t:
                    mod_take(76 + t - 1)
            mod_take(79)
            attention("B")
            residual("b_o", MOD_L1 + 40)
            norm(6, X, "n6", 80)
            ffn(3, "f11_in", "f11_out", MOD_L1 + 64, None)
            norm(N_FINAL, X, dst=X)

            v.memset(U[:, :, 0:SCK - 1], 0.0)
            step(v.memset(CV[:, :, 0:CFK - 1], 0.0))
            norm(N_MIX, X)
            mix = LIN["mix_a"].chunk0
            for c in range(DC):
                split(LIN["mix_a"].tile0 + 2 * c + 2)
                dve.wait_ge(freed["a"], FREE[mix + 4 * c][1])
                take("mix_a", 4 * c + 1, lambda p: v.tensor_tensor(U[:, c, SCK - 1:], p, T0[:, c % 2, :], ALU.mult))
                split(LIN["mix_a"].tile0 + 2 * c + 3)
                dve.wait_ge(freed["a"], FREE[mix + 4 * c + 2][1])
                take("mix_a", 4 * c + 3, lambda p: v.scalar_tensor_tensor(
                    CV[:, c, CFK - 1:], p, col("cf_b_pw1", c), T1[:, c % 2, :], ALU.add, ALU.mult))
                dve.wait_ge(freed["d"], FREE[mix + 4 * c + 3][1])
                w3 = lambda k: col("sc_w", 8 * k + c)
                w31 = lambda k: col("cf_w", 8 * k + c)
                step(v.tensor_scalar(Z[:, c, :], CV[:, c, 0:SEQ], w31(0), col("cf_conv_b", c), ALU.mult, ALU.add), lag=1)
                step(v.tensor_scalar(SQ[:, c, :], CV[:, c, 1:1 + SEQ], w31(1), None, ALU.mult), lag=1)
                for k in range(2, CFK):
                    dst = (Z, SQ)[k % 2]
                    step(v.scalar_tensor_tensor(dst[:, c, :], CV[:, c, k:k + SEQ], w31(k), dst[:, c, :],
                                                ALU.mult, ALU.add), lag=1)
                step(v.tensor_scalar(C3[:, c, :], U[:, c, 0:SEQ], w3(0), None, ALU.mult))
                v.tensor_tensor(Z[:, c, :], Z[:, c, :], SQ[:, c, :], ALU.add).then_inc(conv_done, 1)
                for k in range(1, SCK):
                    step(v.scalar_tensor_tensor(C3[:, c, :], U[:, c, k:k + SEQ], w3(k), C3[:, c, :], ALU.mult, ALU.add))
            for t in range(4):
                split(LIN["mix_b"].tile0 + t + 2)
                for q in (2 * t, 2 * t + 1):
                    take("mix_b", q, lambda p: v.tensor_tensor(C3[:, q, :], p, C3[:, q, :], ALU.mult))
            for t in range(8):
                split(LIN["mix_g"].tile0 + t + 2)
                if t == 0:
                    dve.wait_ge(mean_ready, 1)
                    for half in (slice(0, 4), slice(4, 8)):
                        v.tensor_tensor(Z[:, half, :], Z[:, half, :], ZB.unsqueeze(1).broadcast_to([P, 4, SEQ]),
                                        ALU.subtract).then_inc(centred, 1)
                if t == 3:
                    dve.wait_ge(ln_root, 1)
                    step(v.reciprocal(rinv[:, :], root[:, :]))
                    for half in (slice(0, 4), slice(4, 8)):
                        v.tensor_tensor(Z[:, half, :], Z[:, half, :], rinv[:, :].unsqueeze(1).broadcast_to([P, 4, SEQ]),
                                        ALU.mult).then_inc(ln_scaled, 1)
            dve.wait_ge(freed["a"], LIN["mix_g"].freed_a)
            for t in range(4):
                split(LIN["sc_out"].tile0 + t + 2)
                for q in (2 * t, 2 * t + 1):
                    take("sc_out", q, lambda p: v.tensor_tensor(SG[:, q, :], p, SG[:, q, :], ALU.mult))
            for t in range(4):
                split(LIN["cf_out"].tile0 + t + 2)
                for q in (2 * t, 2 * t + 1):
                    qq = LIN["cf_out"].chunk0 + q
                    dve.wait_ge(units_done, CHUNK_UNIT[qq])
                    step(v.scalar_tensor_tensor(CG[:, q, :], ps[:, qq % BANKS, 0:SEQ], col("b_pw2", q), CG[:, q, :],
                                                ALU.add, ALU.mult))
                    v.tensor_tensor(SG[:, q, :], SG[:, q, :], CG[:, q, :], ALU.add).then_inc(freed["d"], 1)
            norm(N_MEM, MEM)
            residual("mix_out")

            for t in range(4):
                split(LIN["x_k"].tile0 + t + 2)
                if t == 0:
                    dve.wait_ge(hl_ready, SET["n9"] + DC)
                    norm(N_XA, X)
                for q in (2 * t, 2 * t + 1):
                    take("x_k", q, lambda p: v.tensor_copy(KT[:, q, :], p))
            for t in range(4):
                split(LIN["x_v"].tile0 + t + 2)
                take("x_v", 2 * t + 1, lambda p: v.tensor_copy(V[:, 1, t * 256:(t + 1) * 256], p))
            for t in range(4):
                split(LIN["x_q"].tile0 + t + 2)
            attention("X")
            residual("x_o")
            norm(N_PEER, X)

            def head_best(t, h):
                dve.wait_ge(s_ready, 2 * h + t + 1)
                hps = (2 * h, 2 * h + 1)
                s_ = S[t]
                for hp in hps:
                    step(v.max(TV[:, hp, 0:8], s_[:, hp, :]), lag=1)
                for hp in hps:
                    step(v.max_index(TI[:, hp, 0:8], TV[:, hp, 0:8], s_[:, hp, :]), lag=1)
                    step(v.match_replace(S2[:, hp, :], TV[:, hp, 0:8], s_[:, hp, :], -3.0e38), lag=1)
                for hp in hps:
                    step(v.max(TV[:, hp, 8:16], S2[:, hp, :]), lag=1)
                for hp in hps:
                    step(v.max_index(TI[:, hp, 8:16], TV[:, hp, 8:16], S2[:, hp, :]), lag=1)
                pair = [P, TK, TK]
                step(v.tensor_tensor(CA[:, h, :].rearrange("p (a b) -> p a b", a=TK),
                                     TV[:, 2 * h, :].unsqueeze(2).broadcast_to(pair),
                                     TV[:, 2 * h + 1, :].unsqueeze(1).broadcast_to(pair), ALU.add))
                step(v.max(FV[:, h, 0:8], CA[:, h, :]))
                step(v.max_index(FP[:, h, 0:8], FV[:, h, 0:8], CA[:, h, :]), lag=1)
                step(v.match_replace(CA2[:, h, :], FV[:, h, 0:8], CA[:, h, :], -3.0e38))
                step(v.max(FV[:, h, 8:16], CA2[:, h, :]))
                step(v.max_index(FP[:, h, 8:16], FV[:, h, 8:16], CA2[:, h, :]))

            def choose(t, half):
                hs = slice(half * HALF, (half + 1) * HALF)
                hp2 = slice(2 * half * HALF, 2 * (half + 1) * HALF)
                n_ = HALF * TK
                cs = slice(half * n_, (half + 1) * n_)
                v.tensor_copy(TIF[:, hp2, :], TI[:, hp2, :])
                v.tensor_tensor(GT[:, t, cs].rearrange("p (h k) -> p h k", h=HALF), FV[:, hs, :],
                                FV[:, hs, 0:1].broadcast_to([P, HALF, TK]), ALU.subtract).then_inc(gate_diff, 1)
                fp = FP[:, hs, :].rearrange("p h k -> p (h k)")
                v.tensor_scalar(AI[:, cs], fp, 4, None, ALU.logical_shift_right)
                step(v.tensor_scalar(BI[:, cs], fp, TK - 1, None, ALU.bitwise_and))
                v.tensor_copy(AF[:, cs], AI[:, cs])
                step(v.tensor_copy(BF[:, cs], BI[:, cs]))
                tif = TIF[:, hp2, :].rearrange("p (h s) k -> p h s k", s=2)
                for src, side, dst, room in ((AF, 0, I0, S[t]), (BF, 1, I1, S2)):
                    eq = room[:, hp2, :].rearrange("p a n -> p (a n)").rearrange("p (c j) -> p c j", c=n_)
                    step(v.tensor_tensor(eq, src[:, cs].unsqueeze(2).broadcast_to([P, n_, TK]),
                                         iota16[:, :].unsqueeze(1).broadcast_to([P, n_, TK]), ALU.is_equal))
                    e4 = eq.rearrange("p (h k) j -> p h k j", h=HALF)
                    step(v.tensor_tensor(e4, e4, tif[:, :, side, :].unsqueeze(2).broadcast_to([P, HALF, TK, TK]), ALU.mult))
                    step(v.reduce_sum(dst[:, cs], eq, axis=AX.X))
                v.scalar_tensor_tensor(IDX[:, t, cs], I0[:, cs], float(NK), I1[:, cs], ALU.mult, ALU.add
                                       ).then_inc(idx_ready, 1)

            def gates(t):
                gt = GT[:, t, :].rearrange("p (h k) -> p h k", h=PH)
                dve.wait_ge(gate_exp, 2 * t + 2)
                step(v.reduce_sum(GS[:, 8:16], gt, axis=AX.X))
                step(v.reciprocal(GS[:, 8:16], GS[:, 8:16]))
                step(v.tensor_tensor(gt, gt, GS[:, 8:16].unsqueeze(2).broadcast_to([P, PH, TK]), ALU.mult))

            dve.sem_inc(rows_free, GROUP)
            for t in range(PH):
                if t:
                    head_best(0, t - 1)
                take("pq", 2 * t + 1, lambda p: v.tensor_copy(QP[:, 2 * t + 1, :], p))
                if t == HALF:
                    choose(0, 0)
            head_best(0, PH - 1)
            choose(0, 1)
            dve.wait_ge(tok_ready, 8)
            dve.wait_ge(gfin_loaded, 16)

            def dot(t, group, j, dst, i=None):
                dve.wait_ge(row_loaded[j], at(i, 16, 16 * (group + 1)))
                v.tensor_tensor_reduce(out=junk[:, j % 2, :], in0=rows_ring[:, j * D:(j + 1) * D], in1=HTOK[:, t, :],
                                       scale=1.0, scalar=0.0, op0=ALU.mult, op1=ALU.add, accum_out=dst
                                       ).then_inc(rows_free, 1)
                if j >= 1:
                    dve.wait_ge(rows_free, at(i, GROUP, GROUP * (group + 1) + j))

            for t in range(TT):
                seg = 2 * t * N_GROUPS
                if t == 0:
                    for g in range(N_GROUPS):
                        for j in range(GROUP):
                            n_ = g * GROUP + j
                            dot(t, g, j, DOT[:, t, n_:n_ + 1])
                        dve.wait_ge(rows_free, GROUP * (g + 2))
                        head_best(1, g)
                        if g % HALF == HALF - 1:
                            choose(1, g // HALF)
                else:
                    with dve.Fori(0, N_GROUPS) as i:
                        for j in range(GROUP):
                            dot(t, seg, j, dot16[:, j:j + 1], i)
                        dve.wait_ge(rows_free, i * GROUP + GROUP * (seg + 2))
                        step.enter(i, 1)
                        step(v.tensor_copy(DOT[:, t, bass.ds(i * GROUP, GROUP)], dot16[:, :]))
                        step.leave(N_GROUPS)
                dve.sem_inc(dots_ready, 1)
                gates(t)
                step(v.memset(YACC[:, 0, :], 0.0))
                step(v.memset(YACC[:, 1, :], 0.0))
                dve.wait_ge(gelu_ready, t + 1)
                step(v.tensor_tensor(CF[:, t, :], DOT[:, t, :], GT[:, t, :], ALU.mult))
                seg += N_GROUPS
                with dve.Fori(0, N_GROUPS) as i:
                    step.enter(i, 1)
                    step(v.tensor_copy(coef16[:, :], CF[:, t, bass.ds(i * GROUP, GROUP)]))
                    step.leave(N_GROUPS)
                    for j in range(GROUP):
                        dve.wait_ge(row_loaded[j], i * 16 + 16 * (seg + 1))
                        y = YACC[:, j % 2, :]
                        v.scalar_tensor_tensor(y, rows_ring[:, j * D:(j + 1) * D], coef16[:, j:j + 1], y,
                                               ALU.mult, ALU.add).then_inc(rows_free, 1)
                        if j >= 1:
                            dve.wait_ge(rows_free, i * GROUP + (GROUP * (seg + 1) + j))
                    dve.wait_ge(rows_free, i * GROUP + GROUP * (seg + 2))
                step(v.tensor_tensor(YACC[:, 0, :], YACC[:, 0, :], YACC[:, 1, :], ALU.add))
                v.tensor_tensor(YACC[:, 0, :], YACC[:, 0, :], XTOK[:, t, :], ALU.add).then_inc(y_ready, 1)
                dve.wait_ge(yroot_ready, t + 1)
                step(v.reciprocal(YS[:, 2 + t:3 + t], YS[:, t:t + 1]))
                v.scalar_tensor_tensor(YO[:, t, :], YACC[:, 0, :], YS[:, 2 + t:3 + t], gfin,
                                       ALU.mult, ALU.mult).then_inc(yo_ready, 1)


def relative_buckets():
    rel = 255 - np.arange(512)
    n = np.maximum(rel, 0)
    exact = NB // 2
    large = exact + (np.log(np.maximum(n, 1).astype(np.float32) / exact) / math.log(MAX_DISTANCE / exact)
                     * (NB - exact)).astype(np.int32)
    bucket = np.where(n < exact, n, np.minimum(large, NB - 1))
    bucket = np.where(rel >= 0, bucket, NB)
    return (np.arange(NB + 1)[:, None] == bucket[None, :]).astype(np.float32)


def kernel(**inputs):
    import numpy as _np
    import concourse.bacc as _bacc
    from concourse import mybir as _mybir
    from concourse.bass_utils import run_bass_kernel_spmd as _run

    x = {k: _np.asarray(v) for k, v in inputs.items()}
    cat = _np.concatenate

    def cols(v):
        return v.reshape(-1, P).T

    def tiles(w, order=None):
        k, n = w.shape
        w = w.reshape(k // P, P, n // P, P)
        if order is not None:
            w = w[:, :, order]
        w = w.reshape(k // P, P, -1, 2, P)
        return w.transpose(2, 1, 0, 3, 4).reshape(w.shape[2], P, -1)

    def out_tiles(w):
        return w.reshape(2, WO_K, P, DC, P).transpose(3, 0, 2, 1, 4).reshape(2 * DC, P, WO_K * P)

    pairs = [m + half * FC for m in range(FC) for half in range(2)]
    a = {}
    for la in range(2):
        for s in range(2):
            a[f"f{la}{s}_in"] = tiles(x["ffn_w_in"][la, s], pairs)
            a[f"f{la}{s}_out"] = out_tiles(x["ffn_w_out"][la, s])
    qkv = x["a_w_qkv"][0]
    a["a_q"], a["a_k"], a["a_v"] = (tiles(qkv[:, n * D:(n + 1) * D]) for n in range(3))
    a["a_o"] = tiles(x["a_w_o"][0])
    a["s_k"], a["s_v"] = tiles(x["kv_w"][:, :D]), tiles(x["kv_w"][:, D:])
    a["b_q"], a["b_o"] = tiles(x["b_w_q"][0]), tiles(x["b_w_o"][0])
    a["mix_a"] = tiles(x["w_in_2"][0], [b * DC + c for c in range(DC) for b in (1, 2, 4, 3)])
    a["mix_b"] = tiles(x["w_in_2"][0], [c for c in range(DC)])
    a["mix_g"] = tiles(x["w_in_2"][0], [b * DC + c for b in (5, 6) for c in range(DC)])
    a["sc_out"], a["cf_out"] = tiles(x["sc_w_out_2"][0]), tiles(x["cf_w_pw2_2"][0])
    a["mix_out"] = tiles(x["w_mix_out_2"][0])
    a["x_k"], a["x_v"] = tiles(x["w_kv_2"][0][:, :D]), tiles(x["w_kv_2"][0][:, D:])
    a["x_q"], a["x_o"], a["pq"] = tiles(x["w_q_2"][0]), tiles(x["w_xo_2"][0]), tiles(x["w_peer_q_2"][0])
    a["ada"] = cat([tiles(x["ada_w"][0]), tiles(x["kv_ada_w"]), tiles(x["ada_w"][1])])
    a["prm"] = cat([
        cols(x["c"]), cols(x["ada_b"][0]), cols(x["kv_ada_b"]), cols(x["ada_b"][1]), cols(x["norm_g"]),
        cols(x["kv_norm_g"]), cols(x["final_g"]), cols(x["norm_mix_g_2"]), cols(x["cf_b_pw1_2"]),
        cols(x["sc_conv_w_2"]), cols(x["cf_conv_w_2"]), cols(x["cf_conv_b_2"]), cols(x["cf_ln_g_2"]),
        cols(x["cf_ln_b_2"]), cols(x["cf_b_pw2_2"]), cols(x["norm_xa_g_2"]), cols(x["norm_mem_g_2"]),
        cols(x["norm_peer_g_2"]), cols(x["a_subln_g"]),
        x["fgate_w"].reshape(DC, P, B_HEADS).transpose(1, 0, 2).reshape(P, -1)], axis=1)
    a["xT"] = x["x"][0].reshape(SEQ, DC, P).transpose(2, 1, 0)
    a["memT"] = x["mem_2"][0].reshape(SEQ, DC, P).transpose(2, 1, 0)
    a["rel_bias"] = x["rel_bias"]
    a["onehot"] = relative_buckets()
    a["a_lambda"] = x["a_lambda"].reshape(1, -1)
    a["fgate_b"] = x["fgate_b"].reshape(-1, 1)
    a["subkT"] = x["peer_subkeys_2"][0].transpose(2, 0, 1)
    a["final_norm_g"] = x["final_norm_g_2"].reshape(1, -1)
    a["peer_u"], a["peer_v"] = x["peer_u_2"][0], x["peer_v_2"][0]

    nc = _bacc.Bacc("TRN2", target_bir_lowering=False, num_devices=1)
    arrays, aps = {}, {}
    for name, v in a.items():
        arrays["in_" + name] = _np.ascontiguousarray(v)
        aps[name] = nc.dram_tensor("in_" + name, v.shape, _mybir.dt.from_np(v.dtype), kind="ExternalInput").ap()
    out = nc.dram_tensor("out", (TT, P, D), _mybir.dt.float32, kind="ExternalOutput").ap()
    build_program(nc, aps, out)
    r = _run(nc, [arrays], core_ids=[0])
    return r.results[0]["out"].reshape(1, SEQ, D)
```

```python
import math
from contextlib import ExitStack

import numpy as np

import concourse.bass as bass
from concourse import mybir

F32 = mybir.dt.float32
F32R = mybir.dt.float32r
U32 = mybir.dt.uint32
ACT = mybir.ActivationFunctionType
ALU = mybir.AluOpType
AX = mybir.AxisListType

P = 128
D = 1024
DC = D // P
SEQ = 256
TT = SEQ // P
FFN = 256 * ((8 * D // 3 + 255) // 256)
FC = FFN // P
HD = 64
A_HEADS = D // (2 * HD)
B_HEADS = D // HD
NB = 32
MAX_DISTANCE = 128
EPS = 1e-6
LAM_INIT = 0.8 - 0.6 * math.exp(-0.3 * 0)
NEG = -1e30
SCK, CFK = 3, 31
PH, NK, TK = 8, 128, 16
SLOTS_PER_TILE = PH * TK

_COLS = [("c", 8), ("ada_b", 160), ("norm_g", 48), ("kv_norm_g", 8), ("final_g", 8), ("norm_mix_g", 8),
         ("cf_b_pw1", 16), ("sc_w", SCK * 8), ("cf_w", CFK * 8), ("cf_conv_b", 8), ("ln_g", 8), ("ln_b", 8),
         ("b_pw2", 8), ("norm_xa_g", 8), ("norm_mem_g", 8), ("norm_peer_g", 8), ("subln_g", 1),
         ("fgate_w", DC * B_HEADS)]
COL, NCOL = {}, 0
for _n, _w in _COLS:
    COL[_n] = NCOL
    NCOL += _w

ADA_TILES = 80
DIRECT = range(5, 8)
MOD_L0, MOD_KV, MOD_L1 = 0, 72, 88

G = COL["norm_g"]
NORMS = [(G, MOD_L0), (G + 8, MOD_L0 + 24), (G + 16, MOD_L0 + 48), (COL["kv_norm_g"], MOD_KV),
         (G + 24, MOD_L1), (G + 32, MOD_L1 + 24), (G + 40, MOD_L1 + 48),
         (COL["final_g"], None), (COL["norm_mix_g"], None), (COL["norm_mem_g"], None),
         (COL["norm_xa_g"], None), (COL["norm_peer_g"], None)]
N_FINAL, N_MIX, N_MEM, N_XA, N_PEER = 7, 8, 9, 10, 11

RING = 3
BANKS = 3
BODY = 6
TILE = DC * 2 * P
WO_K = FC // 2
WO_TILE = WO_K * P
_LIN = [("f00_in", 22, TILE, "ad"), ("f00_out", 16, WO_TILE, "d"),
        ("a_q", 4, TILE, "aa"), ("a_k", 4, TILE, "dd"), ("a_v", 4, TILE, "ad"), ("a_o", 4, TILE, "dd"),
        ("f01_in", 22, TILE, "ad"), ("f01_out", 16, WO_TILE, "d"),
        ("s_k", 4, TILE, "dd"), ("s_v", 4, TILE, "ad"),
        ("f10_in", 22, TILE, "ad"), ("f10_out", 16, WO_TILE, "d"),
        ("b_q", 4, TILE, "aa"), ("b_o", 4, TILE, "dd"),
        ("f11_in", 22, TILE, "ad"), ("f11_out", 16, WO_TILE, "d"),
        ("mix_a", 16, TILE, "ad"), ("mix_g", 8, TILE, "aa"), ("mix_b", 4, TILE, "dd"),
        ("sc_out", 4, TILE, "dd"), ("cf_out", 4, TILE, "dd"), ("mix_out", 4, TILE, "dd"),
        ("x_k", 4, TILE, "dd"), ("x_v", 4, TILE, "ad"), ("x_q", 4, TILE, "aa"),
        ("x_o", 4, TILE, "dd"), ("pq", 8, TILE, "aa")]


def low_engine(name, t):
    if name in ("mix_a", "pq"):
        return "p" if t >= 2 else "v"
    if name in ("mix_g", "mix_b"):
        return "p" if name == "mix_g" or t < 2 else "v"
    if name.endswith("_in"):
        return "p" if t % 3 == 2 else "v"
    if name[0] == "f":
        return "p" if t % 2 else "v"
    return "v"


class Linear:
    pass


LIN = {}
FREE = []
CHUNK_UNIT = []
TILE_UNIT = []
TILE_WIDTH = []
LOW = []


def _plan():
    counts, unit, lows = {"a": 0, "d": 0}, 0, {"v": 0, "p": 0}
    for e in "adadaaaa":
        counts[e] += 1
        unit += 1
        FREE.append((e, counts[e]))
        CHUNK_UNIT.append(unit)
    for name, tiles, width, who in _LIN:
        ln = Linear()
        ln.name, ln.tiles, ln.width = name, tiles, width
        ln.tile0, ln.chunk0, ln.unit0 = len(TILE_UNIT), len(FREE), unit
        for t in range(tiles):
            TILE_WIDTH.append(width)
            e = low_engine(name, t)
            lows[e] += 1
            LOW.append((e, lows[e]))
            if len(who) == 1:
                unit += 1
                if t % 2:
                    counts[who] += 1
                    FREE.append((who, counts[who]))
                    CHUNK_UNIT.append(unit)
            else:
                for e in who:
                    unit += 1
                    counts[e] += 1
                    FREE.append((e, counts[e]))
                    CHUNK_UNIT.append(unit)
            TILE_UNIT.append(unit)
        ln.unit_end, ln.freed_a, ln.freed_d = unit, counts["a"], counts["d"]
        LIN[name] = ln


_plan()
N_TILES = len(TILE_UNIT)

_SETS = ["n0", "n1", "attA", "n2", "n3", "n4", "n5", "attB", "n6", "n8", "cf", "n9", "attX", "n11"]
SET = {name: 8 * k for k, name in enumerate(_SETS)}
ESET = {name: 8 * k for k, name in enumerate(["c3", "merged", "n10"])}
RANK = {n: k for k, n in enumerate([0, 1, 2, 3, 5, 6, N_FINAL, N_MIX, N_MEM, N_XA, N_PEER])}

STEPS = [("A", c) for c in range(DC)] + [("B", c) for c in range(DC)] + [("X", c) for c in range(2)]
STEP0 = {"A": 0, "B": 8, "X": 16}
STEP_END = {"A": 8, "B": 16, "X": 18}

EARLY_TAPS = 22
GROUP = 16
HALF = PH // 2
N_GROUPS = SLOTS_PER_TILE // GROUP


PRESUM = {n: k + 1 for k, n in enumerate([1, 2, 3, 5, 6, N_FINAL, N_XA, N_PEER])}
PRE = 6
LOW_STEP = {e: sum(LOW[g][0] == e for g in range(BODY)) for e in "vp"}


def summed(n):
    return n + 1 if n < DIRECT[0] else n + 1 - len(DIRECT)


def at(i, step, base):
    return base if i is None else i * step + base


class Chain:

    def __init__(self, eng, sem):
        self.eng, self.sem, self.n, self.i, self.step = eng, sem, 0, None, 0

    def __call__(self, ins, lag=0):
        ins.then_inc(self.sem, 1)
        self.n += 1
        if self.n > lag:
            self.eng.wait_ge(self.sem, at(self.i, self.step, self.n - lag))

    def enter(self, i, step):
        self.i, self.step, self.start = i, step, self.n

    def leave(self, rounds):
        assert self.n - self.start == self.step, (self.n - self.start, self.step)
        self.n = self.start + rounds * self.step
        self.i = None


def build_program(nc, a, out):
    ctx = ExitStack()
    with ctx:
        def sb(name, shape, dt=F32):
            return ctx.enter_context(nc.sbuf_tensor(name, shape, dt))

        def sem(name):
            return ctx.enter_context(nc.semaphore(name))

        arena_at = (nc.sbuf_base + 31) // 32 * 32
        KF = 1024
        RAW_AT, WH_AT, WL_AT = 0, 6 * KF, 12 * KF
        MOD_AT, HH_AT, HL_AT, SQ_AT, KS_AT, VS_AT, X_AT = (18 * KF, 22 * KF, 24 * KF, 26 * KF, 28 * KF, 30 * KF, 32 * KF)
        WORK_AT = 34 * KF
        ARENA = 48 * KF
        sb("arena", [P, ARENA])

        def place(name, at_, n, dt=F32, parts=P):
            assert at_ + n <= ARENA
            return nc.alloc_sbuf_tensor_at(name, [parts, n], dt, offset=arena_at + 4 * at_)

        def three(t, k):
            return t[:, :].rearrange("p (a b) -> p a b", a=k)

        raw = place("raw", RAW_AT, RING * TILE)
        w_hi = place("w_hi", WH_AT, RING * TILE, F32R)
        w_lo = place("w_lo", WL_AT, RING * TILE, F32R)
        rows_ring = place("rows_ring", RAW_AT, GROUP * D)
        YO = three(place("YO", RAW_AT + GROUP * D, TT * D), TT)
        mod_ring = place("mod_ring", MOD_AT, 2 * TILE)
        HH = three(place("HH", HH_AT, DC * SEQ, F32R), DC)
        HL = three(place("HL", HL_AT, DC * SEQ, F32R), DC)
        YACC = three(place("YACC", HH_AT, 2 * D), 2)
        junk = three(place("junk", HL_AT, 2 * D), 2)
        SQ = three(place("SQ", SQ_AT, DC * SEQ), DC)
        XTOK = three(place("XTOK", SQ_AT, TT * D), TT)
        KS = three(place("KS", KS_AT, DC * SEQ), DC)
        bias = KS
        EH = three(place("EH", KS_AT, DC * SEQ, F32R), DC)
        CA2 = three(place("CA2", KS_AT, PH * TK * TK), PH)
        VS = three(place("VS", VS_AT, TT * D), TT)
        EL = three(place("EL", VS_AT, DC * SEQ, F32R), DC)
        HTOK = three(place("HTOK", VS_AT, TT * D), TT)
        X = three(place("X", X_AT, DC * SEQ), DC)
        work = place("work", WORK_AT, 14 * KF)
        first = place("first", WORK_AT + 6 * KF, 4 * TILE)
        first_more = place("first_more", HH_AT, 2 * TILE)
        GUH = three(place("GUH", WORK_AT, FC * SEQ, F32R), FC)
        GUL = three(place("GUL", WORK_AT + FC * SEQ, FC * SEQ, F32R), FC)

        mod_acc = sb("mod_acc", [P, 2, 2, 2 * P])
        prm = sb("prm", [P, NCOL])
        mods = sb("mods", [P, 2 * ADA_TILES])
        c_act = sb("c_act", [P, DC])
        gain = sb("gain", [P, DC])
        half_gate = sb("half_gate", [P, DC])
        root = sb("root", [P, SEQ])
        rinv = sb("rinv", [P, SEQ])
        ident = sb("ident", [P, P])
        ones = sb("ones", [P, P])
        mask = sb("mask", [P, SEQ])
        iota16 = sb("iota16", [P, TK])
        table = sb("table", [NB + 1, A_HEADS])
        table_rep = work[0:NB + 1, 4096:5120].rearrange("p (h n) -> p h n", h=A_HEADS)
        onehot = work[0:NB + 1, 5120:5632]
        lamp = work[:, 5632:5632 + 4 * HD]
        lam_prod = work[:, 5888:5888 + 2 * HD].rearrange("p (a n) -> p a n", a=2)
        lam_sum = sb("lam_sum", [P, 2])
        lam_exp = sb("lam_exp", [P, 2])
        lam_vec = sb("lam_vec", [P, 4])
        sub_gain = sb("sub_gain", [P, 1])
        fgate_b = sb("fgate_b", [B_HEADS, 1])
        f_z, f_t = SQ[0:B_HEADS, 0, :], SQ[0:B_HEADS, 1, :]
        f_sum = sb("f_sum", [B_HEADS, SEQ])
        f_neg = sb("f_neg", [B_HEADS, SEQ])
        subk = sb("subk", [P, 2, NK])
        nmax = sb("nmax", [P, 2, 4])
        rowsum = sb("rowsum", [P, 2, 4])
        rscale = sb("rscale", [P, 2, 4])
        stage = sb("stage", [P, 2, GROUP], U32)
        dot16 = sb("dot16", [P, GROUP])
        coef16 = sb("coef16", [P, GROUP])
        eps = sb("eps", [P, 1])
        act_scratch = sb("act_scratch", [P, 1])

        def wk(lo, n, *shape):
            v = work[:, lo:lo + n]
            if len(shape) == 2:
                return v.rearrange("p (a b) -> p a b", a=shape[0])
            if len(shape) == 3:
                return v.rearrange("p (a b c) -> p a b c", a=shape[0], b=shape[1])
            return v

        silu = wk(2 * FC * SEQ, 512, 2, SEQ)
        graw = wk(2 * FC * SEQ + 512, 512, 2, SEQ)
        stg = wk(0, 4096, A_HEADS, 512)
        T = wk(12288, 2048, DC, SEQ)
        QT = wk(0, 2048, DC, SEQ)
        KT = wk(2048, 2048, DC, SEQ)
        V = wk(4096, 2048, TT, D)
        OT = wk(6144, 2048, DC, SEQ)
        LG = wk(8192, 1024, 2, 2, SEQ)
        EX = (wk(9216, 1024, 2, 2, SEQ), wk(12288, 1024, 2, 2, SEQ))
        PR = wk(10240, 1024, 2, 2, SEQ)
        PT = (wk(11264, 1024, 2, 512), wk(13312, 1024, 2, 512))
        DQ = wk(2048, 2048, DC, SEQ)
        DK = wk(4096, 2048, DC, SEQ)
        UP = SEQ + SCK - 1
        VP = SEQ + CFK - 1
        U = wk(0, DC * UP, DC, UP)
        CV = wk(2064, DC * VP, DC, VP)
        C3 = wk(4352, 2048, DC, SEQ)
        MEM = C3
        Z = wk(6400, 2048, DC, SEQ)
        SG = wk(8448, 2048, DC, SEQ)
        CG = wk(10496, 2048, DC, SEQ)
        T0 = wk(12544, 512, 2, SEQ)
        T1 = wk(13056, 512, 2, SEQ)
        ZB = wk(13568, 256)
        S = (wk(0, 2048, 2 * PH, NK), wk(2048, 2048, 2 * PH, NK))
        S2 = wk(4096, 2048, 2 * PH, NK)
        CA = wk(6144, 2048, PH, TK * TK)
        NS = HALF * TK
        QP = wk(8192, 4096, 2 * PH, SEQ)
        at_mr = [0]

        def mr(n, a0=None, dt=None):
            v = mod_ring[:, at_mr[0]:at_mr[0] + n]
            at_mr[0] += n
            if dt is not None:
                v = v.bitcast(dt)
            return v if a0 is None else v.rearrange("p (a b) -> p a b", a=a0)

        gfin = mr(D)
        TV = mr(256, 2 * PH)
        TI = mr(256, 2 * PH, U32)
        TIF = mr(256, 2 * PH)
        FV = mr(128, PH)
        FP = mr(128, PH, U32)
        AI = mr(128, None, U32)
        BI = mr(128, None, U32)
        AF = mr(128)
        BF = mr(128)
        I0 = mr(128)
        I1 = mr(128)
        IDX = mr(256, 2, U32)
        GT = mr(256, 2)
        DOT = mr(256, 2)
        CF = mr(256, 2)
        GS = mr(16)
        YS = mr(4)
        assert at_mr[0] <= 2 * TILE

        ps = ctx.enter_context(nc.psum_tensor("ps", [P, 8, 512], F32))
        ps_norm = ps[:, 4, 0:SEQ]
        ps_mod = ps[:, 7, 0:8]
        ps_direct = ps[:, 6, 0:2 * len(DIRECT)]
        ps_s = (ps[:, 5:7, :], ps[:, 2:5:2, :])
        PT_BANK = (7, 3)
        ps_f = ps[0:B_HEADS, 5, 0:SEQ]
        SUB_BANK = (1, 3, 0, 2)

        bias_rows = nc.dram_tensor("bias_rows", (A_HEADS, P * 512), F32).ap()

        def col(name, k=0, n=1):
            return prm[:, COL[name] + k:COL[name] + k + n]

        def slot(ring_, g, width=None):
            lo = (g % RING) * TILE
            return ring_[:, lo:lo + (TILE_WIDTH[g] if width is None else width)]

        def first_tile(n):
            if n < 4:
                return first[:, n * TILE:(n + 1) * TILE]
            return first_more[:, (n - 4) * TILE:(n - 3) * TILE]

        def f32(ap):
            return ap.bitcast(F32)

        def low_wait(eng, g, i=None):
            e, n = LOW[g]
            eng.wait_ge(low[e], at(i, LOW_STEP[e], n))

        prm_loaded = sem("prm_loaded")
        x_loaded = sem("x_loaded")
        small_loaded = sem("small_loaded")
        sub_loaded = sem("sub_loaded")
        w_loaded = [sem(f"w_loaded{s}") for s in range(RING)]
        hi_ready = sem("hi_ready")
        low = {"v": sem("low_by_vector"), "p": sem("low_by_pool")}
        mod_loaded = [sem(f"mod_loaded{s}") for s in range(2)]
        first_loaded = [sem(f"first_loaded{n}") for n in range(6)]
        rows_written = sem("rows_written")
        bias_loaded = sem("bias_loaded")
        decay_loaded = sem("decay_loaded")
        mem_loaded = sem("mem_loaded")
        gfin_loaded = sem("gfin_loaded")
        out_written = sem("out_written")
        consts_ready = sem("consts_ready")
        pool_step = sem("pool_step")
        vec_consts = sem("vec_consts")
        dve_step = sem("dve_step")
        act_step = sem("act_step")
        c_ready = sem("c_ready")
        acc_ready = sem("acc_ready")
        modsum_ready = sem("modsum_ready")
        direct_ready = sem("direct_ready")
        mods_ready = sem("mods_ready")
        lam_sum_ready = sem("lam_sum_ready")
        lam_exp_ready = sem("lam_exp_ready")
        table_ready = sem("table_ready")
        squares_ready = sem("squares_ready")
        presum_ready = sem("presum_ready")
        sumsq_ready = sem("sumsq_ready")
        root_ready = sem("root_ready")
        t_ready = sem("t_ready")
        hh_ready = sem("hh_ready")
        hl_ready = sem("hl_ready")
        hidden_hi = sem("hidden_hi")
        hidden_lo = sem("hidden_lo")
        eh_ready = sem("eh_ready")
        el_ready = sem("el_ready")
        units_done = sem("units_done")
        freed = {"a": sem("freed_by_scalar"), "d": sem("freed_by_vector")}
        scores_done = sem("scores_done")
        logits_ready = sem("logits_ready")
        exp_ready = sem("exp_ready")
        probs_ready = sem("probs_ready")
        turned = sem("turned")
        probsT_ready = sem("probsT_ready")
        pv_done = sem("pv_done")
        attn_ready = sem("attn_ready")
        sub_sq = sem("sub_sq")
        sub_sum = sem("sub_sum")
        sub_root = sem("sub_root")
        sub_done = sem("sub_done")
        fz_done = sem("fz_done")
        fz_ln = sem("fz_ln")
        f_ready = sem("f_ready")
        decay_cleared = sem("decay_cleared")
        conv_done = sem("conv_done")
        mean_sum = sem("mean_sum")
        mean_ready = sem("mean_ready")
        centred = sem("centred")
        ln_sq = sem("ln_sq")
        ln_sum = sem("ln_sum")
        ln_root = sem("ln_root")
        ln_scaled = sem("ln_scaled")
        ln_ready = sem("ln_ready")
        tok_turned = sem("tok_turned")
        tok_ready = sem("tok_ready")
        sub_scores = sem("sub_scores")
        s_ready = sem("s_ready")
        gate_diff = sem("gate_diff")
        gate_exp = sem("gate_exp")
        idx_ready = sem("idx_ready")
        dots_ready = sem("dots_ready")
        gelu_ready = sem("gelu_ready")
        staged = sem("staged")
        row_loaded = [sem(f"row_loaded{s}") for s in range(GROUP)]
        rows_free = sem("rows_free")
        rows_asked = sem("rows_asked")
        y_ready = sem("y_ready")
        yroot_ready = sem("yroot_ready")
        yo_ready = sem("yo_ready")

        block = ctx.enter_context(nc.Block())

        @block.sync
        def _(sp):
            sp.dma_start(table[0:NB, :], a["rel_bias"]).then_inc(small_loaded, 16)
            sp.dma_start(onehot[:, :], a["onehot"]).then_inc(small_loaded, 16)
            sp.dma_start(lamp[:, :], a["a_lambda"].partition_broadcast(P).rearrange("q a n -> q (a n)")).then_inc(small_loaded, 16)
            sp.dma_start(fgate_b[:, :], a["fgate_b"]).then_inc(small_loaded, 16)
            sp.dma_start(prm[:, :], a["prm"]).then_inc(prm_loaded, 16)
            sp.dma_start(X[:, :, :], a["xT"]).then_inc(x_loaded, 16)
            sp.dma_start(subk[:, :, :], a["subkT"]).then_inc(sub_loaded, 16)
            sp.wait_ge(acc_ready, 1)

            def tiles(name, t0=0, n=None, i=None):
                ln = LIN[name]
                for t in range(t0, t0 + (ln.tiles if n is None else n)):
                    g = ln.tile0 + t
                    if g >= RING:
                        low_wait(sp, g - RING, i)
                    src = a[name][t] if i is None else a[name][bass.ds(i * BODY + t, 1)].rearrange("a p f -> (a p) f")
                    sp.dma_start(slot(raw, g), src).then_inc(w_loaded[g % RING], 16)

            def ffn(w_in, w_out):
                tiles(w_in, 0, RING)
                with sp.Fori(0, 3) as i:
                    tiles(w_in, RING, BODY, i)
                tiles(w_in, 21, 1)
                tiles(w_out)

            ffn("f00_in", "f00_out")
            for name in ("a_q", "a_k", "a_v", "a_o"):
                tiles(name)
            ffn("f01_in", "f01_out")
            tiles("s_k")
            tiles("s_v")
            ffn("f10_in", "f10_out")
            tiles("b_q")
            sp.wait_ge(f_ready, 1)
            sp.wait_ge(decay_cleared, 4)
            for odd in range(2):
                sp.dma_start(DQ[64 * odd:64 * odd + 1, :, :], f_sum[odd:B_HEADS:2, :]).then_inc(decay_loaded, 16)
                sp.dma_start(DK[64 * odd + 1:64 * odd + 2, :, :], f_neg[odd:B_HEADS:2, :]).then_inc(decay_loaded, 16)
            tiles("b_o")
            ffn("f11_in", "f11_out")
            for name in ("mix_a", "mix_g", "mix_b", "sc_out"):
                tiles(name)
            sp.wait_ge(el_ready, ESET["c3"] + DC)
            sp.dma_start(MEM, a["memT"]).then_inc(mem_loaded, 16)
            for name in ("cf_out", "mix_out"):
                tiles(name)
            for name in ("x_k", "x_v", "x_q", "x_o", "pq"):
                tiles(name)
            sp.dma_start(gfin, a["final_norm_g"].partition_broadcast(P).rearrange("q a n -> q (a n)")).then_inc(gfin_loaded, 16)
            for t in range(TT):
                sp.wait_ge(yo_ready, t + 1)
                sp.dma_start(out[t], YO[:, t, :]).then_inc(out_written, 16)
            sp.wait_ge(out_written, 16 * TT)

        @block.gpsimd
        def _(pool):
            step = Chain(pool, pool_step)
            step(nc.gpsimd.memset(ident[:, :], 0.0))
            nc.gpsimd.affine_select(out=ident[:, :], in_=ident[:, :], compare_op=ALU.not_equal, fill=1.0, base=0,
                                    pattern=[[-1, P]], channel_multiplier=1).then_inc(consts_ready, 1)
            step(nc.gpsimd.memset(mask[:, :], 0.0))
            nc.gpsimd.affine_select(out=mask[:, :], in_=mask[:, :], compare_op=ALU.is_ge, fill=NEG, base=P,
                                    pattern=[[-1, SEQ]], channel_multiplier=1).then_inc(consts_ready, 1)
            nc.gpsimd.iota(iota16[:, :], pattern=[[1, TK]], base=0, channel_multiplier=0,
                           allow_small_or_imprecise_dtypes=True).then_inc(consts_ready, 1)

            def split(g, i=None):
                if g < N_TILES and LOW[g][0] == "p":
                    pool.wait_ge(hi_ready, at(i, BODY, g + 1))
                    nc.gpsimd.tensor_tensor(slot(w_lo, g), slot(raw, g), f32(slot(w_hi, g)), ALU.subtract
                                            ).then_inc(low["p"], 1)

            def splits(name):
                ln = LIN[name]
                for g in range(ln.tile0, ln.tile0 + ln.tiles):
                    split(g)

            def lows(name, src):
                for k in range(DC):
                    pool.wait_ge(hh_ready, SET[name] + k + 1)
                    nc.gpsimd.tensor_tensor(HL[:, k, :], src[:, k, :], f32(HH[:, k, :]), ALU.subtract
                                            ).then_inc(hl_ready, 1)

            def second_lows(name, src):
                for k in range(DC):
                    pool.wait_ge(eh_ready, ESET[name] + k + 1)
                    nc.gpsimd.tensor_tensor(EL[:, k, :], src[:, k, :], f32(EH[:, k, :]), ALU.subtract
                                            ).then_inc(el_ready, 1)

            def presum(n, k):
                if 0 < k < PRE:
                    pool.wait_ge(squares_ready, 8 * RANK[n] + k + 1)
                    ins = nc.gpsimd.tensor_tensor(SQ[:, 0, :], SQ[:, 0, :], SQ[:, k, :], ALU.add)
                    if k < PRE - 1:
                        step(ins)
                    else:
                        ins.then_inc(presum_ready, 1)

            def presums(n):
                for k in range(PRE):
                    presum(n, k)

            def hidden(n, w_in, w_out, nxt):
                def one(j, i=None):
                    split(LIN[w_in].tile0 + j + 2, i)
                    pool.wait_ge(hidden_hi, at(i, BODY, FC * n + j + 1))
                    if i is None:
                        lo, hi = GUL[:, j, :], GUH[:, j, :]
                    else:
                        lo, hi = (g_[:, bass.ds(i * BODY + j, 1), :].rearrange("p a n -> p (a n)") for g_ in (GUL, GUH))
                    nc.gpsimd.tensor_tensor(lo, graw[:, j % 2, :], f32(hi), ALU.subtract).then_inc(hidden_lo, 1)

                with pool.Fori(0, 3) as i:
                    for j in range(BODY):
                        one(j, i)
                for j in range(3 * BODY, FC):
                    one(j)
                for m in range(DC):
                    split(LIN[w_out].tile0 + 2 * m + 2)
                    split(LIN[w_out].tile0 + 2 * m + 3)
                    presum(nxt, m - 1)

            pool.sem_inc(hidden_lo, 2)
            hidden(0, "f00_in", "f00_out", 1)
            lows("attA", OT)
            presums(2)
            hidden(1, "f01_in", "f01_out", 3)
            hidden(2, "f10_in", "f10_out", 5)
            pool.wait_ge(units_done, LIN["f10_out"].unit_end)
            pool.wait_ge(presum_ready, PRESUM[5])
            for n, tile_ in enumerate((DQ, DK)):
                for odd in range(2):
                    nc.gpsimd.memset(tile_[64 * odd:64 * odd + 2, :, :], 1.0).then_inc(decay_cleared, 1)
                    pool.wait_ge(decay_cleared, 2 * n + odd + 1)
            lows("attB", OT)
            presums(6)
            hidden(3, "f11_in", "f11_out", N_FINAL)
            lows("n8", T)
            for name in ("mix_a", "mix_g", "mix_b"):
                splits(name)
            second_lows("c3", C3)
            lows("cf", Z)
            second_lows("merged", SG)
            lows("n9", T)
            presums(N_XA)
            second_lows("n10", T)
            lows("attX", OT)
            presums(N_PEER)
            lows("n11", T)
            splits("pq")
            pool.wait_ge(units_done, LIN["pq"].unit_end)

            def gather(t, part, first, pairs):
                rows = (a["peer_u"], a["peer_v"])[part]
                seg = 2 * t + part
                with pool.Fori(0, pairs) as i:
                    for g in range(2):
                        group = seg * N_GROUPS + first + g
                        lo = i * (2 * GROUP) + (first + g) * GROUP
                        nc.gpsimd.tensor_copy(stage[:, g, :], IDX[:, t, bass.ds(lo, GROUP)]).then_inc(staged, 1)
                        pool.wait_ge(staged, i * 2 + (group + 1))
                        for j in range(GROUP):
                            if j % 4 == 0:
                                pool.wait_ge(rows_free, i * (2 * GROUP) + (group * GROUP + j + 4))
                                pool.sem_inc(rows_asked, 1)
                            pool.indirect_dma_start(
                                out=rows_ring[:, j * D:(j + 1) * D], out_offset=None, in_=rows,
                                in_offset=bass.IndirectOffsetOnAxis(ap=stage[:, g, j:j + 1], axis=0),
                            ).then_inc(row_loaded[j], 16)

            for t in range(TT):
                for half in range(2):
                    pool.wait_ge(idx_ready, 2 * t + half + 1)
                    gather(t, 0, half * N_GROUPS // 2, N_GROUPS // 4)
                gather(t, 1, 0, N_GROUPS // 2)

        @block.tensor
        def _(pe):
            mm, turn = nc.tensor.matmul, nc.tensor.transpose

            def freed_wait(q, i):
                if i is None:
                    e, n = FREE[q - BANKS]
                    pe.wait_ge(freed[e], n)
                    return
                e, n = FREE[q - BANKS + 2 * BODY]
                pe.wait_ge(freed[e], i * BODY + (n - BODY))

            def product(out_, whole, split, k0, k1, first, last, left=False):
                for k in range(k0, k1):
                    for n, (u, v_) in enumerate(((0, 0), (0, 1), (1, 0))):
                        ops = (whole(u, k), split(v_, k))
                        ins = mm(out_, ops[1] if left else ops[0], ops[0] if left else ops[1],
                                 start=(first and k == k0 and n == 0), stop=(last and k == k1 - 1 and n == 2))
                return ins

            def tile_wait(g, i=None):
                low_wait(pe, g, i)

            def wparts(g):
                k = DC if TILE_WIDTH[g] == TILE else WO_K
                return [slot(r, g).rearrange("p (k n) -> p k n", k=k) for r in (w_hi, w_lo)]

            def feat_tile(name, t, i=None, mid=None, new=None):
                ln = LIN[name]
                g = ln.tile0 + t
                tile_wait(g, i)
                w = wparts(g)
                second = name in ("sc_out", "mix_out", "x_q")
                src = (EH, EL) if second else (HH, HL)
                if new is not None and t == 0:
                    hi_sem, lo_sem, n0 = (eh_ready, el_ready, ESET[new]) if second else (hh_ready, hl_ready, SET[new])
                    for part in range(2):
                        for m in range(2):
                            q = ln.chunk0 + m
                            if part == 0:
                                freed_wait(q, i)
                            for k in range(DC):
                                if m == 0:
                                    pe.wait_ge((hi_sem, lo_sem)[part], n0 + k + 1)
                                for u in range(2 - part):
                                    last = mm(ps[:, q % BANKS, 0:SEQ], w[u][:, k, m * P:(m + 1) * P], src[part][:, k, :],
                                              start=(part == 0 and k == 0 and u == 0), stop=(part == 1 and k == DC - 1))
                            if part == 1:
                                last.then_inc(units_done, 1)
                    return
                for m in range(2):
                    q = ln.chunk0 + 2 * t + m
                    freed_wait(q, i)
                    if m == 1 and mid is not None:
                        mid()
                    o = ps[:, q % BANKS, 0:SEQ]
                    wk_ = lambda u, k: w[u][:, k, m * P:(m + 1) * P]
                    xk_ = lambda u, k: src[u][:, k, :]
                    last = product(o, wk_, xk_, 0, DC, True, True)
                    last.then_inc(units_done, 1)

            def tok_tile(name, t, mid=None):
                ln = LIN[name]
                g = ln.tile0 + t
                tile_wait(g)
                w = wparts(g)
                for m in range(TT):
                    q = ln.chunk0 + TT * t + m
                    freed_wait(q, None)
                    if m == 1 and mid is not None:
                        mid()
                    product(ps[:, q % BANKS, 0:2 * P], lambda u, k: w[u][:, k, :],
                            lambda u, k: (HH, HL)[u][:, k, m * P:(m + 1) * P], 0, DC, True, True, left=True
                            ).then_inc(units_done, 1)

            def mod_sum(n, i=None):
                pe.wait_ge(acc_ready, at(i, 4, summed(n)))
                if n >= 1:
                    pe.wait_ge(mods_ready, at(i, 4, summed(n) - 1))
                for m in range(2):
                    last = mm(ps_mod[:, m:m + 1], mod_acc[:, n % 2, 0, m * P:(m + 1) * P], ones[:, 0:1],
                              start=True, stop=True)
                last.then_inc(modsum_ready, 1)

            def norm_sum(n, ks=range(DC)):
                for k in ks:
                    if n in PRESUM and 0 < k < PRE:
                        continue
                    if n in PRESUM and k == 0:
                        pe.wait_ge(presum_ready, PRESUM[n])
                    pe.wait_ge(squares_ready, 8 * RANK[n] + k + 1)
                    last = mm(ps_norm, ones[:, :], SQ[:, k, :], start=(k == 0), stop=(k == DC - 1))
                    if k == DC - 1:
                        last.then_inc(sumsq_ready, 1)

            def ffn(f, w_in, w_out, new, nxt, ada):
                ln = LIN[w_in]
                more = ada is not None
                pe.wait_ge(freed["a"], FREE[ln.chunk0][1] - 1)
                pe.wait_ge(freed["d"], FREE[ln.chunk0 + 1][1] - 1)
                with pe.Fori(0, 3) as i:
                    for t in range(BODY):
                        n = {1: 0, 2: 1, 4: 2, 5: 3}.get(t)
                        feat_tile(w_in, t, i=i, new=new, mid=(lambda: mod_sum(ada + n, i)) if more and n is not None else None)
                for t in range(18, 22):
                    n = {19: 12, 20: 13}.get(t)
                    feat_tile(w_in, t, mid=(lambda: mod_sum(ada + n)) if more and n is not None else None)
                lo = LIN[w_out]
                for t in range(16):
                    g = lo.tile0 + t
                    tile_wait(g)
                    m, half = t // 2, t % 2
                    q = lo.chunk0 + m
                    if half == 0:
                        freed_wait(q, None)
                    if m == 0:
                        pe.wait_ge(hidden_lo, 2 + FC * f + WO_K * (half + 1))
                    w = wparts(g)
                    product(ps[:, q % BANKS, 0:SEQ], lambda u, k: w[u][:, k - WO_K * half, :],
                            lambda u, k: (GUH, GUL)[u][:, k, :], WO_K * half, WO_K * (half + 1), half == 0, half == 1
                            ).then_inc(units_done, 1)
                    if more and half == 0 and 1 <= m <= 5:
                        mod_sum(ada + 14 + m - 1)
                norm_sum(nxt)
                if more:
                    pe.wait_ge(root_ready, RANK[nxt] + 1)
                    mod_sum(ada + 19)

            def residual(name, new, nxt):
                for t in range(4):
                    feat_tile(name, t, new=new)
                norm_sum(nxt)

            def attention(kind):
                s0, s1 = STEP0[kind], STEP_END[kind]
                kt = KS if kind == "B" else KT
                v = VS if kind == "B" else V
                hw = {"A": 128, "B": 64, "X": 256}[kind]

                def scores(s):
                    c = s - s0
                    for qt in range(TT):
                        u = 2 * s + qt
                        if s and kind == "X" and s > s0:
                            pe.wait_ge(exp_ready, u - 1)
                        elif s:
                            pe.wait_ge(logits_ready, u - 1)
                        nk = SEQ if kind == "X" or qt == 1 else P
                        for m in range(2):
                            o = ps_s[qt][:, m, 0:nk]
                            if kind == "X":
                                for e in range(2):
                                    cc = 4 * c + 2 * m + e
                                    last = mm(o, QT[:, cc, qt * P:(qt + 1) * P], kt[:, cc, 0:nk],
                                              start=(e == 0), stop=(e == 1))
                            else:
                                r = slice(64 * m, 64 * m + 64)
                                last = mm(o, QT[r, c, qt * P:(qt + 1) * P], kt[r, c, 0:nk],
                                          start=True, stop=(kind == "A"))
                                if kind == "B":
                                    r = slice(64 * m, 64 * m + 2)
                                    last = mm(o, DQ[r, c, qt * P:(qt + 1) * P], DK[r, c, 0:nk], start=False, stop=True)
                        last.then_inc(scores_done, 1)

                def turn_probs(s):
                    pe.wait_ge(probs_ready, 2 * s + 2)
                    if s:
                        pe.wait_ge(probsT_ready, s)
                    for m in range(1 if kind == "A" else 2):
                        bank = PT_BANK[m]
                        blocks = [(0, 0), (0, 1), (1, 1)] if kind != "X" else [(0, 0), (0, 1), (1, 0), (1, 1)]
                        for b, (k, qt) in enumerate(blocks):
                            last = turn(ps[:, bank, b * P:(b + 1) * P], PR[:, qt, m, k * P:(k + 1) * P], ident[:, :])
                    last.then_inc(turned, 1)

                def values(s):
                    c = s - s0
                    pe.wait_ge(probsT_ready, s + 1)
                    if s:
                        pe.wait_ge(attn_ready, s)
                    if kind == "X":
                        for m in range(2):
                            for e in range(2):
                                f = (2 * c + m) * hw + e * P
                                for k in range(2):
                                    last = mm(ps[:, m, e * SEQ:(e + 1) * SEQ], v[:, k, f:f + P],
                                              PT[s % 2][:, m, k * SEQ:(k + 1) * SEQ], start=(k == 0), stop=(k == 1))
                    else:
                        for m in range(1 if kind == "A" else 2):
                            f = c * P + m * hw
                            rows = slice(m * hw, m * hw + hw)
                            mm(ps[rows, 0, 0:SEQ], v[:, 0, f:f + hw], PT[s % 2][:, m, 0:SEQ], start=True, stop=False)
                            last = mm(ps[rows, 0, P:SEQ], v[:, 1, f:f + hw], PT[s % 2][:, m, SEQ:SEQ + P],
                                      start=False, stop=True)
                    last.then_inc(pv_done, 1)

                scores(s0)
                scores(s0 + 1)
                for s in range(s0, s1):
                    if s + 2 < s1:
                        scores(s + 2)
                    turn_probs(s)
                    if s > s0:
                        values(s - 1)
                values(s1 - 1)

            pe.wait_ge(vec_consts, 1)
            pe.wait_ge(consts_ready, 3)
            pe.wait_ge(table_ready, 1)
            for h in range(A_HEADS):
                if h >= BANKS:
                    freed_wait(h, None)
                mm(ps[:, h % BANKS, :], table_rep[:, h, :], onehot, start=True, stop=True).then_inc(units_done, 1)
            norm_sum(0)
            pe.wait_ge(c_ready, 1)
            for n in DIRECT:
                if n < 6:
                    pe.wait_ge(first_loaded[n], 16)
                    w = first_tile(n)
                else:
                    pe.wait_ge(mod_loaded[n % 2], 16)
                    w = mod_ring[:, (n % 2) * TILE:(n % 2 + 1) * TILE]
                w = w.rearrange("p (k n) -> p k n", k=DC)
                for m in range(2):
                    c0 = 2 * (n - DIRECT[0]) + m
                    for k in range(DC):
                        last = mm(ps_direct[:, c0:c0 + 1], w[:, k, m * P:(m + 1) * P], c_act[:, k:k + 1],
                                  start=(k == 0), stop=(k == DC - 1))
                if n == DIRECT[-1]:
                    last.then_inc(direct_ready, 1)
                for k in range(2 * (n - DIRECT[0]), min(2 * (n - DIRECT[0]) + 2, DIRECT[0])):
                    mod_sum(k)
            ffn(0, "f00_in", "f00_out", "n0", 1, 8)

            for t in range(4):
                feat_tile("a_q", t, new="n1", mid=(lambda: mod_sum(28 + t - 1)) if t else None)
            for t in range(4):
                feat_tile("a_k", t, mid=lambda: mod_sum(31 + t))
            for t in range(4):
                tok_tile("a_v", t, mid=(lambda: mod_sum(35)) if t == 0 else None)
            pe.wait_ge(freed["a"], LIN["a_v"].freed_a)
            pe.wait_ge(freed["d"], LIN["a_v"].freed_d)
            attention("A")
            pe.wait_ge(attn_ready, STEP_END["A"])
            for b in range(4):
                pe.wait_ge(sub_sq, b + 1)
                mm(ps[:, SUB_BANK[b], :], ones[:, :], SQ[:, 2 * b:2 * b + 2, :], start=True, stop=True
                   ).then_inc(sub_sum, 1)
            pe.wait_ge(sub_root, 4)
            residual("a_o", "attA", 2)

            ffn(1, "f01_in", "f01_out", "n2", 3, 36)
            for t in range(4):
                feat_tile("s_k", t, new="n3")
            for t in range(4):
                tok_tile("s_v", t)
            fw = col("fgate_w", 0, DC * B_HEADS).rearrange("p (k n) -> p k n", k=DC)
            for k in range(DC):
                for n, part in enumerate((HH, HL)):
                    last = mm(ps_f, fw[:, k, :], f32(part[:, k, :]), start=(k == 0 and n == 0),
                              stop=(k == DC - 1 and n == 1))
            last.then_inc(fz_done, 1)

            ffn(2, "f10_in", "f10_out", "n4", 5, 56)
            for t in range(4):
                feat_tile("b_q", t, new="n5", mid=(lambda: mod_sum(76 + t - 1)) if t else None)
            mod_sum(79)
            pe.wait_ge(freed["a"], LIN["b_q"].freed_a)
            pe.wait_ge(mods_ready, summed(ADA_TILES - 1))
            pe.wait_ge(decay_loaded, 64)
            attention("B")
            pe.wait_ge(attn_ready, STEP_END["B"])
            residual("b_o", "attB", 6)
            ffn(3, "f11_in", "f11_out", "n6", N_FINAL, None)

            norm_sum(N_MIX)
            for t in range(16):
                feat_tile("mix_a", t, new="n8")
            for t in range(8):
                feat_tile("mix_g", t)
            for t in range(4):
                feat_tile("mix_b", t)
                if t == 0:
                    for k in range(DC):
                        pe.wait_ge(conv_done, k + 1)
                        last = mm(ps_norm, ones[:, :], Z[:, k, :], start=(k == 0), stop=(k == DC - 1))
                    last.then_inc(mean_sum, 1)
            for k in range(DC):
                pe.wait_ge(ln_sq, k + 1)
                last = mm(ps_norm, ones[:, :], SQ[:, k, :], start=(k == 0), stop=(k == DC - 1))
            last.then_inc(ln_sum, 1)
            for t in range(4):
                feat_tile("sc_out", t, new="c3")
            for t in range(4):
                feat_tile("cf_out", t, new="cf")
            norm_sum(N_MEM)
            residual("mix_out", "merged", N_XA)

            for t in range(4):
                feat_tile("x_k", t, new="n9")
            for t in range(4):
                tok_tile("x_v", t)
            for t in range(4):
                feat_tile("x_q", t, new="n10")
            pe.wait_ge(freed["a"], LIN["x_q"].freed_a)
            pe.wait_ge(freed["d"], LIN["x_v"].freed_d)
            attention("X")
            pe.wait_ge(attn_ready, STEP_END["X"])
            residual("x_o", "attX", N_PEER)

            def head_scores(h):
                pe.wait_ge(freed["a"], FREE[LIN["pq"].chunk0 + 2 * h + 1][1])
                for t in range(TT):
                    if h >= 2:
                        pe.wait_ge(s_ready, 2 * (h - 2) + t + 1)
                    if h == 0 and t == 0:
                        pe.wait_ge(sub_loaded, 16)
                    for p_ in range(2):
                        last = mm(ps[:, 3 + 2 * (h % 2) + t, p_ * NK:(p_ + 1) * NK], QP[:, 2 * h + p_, t * P:(t + 1) * P],
                                  subk[:, p_, :], start=True, stop=True)
                    last.then_inc(sub_scores, 1)

            for t in range(8):
                feat_tile("pq", t, new="n11", mid=(lambda: head_scores(t - 1)) if t else None)
            head_scores(7)
            for b in range(8):
                src, t, half = (T, X)[b // 4], (b // 2) % 2, b % 2
                if b >= 2:
                    pe.wait_ge(tok_ready, b - 1)
                for c in range(4):
                    last = turn(ps[:, b % 2, c * P:(c + 1) * P], src[:, 4 * half + c, t * P:(t + 1) * P], ident[:, :])
                last.then_inc(tok_turned, 1)

        @block.scalar
        def _(act):
            step = Chain(act, act_step)
            f = nc.scalar.activation

            def split(g, i=None):
                if g >= N_TILES:
                    return
                act.wait_ge(w_loaded[g % RING], at(i, 16 * BODY // RING, 16 * (g // RING + 1)))
                if g >= RING:
                    act.wait_ge(units_done, at(i, 2 * BODY, TILE_UNIT[g - RING]))
                f(slot(w_hi, g), slot(raw, g), ACT.Copy).then_inc(hi_ready, 1)

            def preload(func):
                f(act_scratch[:, :], eps[:, :], func)

            def load_mod(n, i=None):
                act.wait_ge(acc_ready, at(i, 4, summed(n - 2)))
                src = a["ada"][n] if i is None else a["ada"][bass.ds(i * 4 + n, 1)].rearrange("a p f -> (a p) f")
                act.dma_start(mod_ring[:, (n % 2) * TILE:(n % 2 + 1) * TILE], src).then_inc(mod_loaded[n % 2], 16)

            def square(n, k, ready=None):
                if ready is not None:
                    act.wait_ge(freed["d"], ready)
                f(SQ[:, k, :], X[:, k, :], ACT.Square).then_inc(squares_ready, 1)

            def residual(name, nxt):
                ln = LIN[name]
                preload(ACT.Sqrt)
                for t in range(4):
                    split(ln.tile0 + t + 2)
                    if nxt is not None and t:
                        for k in (2 * t - 2, 2 * t - 1):
                            square(nxt, k, FREE[ln.chunk0 + k][1])
                if nxt is not None:
                    for k in (6, 7):
                        square(nxt, k, FREE[ln.chunk0 + k][1])

            def norm_root(n):
                act.wait_ge(sumsq_ready, RANK[n] + 1)
                f(root[:, :], ps_norm, ACT.Sqrt, scale=1.0 / D, bias=eps[:, :]).then_inc(root_ready, 1)

            def shift_high(name, n):
                m0 = NORMS[n][1]
                for k in range(DC):
                    act.wait_ge(t_ready, 8 * n + k + 1)
                    f(HH[:, k, :], T[:, k, :], ACT.Identity, bias=mods[:, m0 + k:m0 + k + 1]).then_inc(hh_ready, 1)

            def norm_high(n, second=False):
                for k in range(DC):
                    act.wait_ge(t_ready, 8 * n + k + 1)
                    if second:
                        f(EH[:, k, :], T[:, k, :], ACT.Copy).then_inc(eh_ready, 1)
                    else:
                        f(HH[:, k, :], T[:, k, :], ACT.Copy).then_inc(hh_ready, 1)

            def take(name, q, dst, func=ACT.Copy, **kw):
                q = LIN[name].chunk0 + q
                act.wait_ge(units_done, CHUNK_UNIT[q])
                assert FREE[q][0] == "a"
                f(dst, ps[:, q % BANKS, 0:SEQ], func, **kw).then_inc(freed["a"], 1)

            def ffn(n, w_in, w_out, nxt, ada):
                ln = LIN[w_in]
                more = ada is not None

                def slot_(t, i=None):
                    if more and t in (1, 2, 4, 5, 19, 20):
                        k = {1: 0, 2: 1, 4: 2, 5: 3, 19: 12, 20: 13}[t]
                        load_mod(ada + k + 2, i)
                    q = ln.chunk0 + 2 * t
                    act.wait_ge(units_done, at(i, 2 * BODY, CHUNK_UNIT[q]))
                    act.wait_ge(freed["d"], at(i, BODY, FREE[q + 1][1] - 2))
                    f(silu[:, t % 2, :], ps[:, q % BANKS, 0:SEQ], ACT.Silu).then_inc(freed["a"], 1)
                    act.wait_ge(freed["d"], at(i, BODY, FREE[q + 1][1]))
                    dst = GUH[:, t, :] if i is None else GUH[:, bass.ds(i * BODY + t, 1), :].rearrange("p a n -> p (a n)")
                    f(dst, graw[:, t % 2, :], ACT.Copy).then_inc(hidden_hi, 1)
                    split(ln.tile0 + t + 3, i)

                split(ln.tile0 + 2)
                with act.Fori(0, 3) as i:
                    for t in range(BODY):
                        slot_(t, i)
                for t in range(18, 22):
                    slot_(t)
                preload(ACT.Sqrt)
                lo = LIN[w_out]
                for m in range(DC):
                    if m:
                        split(lo.tile0 + 2 * m + 2)
                    if more and 1 <= m <= 6 and ada + 14 + m + 1 < ADA_TILES:
                        load_mod(ada + 14 + m + 1)
                    split(lo.tile0 + 2 * m + 3)
                    if m:
                        square(nxt, m - 1, FREE[lo.chunk0 + m - 1][1])
                square(nxt, 7, FREE[lo.chunk0 + 7][1])

            def exps(s):
                par = s % 2
                kind = STEPS[s][0]
                for qt in range(TT):
                    act.wait_ge(logits_ready, 2 * s + qt + 1)
                    if s >= 2:
                        act.wait_ge(probs_ready, 2 * s + qt - 3)
                    nk = SEQ if kind == "X" or qt == 1 else P
                    for m in range(2):
                        b = 2 * qt + m
                        src, sign = (ps_s[qt][:, m, 0:nk], 1.0) if kind == "X" else (LG[:, qt, m, 0:nk], -1.0)
                        last = f(EX[par][:, qt, m, 0:nk], src, ACT.Exp, bias=nmax[:, par, b:b + 1], scale=sign,
                                 accum_out=rowsum[:, par, b:b + 1])
                    last.then_inc(exp_ready, 1)

            def attention(kind):
                s0, s1 = STEP0[kind], STEP_END[kind]
                def output(s):
                    c = s - s0
                    act.wait_ge(pv_done, s + 1)
                    if kind == "X":
                        f(OT[:, 4 * c:4 * c + 4, :].rearrange("p (a b) n -> p a (b n)", a=2), ps[:, 0:2, :],
                          ACT.Copy).then_inc(attn_ready, 1)
                    else:
                        f(OT[:, c, :], ps[:, 0, 0:SEQ], ACT.Copy).then_inc(attn_ready, 1)
                    if kind != "A" or c % 2:
                        act.wait_ge(attn_ready, s + 1)
                    if kind == "X":
                        for k in range(4 * c, 4 * c + 4):
                            f(HH[:, k, :], OT[:, k, :], ACT.Copy).then_inc(hh_ready, 1)
                    elif kind == "B":
                        f(HH[:, c, :], OT[:, c, :], ACT.Copy).then_inc(hh_ready, 1)
                    elif c % 2:
                        f(SQ[:, c - 1:c + 1, :], OT[:, c - 1:c + 1, :], ACT.Square).then_inc(sub_sq, 1)

                exps(s0)
                for s in range(s0, s1):
                    if s + 1 < s1:
                        exps(s + 1)
                    act.wait_ge(turned, s + 1)
                    if s >= 2:
                        act.wait_ge(pv_done, s - 1)
                    n = 512 if kind == "X" else 384
                    for m in range(1 if kind == "A" else 2):
                        last = f(PT[s % 2][:, m, 0:n], ps[:, PT_BANK[m], 0:n], ACT.Copy)
                    last.then_inc(probsT_ready, 1)
                    if s > s0:
                        output(s - 1)
                output(s1 - 1)

            act.wait_ge(prm_loaded, 16)
            for n in (0, 5, 1, 2, 6, 3, 7, 4):
                if n < 6:
                    act.dma_start(first_tile(n), a["ada"][n]).then_inc(first_loaded[n], 16)
                else:
                    act.dma_start(mod_ring[:, (n % 2) * TILE:(n % 2 + 1) * TILE], a["ada"][n]).then_inc(mod_loaded[n % 2], 16)
            act.wait_ge(vec_consts, 1)
            f(c_act[:, :], col("c", 0, DC), ACT.Silu).then_inc(c_ready, 1)
            act.wait_ge(lam_sum_ready, 1)
            f(lam_exp[:, :], lam_sum[:, :], ACT.Exp).then_inc(lam_exp_ready, 1)
            for h in (0, 2, 4, 5, 6, 7):
                act.wait_ge(units_done, h + 1)
                f(stg[:, h, :], ps[:, h % BANKS, :], ACT.Copy).then_inc(freed["a"], 1)
            act.wait_ge(x_loaded, 16)
            for k in range(DC):
                square(0, k)
            norm_root(0)
            act.wait_ge(freed["a"], 6)
            act.wait_ge(freed["d"], 2)
            act.dma_start(bias_rows.rearrange("h (p j) -> p h j", p=P), stg).then_inc(rows_written, 16)
            split(0)
            split(1)
            act.wait_ge(direct_ready, 1)
            load_mod(8)
            load_mod(9)
            act.wait_ge(rows_written, 16)
            act.dma_start(bias, bias_rows[:, 0:P * 511].rearrange("h (p x) -> p h x", p=P)[:, :, 127:127 + SEQ]
                          ).then_inc(bias_loaded, 16)
            shift_high("n0", 0)
            ffn(0, "f00_in", "f00_out", 1, 8)

            norm_root(1)
            shift_high("n1", 1)
            for t in range(4):
                split(LIN["a_q"].tile0 + t + 2)
                if t:
                    load_mod(28 + t + 1)
                for m in range(2):
                    q = 2 * t + m
                    take("a_q", q, QT[:, q, :], scale=HD ** -0.5)
            for t in range(4):
                split(LIN["a_k"].tile0 + t + 2)
                load_mod(32 + t + 1)
            for t in range(4):
                split(LIN["a_v"].tile0 + t + 2)
                if t == 0:
                    load_mod(37)
                take("a_v", 2 * t, V[:, 0, t * 256:(t + 1) * 256])
            attention("A")
            for b in range(4):
                act.wait_ge(sub_sum, b + 1)
                f(T[:, 2 * b:2 * b + 2, :].rearrange("p a n -> p (a n)"), ps[:, SUB_BANK[b], :], ACT.Sqrt, scale=1.0 / P,
                  bias=eps[:, :]).then_inc(sub_root, 1)
            for c in range(DC):
                act.wait_ge(sub_done, c // 2 + 1)
                f(HH[:, c, :], OT[:, c, :], ACT.Copy).then_inc(hh_ready, 1)
            residual("a_o", 2)

            norm_root(2)
            shift_high("n2", 2)
            ffn(1, "f01_in", "f01_out", 3, 36)
            norm_root(3)
            shift_high("n3", 3)
            for t in range(4):
                split(LIN["s_k"].tile0 + t + 2)
            for t in range(4):
                split(LIN["s_v"].tile0 + t + 2)
                take("s_v", 2 * t, VS[:, 0, t * 256:(t + 1) * 256])
            act.wait_ge(fz_done, 1)
            shift_high("n4", 4)
            act.wait_ge(fz_done, 1)
            step(f(f_z, ps_f, ACT.Identity, bias=fgate_b[:, :]))
            step(f(f_t, f_z, ACT.Abs))
            step(f(f_t, f_t, ACT.Exp, scale=-1.0))
            f(f_t, f_t, ACT.Ln, bias=1.0).then_inc(fz_ln, 1)
            ffn(2, "f10_in", "f10_out", 5, 56)
            norm_root(5)
            shift_high("n5", 5)
            for t in range(4):
                split(LIN["b_q"].tile0 + t + 2)
                if t in (1, 2):
                    load_mod(76 + t + 1)
                for m in range(2):
                    q = 2 * t + m
                    take("b_q", q, QT[:, q, :], scale=HD ** -0.5)
            attention("B")
            residual("b_o", 6)
            norm_root(6)
            shift_high("n6", 6)
            ffn(3, "f11_in", "f11_out", N_FINAL, None)
            norm_root(N_FINAL)

            for k in range(DC):
                act.wait_ge(t_ready, 8 * N_FINAL + k + 1)
                square(N_MIX, k)
            norm_root(N_MIX)
            norm_high(N_MIX)
            for c in range(DC):
                split(LIN["mix_a"].tile0 + 2 * c + 2)
                if c >= 2:
                    act.wait_ge(freed["d"], FREE[LIN["mix_a"].chunk0 + 4 * (c - 2) + 3][1])
                take("mix_a", 4 * c, T0[:, c % 2, :])
                split(LIN["mix_a"].tile0 + 2 * c + 3)
                take("mix_a", 4 * c + 2, T1[:, c % 2, :], ACT.Sigmoid, bias=col("cf_b_pw1", 8 + c))
            for t in range(8):
                split(LIN["mix_g"].tile0 + t + 2)
                for q in (2 * t, 2 * t + 1):
                    take("mix_g", q, SG[:, q, :] if q < DC else CG[:, q - DC, :], ACT.Sigmoid)

            def short_high(k):
                act.wait_ge(freed["d"], FREE[LIN["mix_b"].chunk0 + k][1])
                f(EH[:, k, :], C3[:, k, :], ACT.Copy).then_inc(eh_ready, 1)

            preload(ACT.Sqrt)
            for t in range(4):
                split(LIN["mix_b"].tile0 + t + 2)
                if t:
                    short_high(2 * t - 2)
                    short_high(2 * t - 1)
                if t == 1:
                    act.wait_ge(mean_sum, 1)
                    f(ZB, ps_norm, ACT.Copy, scale=1.0 / D).then_inc(mean_ready, 1)
                if t == 2:
                    for k in range(DC):
                        act.wait_ge(centred, k // 4 + 1)
                        f(SQ[:, k, :], Z[:, k, :], ACT.Square).then_inc(ln_sq, 1)
            short_high(6)
            short_high(7)
            act.wait_ge(ln_sum, 1)
            f(root[:, :], ps_norm, ACT.Sqrt, scale=1.0 / D, bias=eps[:, :]).then_inc(ln_root, 1)
            split(LIN["sc_out"].tile0 + 2)
            for k in range(DC):
                act.wait_ge(ln_scaled, k // 4 + 1)
                f(Z[:, k, :], Z[:, k, :], ACT.Silu, scale=col("ln_g", k), bias=col("ln_b", k)).then_inc(ln_ready, 1)
            split(LIN["sc_out"].tile0 + 3)
            act.wait_ge(ln_ready, DC)
            act.wait_ge(units_done, LIN["mix_b"].unit_end)
            for k in range(DC):
                f(HH[:, k, :], Z[:, k, :], ACT.Copy).then_inc(hh_ready, 1)
            for t in range(2, 4):
                split(LIN["sc_out"].tile0 + t + 2)

            def merged_high(k):
                act.wait_ge(freed["d"], FREE[LIN["cf_out"].chunk0 + k][1])
                f(EH[:, k, :], SG[:, k, :], ACT.Copy).then_inc(eh_ready, 1)

            for t in range(4):
                split(LIN["cf_out"].tile0 + t + 2)
                if t == 1:
                    act.wait_ge(mem_loaded, 16)
                    for k in range(DC):
                        f(SQ[:, k, :], MEM[:, k, :], ACT.Square).then_inc(squares_ready, 1)
                if t:
                    merged_high(2 * t - 2)
                    merged_high(2 * t - 1)
            merged_high(6)
            merged_high(7)
            norm_root(N_MEM)
            norm_high(N_MEM)
            residual("mix_out", N_XA)
            norm_root(N_XA)
            for t in range(4):
                split(LIN["x_k"].tile0 + t + 2)
                if t == 0:
                    norm_high(N_XA, second=True)
            for t in range(4):
                split(LIN["x_v"].tile0 + t + 2)
                take("x_v", 2 * t, V[:, 0, t * 256:(t + 1) * 256])
            for t in range(4):
                split(LIN["x_q"].tile0 + t + 2)
                for q in (2 * t, 2 * t + 1):
                    take("x_q", q, QT[:, q, :], scale=(D // 4) ** -0.5)
            attention("X")
            residual("x_o", N_PEER)
            norm_root(N_PEER)
            norm_high(N_PEER)

            def sub_copies(h):
                for t in range(TT):
                    act.wait_ge(sub_scores, 2 * h + t + 1)
                    f(S[t][:, 2 * h:2 * h + 2, :].rearrange("p a n -> p (a n)"), ps[:, 3 + 2 * (h % 2) + t, 0:2 * NK],
                      ACT.Copy).then_inc(s_ready, 1)

            for t in range(8):
                split(LIN["pq"].tile0 + t + 2)
                for q in (2 * t, 2 * t + 1):
                    take("pq", q, QP[:, q, :])
                if t:
                    sub_copies(t - 1)
            sub_copies(7)
            for b in range(8):
                dst = (HTOK, XTOK)[b // 4]
                act.wait_ge(tok_turned, b + 1)
                f(dst[:, (b // 2) % 2, (b % 2) * 512:(b % 2 + 1) * 512], ps[:, b % 2, :], ACT.Copy).then_inc(tok_ready, 1)

            def gates_exp(n):
                t, cs = n // 2, slice(n % 2 * HALF * TK, (n % 2 + 1) * HALF * TK)
                act.wait_ge(gate_diff, n + 1)
                f(GT[:, t, cs], GT[:, t, cs], ACT.Exp).then_inc(gate_exp, 1)

            gates_exp(0)
            gates_exp(1)
            for t in range(TT):
                if t:
                    gates_exp(3)
                act.wait_ge(dots_ready, t + 1)
                f(DOT[:, t, :], DOT[:, t, :], ACT.Gelu).then_inc(gelu_ready, 1)
                if t == 0:
                    gates_exp(2)
                act.wait_ge(y_ready, t + 1)
                step(f(YO[:, t, :], YACC[:, 0, :], ACT.Square, accum_out=YS[:, t:t + 1]))
                f(YS[:, t:t + 1], YS[:, t:t + 1], ACT.Sqrt, scale=1.0 / D, bias=eps[:, :]).then_inc(yroot_ready, 1)

        @block.vector
        def _(dve):
            step = Chain(dve, dve_step)
            v = nc.vector

            def split(g, i=None):
                if g < N_TILES and LOW[g][0] == "v":
                    dve.wait_ge(hi_ready, at(i, BODY, g + 1))
                    v.tensor_tensor(slot(w_lo, g), slot(raw, g), f32(slot(w_hi, g)), ALU.subtract
                                    ).then_inc(low["v"], 1)

            def mod_acc_tile(n, i=None):
                s = n % 2
                if n < 6:
                    dve.wait_ge(first_loaded[n], 16)
                    w = first_tile(n)
                else:
                    dve.wait_ge(mod_loaded[s], at(i, 32, 16 * (n // 2 - 2)))
                    w = mod_ring[:, s * TILE:(s + 1) * TILE]
                w = w.rearrange("p (k n) -> p k n", k=DC)
                for k in range(DC):
                    acc = mod_acc[:, s, k % 2, :]
                    if k < 2:
                        ins = v.tensor_scalar(acc, w[:, k, :], c_act[:, k:k + 1], None, ALU.mult)
                    else:
                        ins = v.scalar_tensor_tensor(acc, w[:, k, :], c_act[:, k:k + 1], acc, ALU.mult, ALU.add)
                    step(ins, lag=1 if k < DC - 1 else 0)
                v.tensor_tensor(mod_acc[:, s, 0, :], mod_acc[:, s, 0, :], mod_acc[:, s, 1, :], ALU.add
                                ).then_inc(acc_ready, 1)

            def mod_take(n, i=None):
                dve.wait_ge(modsum_ready, at(i, 4, summed(n)))
                if i is None:
                    dst, b = mods[:, 2 * n:2 * n + 2], col("ada_b", 2 * n, 2)
                else:
                    dst = mods[:, bass.ds(i * 8 + 2 * n, 2)]
                    b = prm[:, bass.ds(i * 8 + (COL["ada_b"] + 2 * n), 2)]
                v.tensor_tensor(dst, ps_mod[:, 0:2], b, ALU.add).then_inc(mods_ready, 1)

            def norm(n, src, name=None, mods_done=None, dst=None):
                g, m0 = NORMS[n]
                dst = T if dst is None else dst
                if m0 is not None:
                    dve.wait_ge(mods_ready, summed(mods_done - 1))
                    step(v.scalar_tensor_tensor(gain[:, :], mods[:, m0 + 8:m0 + 16], 1.0, prm[:, g:g + 8],
                                                ALU.add, ALU.mult))
                if n in RANK:
                    dve.wait_ge(root_ready, RANK[n] + 1)
                    step(v.reciprocal(rinv[:, :], root[:, :]))

                def low(k):
                    dve.wait_ge(hh_ready, SET[name] + k + 1)
                    v.scalar_tensor_tensor(HL[:, k, :], T[:, k, :], mods[:, m0 + k:m0 + k + 1], f32(HH[:, k, :]),
                                           ALU.add, ALU.subtract).then_inc(hl_ready, 1)

                for k in range(DC):
                    gk = prm[:, g + k:g + k + 1] if m0 is None else gain[:, k:k + 1]
                    v.scalar_tensor_tensor(dst[:, k, :], src[:, k, :], gk, rinv[:, :], ALU.mult, ALU.mult
                                           ).then_inc(t_ready, 1)
                if m0 is not None:
                    for k in range(DC):
                        low(k)

            def take(name, q, op):
                q = LIN[name].chunk0 + q
                dve.wait_ge(units_done, CHUNK_UNIT[q])
                assert FREE[q][0] == "d"
                op(ps[:, q % BANKS, 0:SEQ]).then_inc(freed["d"], 1)

            def ffn(n, w_in, w_out, gate0, ada):
                ln = LIN[w_in]
                more = ada is not None

                def slot_(t, i=None):
                    acc = {0: 0, 1: 1, 3: 2, 4: 3, 18: 12, 19: 13}.get(t) if more else None
                    got = {1: 0, 2: 1, 4: 2, 5: 3, 19: 12, 20: 13}.get(t) if more else None
                    if acc is not None:
                        mod_acc_tile(ada + acc, i)
                    split(ln.tile0 + t + 2, i)
                    if got is not None:
                        mod_take(ada + got, i)
                    q = ln.chunk0 + 2 * t + 1
                    dve.wait_ge(units_done, at(i, 2 * BODY, CHUNK_UNIT[q]))
                    dve.wait_ge(freed["a"], at(i, BODY, FREE[q - 1][1]))
                    dve.wait_ge(hidden_lo, at(i, BODY, FC * n + t + 1))
                    v.tensor_tensor(graw[:, t % 2, :], ps[:, q % BANKS, 0:SEQ], silu[:, t % 2, :], ALU.mult
                                    ).then_inc(freed["d"], 1)

                with dve.Fori(0, 3) as i:
                    if more:
                        step.enter(i, 4 * DC)
                    for t in range(BODY):
                        slot_(t, i)
                    if more:
                        step.leave(3)
                for t in range(18, 22):
                    slot_(t)
                dve.wait_ge(mods_ready, summed(ada + 13 if more else ADA_TILES - 1))
                step(v.tensor_scalar(half_gate[:, :], mods[:, gate0:gate0 + 8], 0.5, None, ALU.mult))
                lo = LIN[w_out]
                for m in range(DC):
                    with_mod = more and 1 <= m <= 6
                    if with_mod:
                        mod_acc_tile(ada + 14 + m - 1)
                    split(lo.tile0 + 2 * m + 2)
                    if m < DC - 1:
                        split(lo.tile0 + 2 * m + 3)
                    if with_mod and m < 6:
                        mod_take(ada + 14 + m - 1)
                    take(w_out, m, lambda p: v.scalar_tensor_tensor(
                        X[:, m, :], p, half_gate[:, m:m + 1], X[:, m, :], ALU.mult, ALU.add))
                split(lo.tile0 + 2 * DC + 1)

            def residual(name, gate0=None):
                for t in range(4):
                    split(LIN[name].tile0 + t + 2)
                    for q in (2 * t, 2 * t + 1):
                        if gate0 is None:
                            take(name, q, lambda p: v.tensor_tensor(X[:, q, :], p, X[:, q, :], ALU.add))
                        else:
                            take(name, q, lambda p: v.scalar_tensor_tensor(
                                X[:, q, :], p, mods[:, gate0 + q:gate0 + q + 1], X[:, q, :], ALU.mult, ALU.add))

            def logits(s):
                kind, c = STEPS[s]
                par = s % 2
                for qt in range(TT):
                    u = 2 * s + qt
                    dve.wait_ge(scores_done, u + 1)
                    if s:
                        dve.wait_ge(exp_ready, u - 1)
                    if kind == "X":
                        v.reduce_max(nmax[:, par, 2 * qt:2 * qt + 2], ps_s[qt][:, :, 0:SEQ], axis=AX.X, negate=True
                                     ).then_inc(logits_ready, 1)
                        continue
                    nk = SEQ if qt == 1 else P
                    b = bias[:, c, SEQ - nk:SEQ] if kind == "A" else mask[:, SEQ - nk:SEQ]
                    for m in range(2):
                        last = v.tensor_tensor_reduce(out=LG[:, qt, m, 0:nk], in0=ps_s[qt][:, m, 0:nk], in1=b,
                                                      scale=-1.0, scalar=3.0e38, op0=ALU.add, op1=ALU.min,
                                                      accum_out=nmax[:, par, 2 * qt + m:2 * qt + m + 1])
                    last.then_inc(logits_ready, 1)

            def probs(s):
                kind, c = STEPS[s]
                par = s % 2
                dve.wait_ge(exp_ready, 2 * s + 2)
                r = rscale[:, par, :]
                step(v.reciprocal(r, rowsum[:, par, :]))
                if kind == "A":
                    step(v.tensor_tensor(r, r, lam_vec[:, :], ALU.mult))
                if s:
                    dve.wait_ge(turned, s)
                if kind == "A":
                    for qt, nk in ((0, P), (1, SEQ)):
                        step(v.tensor_scalar(PR[:, qt, 0, 0:nk], EX[par][:, qt, 0, 0:nk], r[:, 2 * qt:2 * qt + 1], None,
                                             ALU.mult), lag=1)
                    for qt, nk in ((0, P), (1, SEQ)):
                        if qt:
                            dve.wait_ge(dve_step, step.n)
                        v.scalar_tensor_tensor(PR[:, qt, 0, 0:nk], EX[par][:, qt, 1, 0:nk], r[:, 2 * qt + 1:2 * qt + 2],
                                               PR[:, qt, 0, 0:nk], ALU.mult, ALU.add).then_inc(probs_ready, 1)
                    return
                for qt in range(TT):
                    nk = SEQ if kind == "X" or qt == 1 else P
                    v.tensor_tensor(PR[:, qt, :, 0:nk], EX[par][:, qt, :, 0:nk],
                                    r[:, 2 * qt:2 * qt + 2].unsqueeze(2).broadcast_to([P, 2, nk]), ALU.mult
                                    ).then_inc(probs_ready, 1)

            def attention(kind):
                s0, s1 = STEP0[kind], STEP_END[kind]
                logits(s0)
                for s in range(s0, s1):
                    if s + 1 < s1:
                        logits(s + 1)
                    probs(s)

            v.memset(eps[:, :], EPS)
            step(v.memset(ones[:, :], 1.0))
            v.memset(table[NB:NB + 1, :], NEG)
            step(v.memset(lam_vec[:, :], 1.0))
            dve.sem_inc(vec_consts, 1)
            dve.wait_ge(small_loaded, 64)
            v.tensor_copy(table_rep[:, :, :], table[:, :].unsqueeze(2).broadcast_to([NB + 1, A_HEADS, P])
                          ).then_inc(table_ready, 1)
            lp = lamp[:, :].rearrange("p (a b n) -> p a b n", a=2, b=2)
            step(v.tensor_tensor(lam_prod[:, :, :], lp[:, :, 0, :], lp[:, :, 1, :], ALU.mult))
            v.reduce_sum(lam_sum[:, :], lam_prod[:, :, :], axis=AX.X).then_inc(lam_sum_ready, 1)
            for h in (1, 3):
                dve.wait_ge(units_done, h + 1)
                v.tensor_copy(stg[:, h, :], ps[:, h % BANKS, :]).then_inc(freed["d"], 1)
            dve.wait_ge(prm_loaded, 16)
            dve.wait_ge(c_ready, 1)
            dve.wait_ge(lam_exp_ready, 1)
            step(v.tensor_tensor(lam_vec[:, 1:2], lam_exp[:, 1:2], lam_exp[:, 0:1], ALU.subtract))
            step(v.tensor_scalar(lam_vec[:, 1:2], lam_vec[:, 1:2], -LAM_INIT, None, ALU.add))
            step(v.tensor_copy(lam_vec[:, 3:4], lam_vec[:, 1:2]))
            step(v.tensor_scalar(sub_gain[:, :], col("subln_g"), 1.0 - LAM_INIT, None, ALU.mult))
            for n in range(DIRECT[0]):
                mod_acc_tile(n)
                if n:
                    mod_take(n - 1)
                if n >= 2:
                    split(n - 2)
            mod_take(DIRECT[0] - 1)
            n0, n_ = 2 * DIRECT[0], 2 * len(DIRECT)
            dve.wait_ge(direct_ready, 1)
            step(v.tensor_tensor(mods[:, n0:n0 + n_], ps_direct, col("ada_b", n0, n_), ALU.add))
            norm(0, X, "n0", 8)
            ffn(0, "f00_in", "f00_out", MOD_L0 + 16, 8)

            norm(1, X, "n1", 24)
            mod_take(27)
            for t in range(4):
                mod_acc_tile(28 + t)
                split(LIN["a_q"].tile0 + t + 2)
                if t:
                    mod_take(28 + t - 1)
            for t in range(4):
                mod_acc_tile(32 + t)
                split(LIN["a_k"].tile0 + t + 2)
                mod_take(31 + t)
                for q in (2 * t, 2 * t + 1):
                    take("a_k", q, lambda p: v.tensor_copy(KT[:, q, :], p))
            for t in range(4):
                split(LIN["a_v"].tile0 + t + 2)
                if t == 0:
                    mod_take(35)
                take("a_v", 2 * t + 1, lambda p: v.tensor_copy(V[:, 1, t * 256:(t + 1) * 256], p))
            dve.wait_ge(bias_loaded, 16)
            attention("A")
            for b in range(4):
                tq = T[:, 2 * b:2 * b + 2, :]
                oq = OT[:, 2 * b:2 * b + 2, :]
                dve.wait_ge(sub_root, b + 1)
                step(v.reciprocal(tq, tq))
                v.scalar_tensor_tensor(oq, oq, sub_gain[:, :], tq, ALU.mult, ALU.mult).then_inc(sub_done, 1)
            residual("a_o", MOD_L0 + 40)
            norm(2, X, "n2", 36)
            ffn(1, "f01_in", "f01_out", MOD_L0 + 64, 36)

            norm(3, X, "n3", 44)
            mod_take(55)
            for t in range(4):
                split(LIN["s_k"].tile0 + t + 2)
                for q in (2 * t, 2 * t + 1):
                    take("s_k", q, lambda p: v.tensor_copy(KS[:, q, :], p))
            for t in range(4):
                split(LIN["s_v"].tile0 + t + 2)
                take("s_v", 2 * t + 1, lambda p: v.tensor_copy(VS[:, 1, t * 256:(t + 1) * 256], p))
            norm(4, X, "n4", 52)
            dve.wait_ge(fz_ln, 1)
            step(v.tensor_scalar(f_z[:, :], f_z[:, :], 0.0, None, ALU.min))
            step(v.tensor_tensor(f_z[:, :], f_z[:, :], f_t[:, :], ALU.subtract))
            step(v.memset(f_t[:, :], 1.0))
            step(v.tensor_tensor_scan(f_sum[:, :], f_t[:, :], f_z[:, :], 0.0, ALU.mult, ALU.add))
            v.tensor_scalar(f_neg[:, :], f_sum[:, :], -1.0, None, ALU.mult).then_inc(f_ready, 1)
            ffn(2, "f10_in", "f10_out", MOD_L1 + 16, 56)
            norm(5, X, "n5", 68)
            mod_take(75)
            for t in range(4):
                mod_acc_tile(76 + t)
                split(LIN["b_q"].tile0 + t + 2)
                if t:
                    mod_take(76 + t - 1)
            mod_take(79)
            attention("B")
            residual("b_o", MOD_L1 + 40)
            norm(6, X, "n6", 80)
            ffn(3, "f11_in", "f11_out", MOD_L1 + 64, None)
            norm(N_FINAL, X, dst=X)

            v.memset(U[:, :, 0:SCK - 1], 0.0)
            step(v.memset(CV[:, :, 0:CFK - 1], 0.0))
            norm(N_MIX, X)
            mix = LIN["mix_a"].chunk0

            def taps(c, k0, k1):
                for k in range(k0, k1):
                    dst = (Z, SQ)[k % 2]
                    step(v.scalar_tensor_tensor(dst[:, c, :], CV[:, c, k:k + SEQ], col("cf_w", 8 * k + c), dst[:, c, :],
                                                ALU.mult, ALU.add), lag=1)

            for c in range(DC):
                split(LIN["mix_a"].tile0 + 2 * c + 2)
                dve.wait_ge(freed["a"], FREE[mix + 4 * c][1])
                take("mix_a", 4 * c + 1, lambda p: v.tensor_tensor(U[:, c, SCK - 1:], p, T0[:, c % 2, :], ALU.mult))
                split(LIN["mix_a"].tile0 + 2 * c + 3)
                dve.wait_ge(freed["a"], FREE[mix + 4 * c + 2][1])
                take("mix_a", 4 * c + 3, lambda p: v.scalar_tensor_tensor(
                    CV[:, c, CFK - 1:], p, col("cf_b_pw1", c), T1[:, c % 2, :], ALU.add, ALU.mult))
                dve.wait_ge(freed["d"], FREE[mix + 4 * c + 3][1])
                w31 = lambda k: col("cf_w", 8 * k + c)
                step(v.tensor_scalar(Z[:, c, :], CV[:, c, 0:SEQ], w31(0), col("cf_conv_b", c), ALU.mult, ALU.add), lag=1)
                step(v.tensor_scalar(SQ[:, c, :], CV[:, c, 1:1 + SEQ], w31(1), None, ALU.mult), lag=1)
                taps(c, 2, EARLY_TAPS)
            for c in range(DC):
                w3 = lambda k: col("sc_w", 8 * k + c)
                step(v.tensor_scalar(C3[:, c, :], U[:, c, 0:SEQ], w3(0), None, ALU.mult), lag=1)
                taps(c, EARLY_TAPS, CFK)
                step(v.scalar_tensor_tensor(C3[:, c, :], U[:, c, 1:1 + SEQ], w3(1), C3[:, c, :], ALU.mult, ALU.add), lag=1)
                v.tensor_tensor(Z[:, c, :], Z[:, c, :], SQ[:, c, :], ALU.add).then_inc(conv_done, 1)
                dve.wait_ge(conv_done, c + 1)
                step(v.scalar_tensor_tensor(C3[:, c, :], U[:, c, 2:2 + SEQ], w3(2), C3[:, c, :], ALU.mult, ALU.add), lag=1)
            dve.wait_ge(dve_step, step.n)
            for t in range(4):
                split(LIN["mix_b"].tile0 + t + 2)
                for q in (2 * t, 2 * t + 1):
                    take("mix_b", q, lambda p: v.tensor_tensor(C3[:, q, :], p, C3[:, q, :], ALU.mult))
                if t == 1:
                    dve.wait_ge(mean_ready, 1)
                    for half in (slice(0, 4), slice(4, 8)):
                        v.tensor_tensor(Z[:, half, :], Z[:, half, :], ZB.unsqueeze(1).broadcast_to([P, 4, SEQ]),
                                        ALU.subtract).then_inc(centred, 1)
            dve.wait_ge(ln_root, 1)
            step(v.reciprocal(rinv[:, :], root[:, :]))
            for half in (slice(0, 4), slice(4, 8)):
                v.tensor_tensor(Z[:, half, :], Z[:, half, :], rinv[:, :].unsqueeze(1).broadcast_to([P, 4, SEQ]),
                                ALU.mult).then_inc(ln_scaled, 1)
            dve.wait_ge(freed["a"], LIN["mix_g"].freed_a)
            for t in range(4):
                split(LIN["sc_out"].tile0 + t + 2)
                for q in (2 * t, 2 * t + 1):
                    take("sc_out", q, lambda p: v.tensor_tensor(SG[:, q, :], p, SG[:, q, :], ALU.mult))
            for t in range(4):
                split(LIN["cf_out"].tile0 + t + 2)
                for q in (2 * t, 2 * t + 1):
                    qq = LIN["cf_out"].chunk0 + q
                    dve.wait_ge(units_done, CHUNK_UNIT[qq])
                    step(v.scalar_tensor_tensor(CG[:, q, :], ps[:, qq % BANKS, 0:SEQ], col("b_pw2", q), CG[:, q, :],
                                                ALU.add, ALU.mult))
                    v.tensor_tensor(SG[:, q, :], SG[:, q, :], CG[:, q, :], ALU.add).then_inc(freed["d"], 1)
            norm(N_MEM, MEM)
            residual("mix_out")

            for t in range(4):
                split(LIN["x_k"].tile0 + t + 2)
                if t == 0:
                    dve.wait_ge(hl_ready, SET["n9"] + DC)
                    norm(N_XA, X)
                for q in (2 * t, 2 * t + 1):
                    take("x_k", q, lambda p: v.tensor_copy(KT[:, q, :], p))
            for t in range(4):
                split(LIN["x_v"].tile0 + t + 2)
                take("x_v", 2 * t + 1, lambda p: v.tensor_copy(V[:, 1, t * 256:(t + 1) * 256], p))
            for t in range(4):
                split(LIN["x_q"].tile0 + t + 2)
            attention("X")
            residual("x_o")
            norm(N_PEER, X)

            def head_best(t, h):
                dve.wait_ge(s_ready, 2 * h + t + 1)
                hps = (2 * h, 2 * h + 1)
                s_ = S[t]
                for hp in hps:
                    step(v.max(TV[:, hp, 0:8], s_[:, hp, :]), lag=1)
                for hp in hps:
                    step(v.max_index(TI[:, hp, 0:8], TV[:, hp, 0:8], s_[:, hp, :]), lag=1)
                    step(v.match_replace(S2[:, hp, :], TV[:, hp, 0:8], s_[:, hp, :], -3.0e38), lag=1)
                for hp in hps:
                    step(v.max(TV[:, hp, 8:16], S2[:, hp, :]), lag=1)
                for hp in hps:
                    step(v.max_index(TI[:, hp, 8:16], TV[:, hp, 8:16], S2[:, hp, :]), lag=1)
                pair = [P, TK, TK]
                step(v.tensor_tensor(CA[:, h, :].rearrange("p (a b) -> p a b", a=TK),
                                     TV[:, 2 * h, :].unsqueeze(2).broadcast_to(pair),
                                     TV[:, 2 * h + 1, :].unsqueeze(1).broadcast_to(pair), ALU.add))
                step(v.max(FV[:, h, 0:8], CA[:, h, :]))
                step(v.max_index(FP[:, h, 0:8], FV[:, h, 0:8], CA[:, h, :]), lag=1)
                step(v.match_replace(CA2[:, h, :], FV[:, h, 0:8], CA[:, h, :], -3.0e38))
                step(v.max(FV[:, h, 8:16], CA2[:, h, :]))
                step(v.max_index(FP[:, h, 8:16], FV[:, h, 8:16], CA2[:, h, :]))

            def choose(t, half):
                hs = slice(half * HALF, (half + 1) * HALF)
                hp2 = slice(2 * half * HALF, 2 * (half + 1) * HALF)
                n_ = HALF * TK
                cs = slice(half * n_, (half + 1) * n_)
                v.tensor_copy(TIF[:, hp2, :], TI[:, hp2, :])
                v.tensor_tensor(GT[:, t, cs].rearrange("p (h k) -> p h k", h=HALF), FV[:, hs, :],
                                FV[:, hs, 0:1].broadcast_to([P, HALF, TK]), ALU.subtract).then_inc(gate_diff, 1)
                fp = FP[:, hs, :].rearrange("p h k -> p (h k)")
                v.tensor_scalar(AI[:, cs], fp, 4, None, ALU.logical_shift_right)
                step(v.tensor_scalar(BI[:, cs], fp, TK - 1, None, ALU.bitwise_and))
                v.tensor_copy(AF[:, cs], AI[:, cs])
                step(v.tensor_copy(BF[:, cs], BI[:, cs]))
                tif = TIF[:, hp2, :].rearrange("p (h s) k -> p h s k", s=2)
                for src, side, dst, room in ((AF, 0, I0, S[t]), (BF, 1, I1, S2)):
                    eq = room[:, hp2, :].rearrange("p a n -> p (a n)").rearrange("p (c j) -> p c j", c=n_)
                    step(v.tensor_tensor(eq, src[:, cs].unsqueeze(2).broadcast_to([P, n_, TK]),
                                         iota16[:, :].unsqueeze(1).broadcast_to([P, n_, TK]), ALU.is_equal))
                    e4 = eq.rearrange("p (h k) j -> p h k j", h=HALF)
                    step(v.tensor_tensor(e4, e4, tif[:, :, side, :].unsqueeze(2).broadcast_to([P, HALF, TK, TK]), ALU.mult))
                    step(v.reduce_sum(dst[:, cs], eq, axis=AX.X))
                v.scalar_tensor_tensor(IDX[:, t, cs], I0[:, cs], float(NK), I1[:, cs], ALU.mult, ALU.add
                                       ).then_inc(idx_ready, 1)

            def gates(t):
                gt = GT[:, t, :].rearrange("p (h k) -> p h k", h=PH)
                dve.wait_ge(gate_exp, 2 * t + 2)
                step(v.reduce_sum(GS[:, 8:16], gt, axis=AX.X))
                step(v.reciprocal(GS[:, 8:16], GS[:, 8:16]))
                step(v.tensor_tensor(gt, gt, GS[:, 8:16].unsqueeze(2).broadcast_to([P, PH, TK]), ALU.mult))

            dve.sem_inc(rows_free, GROUP)
            for h in range(PH):
                head_best(0, h)
                if h % HALF == HALF - 1:
                    choose(0, h // HALF)
            dve.wait_ge(tok_ready, 8)
            dve.wait_ge(gfin_loaded, 16)

            def dot(t, group, j, dst, i=None):
                dve.wait_ge(row_loaded[j], at(i, 16, 16 * (group + 1)))
                v.tensor_tensor_reduce(out=junk[:, j % 2, :], in0=rows_ring[:, j * D:(j + 1) * D], in1=HTOK[:, t, :],
                                       scale=1.0, scalar=0.0, op0=ALU.mult, op1=ALU.add, accum_out=dst
                                       ).then_inc(rows_free, 1)
                if j >= 1:
                    dve.wait_ge(rows_free, at(i, GROUP, GROUP * (group + 1) + j))

            def weighted(t, first, n):
                seg = (2 * t + 1) * N_GROUPS + first
                with dve.Fori(0, n) as i:
                    step.enter(i, 1)
                    step(v.tensor_copy(coef16[:, :], CF[:, t, bass.ds(i * GROUP + first * GROUP, GROUP)]))
                    step.leave(n)
                    for j in range(GROUP):
                        dve.wait_ge(row_loaded[j], i * 16 + 16 * (seg + 1))
                        y = YACC[:, j % 2, :]
                        v.scalar_tensor_tensor(y, rows_ring[:, j * D:(j + 1) * D], coef16[:, j:j + 1], y,
                                               ALU.mult, ALU.add).then_inc(rows_free, 1)
                        if j >= 1:
                            dve.wait_ge(rows_free, i * GROUP + (GROUP * (seg + 1) + j))
                    dve.wait_ge(rows_free, i * GROUP + GROUP * (seg + 2))

            def dots(t, first, n):
                seg = 2 * t * N_GROUPS + first
                with dve.Fori(0, n) as i:
                    for j in range(GROUP):
                        dot(t, seg, j, dot16[:, j:j + 1], i)
                    dve.wait_ge(rows_free, i * GROUP + GROUP * (seg + 2))
                    step.enter(i, 1)
                    step(v.tensor_copy(DOT[:, t, bass.ds(i * GROUP + first * GROUP, GROUP)], dot16[:, :]))
                    step.leave(n)

            for t in range(TT):
                if t == 0:
                    for g in range(N_GROUPS):
                        for j in range(GROUP):
                            n_ = g * GROUP + j
                            dot(t, g, j, DOT[:, t, n_:n_ + 1])
                        dve.wait_ge(rows_free, GROUP * (g + 2))
                        if g >= HALF:
                            head_best(1, g - HALF)
                else:
                    dots(t, 0, 2)
                    for h in range(HALF + 2, PH):
                        head_best(1, h)
                    choose(1, 1)
                    dots(t, 2, N_GROUPS - 2)
                dve.sem_inc(dots_ready, 1)
                gates(t)
                step(v.memset(YACC[:, 0, :], 0.0))
                step(v.memset(YACC[:, 1, :], 0.0))
                dve.wait_ge(gelu_ready, t + 1)
                step(v.tensor_tensor(CF[:, t, :], DOT[:, t, :], GT[:, t, :], ALU.mult))
                if t == 0:
                    for part in range(N_GROUPS // 2):
                        weighted(t, 2 * part, 2)
                        if part < 2:
                            head_best(1, HALF + part)
                        if part == 2:
                            choose(1, 0)
                else:
                    weighted(t, 0, N_GROUPS)
                step(v.tensor_tensor(YACC[:, 0, :], YACC[:, 0, :], YACC[:, 1, :], ALU.add))
                v.tensor_tensor(YACC[:, 0, :], YACC[:, 0, :], XTOK[:, t, :], ALU.add).then_inc(y_ready, 1)
                dve.wait_ge(yroot_ready, t + 1)
                step(v.reciprocal(YS[:, 2 + t:3 + t], YS[:, t:t + 1]))
                v.scalar_tensor_tensor(YO[:, t, :], YACC[:, 0, :], YS[:, 2 + t:3 + t], gfin,
                                       ALU.mult, ALU.mult).then_inc(yo_ready, 1)


def relative_buckets():
    rel = 255 - np.arange(512)
    n = np.maximum(rel, 0)
    exact = NB // 2
    large = exact + (np.log(np.maximum(n, 1).astype(np.float32) / exact) / math.log(MAX_DISTANCE / exact)
                     * (NB - exact)).astype(np.int32)
    bucket = np.where(n < exact, n, np.minimum(large, NB - 1))
    bucket = np.where(rel >= 0, bucket, NB)
    return (np.arange(NB + 1)[:, None] == bucket[None, :]).astype(np.float32)


def kernel(**inputs):
    import numpy as _np
    import concourse.bacc as _bacc
    from concourse import mybir as _mybir
    from concourse.bass_utils import run_bass_kernel_spmd as _run

    x = {k: _np.asarray(v) for k, v in inputs.items()}
    cat = _np.concatenate

    def cols(v):
        return v.reshape(-1, P).T

    def tiles(w, order=None):
        k, n = w.shape
        w = w.reshape(k // P, P, n // P, P)
        if order is not None:
            w = w[:, :, order]
        w = w.reshape(k // P, P, -1, 2, P)
        return w.transpose(2, 1, 0, 3, 4).reshape(w.shape[2], P, -1)

    def out_tiles(w):
        return w.reshape(2, WO_K, P, DC, P).transpose(3, 0, 2, 1, 4).reshape(2 * DC, P, WO_K * P)

    pairs = [m + half * FC for m in range(FC) for half in range(2)]
    a = {}
    for la in range(2):
        for s in range(2):
            a[f"f{la}{s}_in"] = tiles(x["ffn_w_in"][la, s], pairs)
            a[f"f{la}{s}_out"] = out_tiles(x["ffn_w_out"][la, s])
    qkv = x["a_w_qkv"][0]
    a["a_q"], a["a_k"], a["a_v"] = (tiles(qkv[:, n * D:(n + 1) * D]) for n in range(3))
    a["a_o"] = tiles(x["a_w_o"][0])
    a["s_k"], a["s_v"] = tiles(x["kv_w"][:, :D]), tiles(x["kv_w"][:, D:])
    a["b_q"], a["b_o"] = tiles(x["b_w_q"][0]), tiles(x["b_w_o"][0])
    a["mix_a"] = tiles(x["w_in_2"][0], [b * DC + c for c in range(DC) for b in (1, 2, 4, 3)])
    a["mix_b"] = tiles(x["w_in_2"][0], [c for c in range(DC)])
    a["mix_g"] = tiles(x["w_in_2"][0], [b * DC + c for b in (5, 6) for c in range(DC)])
    a["sc_out"], a["cf_out"] = tiles(x["sc_w_out_2"][0]), tiles(x["cf_w_pw2_2"][0])
    a["mix_out"] = tiles(x["w_mix_out_2"][0])
    a["x_k"], a["x_v"] = tiles(x["w_kv_2"][0][:, :D]), tiles(x["w_kv_2"][0][:, D:])
    a["x_q"], a["x_o"], a["pq"] = tiles(x["w_q_2"][0]), tiles(x["w_xo_2"][0]), tiles(x["w_peer_q_2"][0])
    a["ada"] = cat([tiles(x["ada_w"][0]), tiles(x["kv_ada_w"]), tiles(x["ada_w"][1])])
    a["prm"] = cat([
        cols(x["c"]), cols(x["ada_b"][0]), cols(x["kv_ada_b"]), cols(x["ada_b"][1]), cols(x["norm_g"]),
        cols(x["kv_norm_g"]), cols(x["final_g"]), cols(x["norm_mix_g_2"]), cols(x["cf_b_pw1_2"]),
        cols(x["sc_conv_w_2"]), cols(x["cf_conv_w_2"]), cols(x["cf_conv_b_2"]), cols(x["cf_ln_g_2"]),
        cols(x["cf_ln_b_2"]), cols(x["cf_b_pw2_2"]), cols(x["norm_xa_g_2"]), cols(x["norm_mem_g_2"]),
        cols(x["norm_peer_g_2"]), cols(x["a_subln_g"]),
        x["fgate_w"].reshape(DC, P, B_HEADS).transpose(1, 0, 2).reshape(P, -1)], axis=1)
    a["xT"] = x["x"][0].reshape(SEQ, DC, P).transpose(2, 1, 0)
    a["memT"] = x["mem_2"][0].reshape(SEQ, DC, P).transpose(2, 1, 0)
    a["rel_bias"] = x["rel_bias"]
    a["onehot"] = relative_buckets()
    a["a_lambda"] = x["a_lambda"].reshape(1, -1)
    a["fgate_b"] = x["fgate_b"].reshape(-1, 1)
    a["subkT"] = x["peer_subkeys_2"][0].transpose(2, 0, 1)
    a["final_norm_g"] = x["final_norm_g_2"].reshape(1, -1)
    a["peer_u"], a["peer_v"] = x["peer_u_2"][0], x["peer_v_2"][0]

    nc = _bacc.Bacc("TRN2", target_bir_lowering=False, num_devices=1)
    arrays, aps = {}, {}
    for name, v in a.items():
        arrays["in_" + name] = _np.ascontiguousarray(v)
        aps[name] = nc.dram_tensor("in_" + name, v.shape, _mybir.dt.from_np(v.dtype), kind="ExternalInput").ap()
    out = nc.dram_tensor("out", (TT, P, D), _mybir.dt.float32, kind="ExternalOutput").ap()
    build_program(nc, aps, out)
    r = _run(nc, [arrays], core_ids=[0])
    return r.results[0]["out"].reshape(1, SEQ, D)
```
